# Optimizing a Trainium2 kernel written in Bass

```python
import jax, jax.numpy as jnp
from jax import lax
import numpy as np

D_MODEL = 1024
BATCH = 1
SEQ = 1024
DEPTH = 2
DEC_BATCH = 1
DEC_SEQ = 64
PAST_LEN = 2048

CHUNK = 64
N_EVEN = (DEPTH + 1) // 2
N_ODD = DEPTH // 2
EPS = 1e-6
A_HEADS = 16
A_KV_HEADS = 4
A_HEAD_DIM = 64
A_GROUP = A_HEADS // A_KV_HEADS
A_WIDTH = A_HEADS * A_HEAD_DIM
WINDOW = 128
WIN_CHUNKS = -(-WINDOW // CHUNK)
WIN_ROWS = WIN_CHUNKS * CHUNK
B_HEADS = 4
B_DK = 128
B_DV = 256
B_WIDTH = B_HEADS * B_DV
B_LOWRANK = 16
B_GATE_NORM = 16.0
C_WIDTH = 1536
C_BLOCKS = 8
C_BLOCK = C_WIDTH // C_BLOCKS
CONV_W = 4
LRU_C = 8.0
MIX_EVEN = A_WIDTH + B_WIDTH
SPLIT_EVEN = (A_WIDTH, A_KV_HEADS * A_HEAD_DIM, A_KV_HEADS * A_HEAD_DIM,
              B_HEADS * B_DK, B_HEADS * B_DK, B_WIDTH, B_LOWRANK, MIX_EVEN)
IN_EVEN = sum(SPLIT_EVEN)
IN_ODD = 2 * C_WIDTH

kernel_name = "hybrid_swa_gla_rglru_stream_step"

def _rmsnorm(x, g):
    xf = x.astype(jnp.float32)
    y = xf * lax.rsqrt(jnp.mean(xf * xf, axis=-1, keepdims=True) + EPS) * g.astype(jnp.float32)
    return y.astype(x.dtype)

def _split(z, sizes):
    offs = [int(o) for o in np.cumsum(sizes)[:-1]]
    return jnp.split(z, offs, axis=-1)

def _alibi_slopes():
    return 2.0 ** (-8.0 * jnp.arange(1, A_HEADS + 1, dtype=jnp.float32) / A_HEADS)

def _band(t):
    b, tl = t.shape[:2]
    nc = tl // CHUNK
    tp = jnp.pad(t, ((0, 0), (WIN_ROWS, 0), (0, 0), (0, 0)))
    tp = tp.reshape(b, nc + WIN_CHUNKS, CHUNK, t.shape[2], t.shape[3])
    return jnp.concatenate([tp[:, w:w + nc] for w in range(WIN_CHUNKS + 1)], axis=2)

def _sink_alibi_attention(qb, kb, vb, key_ok, sinks):
    lq, lk = qb.shape[2], kb.shape[2]
    s = jnp.einsum('bnikgd,bnjkd->bnkgij', qb, kb).astype(jnp.float32) * (A_HEAD_DIM ** -0.5)
    dist = jnp.abs(WIN_ROWS + jnp.arange(lq)[:, None] - jnp.arange(lk)[None, :]).astype(jnp.float32)
    slopes = _alibi_slopes().reshape(A_KV_HEADS, A_GROUP)
    s = s - slopes[:, :, None, None] * dist
    s = jnp.where(key_ok[None, :, None, None, None, :], s, jnp.float32(-1e30))
    sk = jnp.broadcast_to(sinks.astype(jnp.float32).reshape(A_KV_HEADS, A_GROUP)[:, :, None, None],
                          s.shape[:-1] + (1,))
    p = jax.nn.softmax(jnp.concatenate([s, sk], axis=-1), axis=-1)[..., :-1]
    o = jnp.einsum('bnkgij,bnjkd->bnikgd', p.astype(vb.dtype), vb)
    return o

def _gla(q, k, v, g, s0, blk):
    b, tl, h, dk = q.shape
    dv = v.shape[-1]
    n = tl // blk
    q = q.astype(jnp.float32).reshape(b, n, blk, h, dk)
    k = k.astype(jnp.float32).reshape(b, n, blk, h, dk)
    v = v.astype(jnp.float32).reshape(b, n, blk, h, dv)
    G = jnp.cumsum(g.reshape(b, n, blk, h, dk), axis=2)
    g_last = G[:, :, -1]
    qg = q * jnp.exp(G)
    kg = k * jnp.exp(-G)
    a = jnp.einsum('bnihd,bnjhd->bnhij', qg, kg)
    a = jnp.where(jnp.tril(jnp.ones((blk, blk), bool)), a, 0.0)
    o = jnp.einsum('bnhij,bnjhe->bnihe', a, v)
    kd = k * jnp.exp(g_last[:, :, None] - G)
    ds = jnp.einsum('bnjhd,bnjhe->bnhde', kd, v)

    def step(S, inp):
        dec, d = inp
        return jnp.exp(dec)[..., None] * S + d, S

    s_fin, s_in = lax.scan(step, s0, (jnp.moveaxis(g_last, 1, 0), jnp.moveaxis(ds, 1, 0)))
    o = o + jnp.einsum('bnihd,bnhde->bnihe', qg, jnp.moveaxis(s_in, 0, 1))
    return o.reshape(b, tl, h, dv), s_fin

def _even_layer(x, past, norm_g, w_in, w_lr, b_lr, sinks, gla_g, w_out):
    b, tl, _ = x.shape
    h = _rmsnorm(x, norm_g)
    z = h @ w_in
    aq, ak, av, bq, bk, bv, blr, gate = _split(z, SPLIT_EVEN)
    aq = aq.reshape(b, tl, A_KV_HEADS, A_GROUP, A_HEAD_DIM)
    ak = ak.reshape(b, tl, A_KV_HEADS, A_HEAD_DIM)
    av = av.reshape(b, tl, A_KV_HEADS, A_HEAD_DIM)
    if past is None:
        nc = tl // CHUNK
        qb = aq.reshape(b, nc, CHUNK, A_KV_HEADS, A_GROUP, A_HEAD_DIM)
        kb, vb = _band(ak), _band(av)
        key_pos = (jnp.arange(nc)[:, None] - WIN_CHUNKS) * CHUNK + jnp.arange(WIN_ROWS + CHUNK)[None, :]
        key_ok = key_pos >= 0
        new_k, new_v = ak[:, -WIN_ROWS:], av[:, -WIN_ROWS:]
        s0 = jnp.zeros((b, B_HEADS, B_DK, B_DV), jnp.float32)
        blk = CHUNK
    else:
        ck, cv, s0 = past
        qb = aq[:, None]
        kb = jnp.concatenate([ck.astype(ak.dtype), ak], axis=1)[:, None]
        vb = jnp.concatenate([cv.astype(av.dtype), av], axis=1)[:, None]
        key_ok = jnp.ones((1, WIN_ROWS + tl), bool)
        new_k, new_v = ak, av
        blk = tl
    ao = _sink_alibi_attention(qb, kb, vb, key_ok, sinks).reshape(b, tl, A_WIDTH)
    glog = jax.nn.log_sigmoid((blr @ w_lr + b_lr).astype(jnp.float32)) / B_GATE_NORM
    bo, s_new = _gla(bq.reshape(b, tl, B_HEADS, B_DK) * (B_DK ** -0.5),
                     bk.reshape(b, tl, B_HEADS, B_DK),
                     bv.reshape(b, tl, B_HEADS, B_DV),
                     glog.reshape(b, tl, B_HEADS, B_DK),
                     s0.astype(jnp.float32), blk)
    bo = _rmsnorm(bo, gla_g).reshape(b, tl, B_WIDTH).astype(x.dtype)
    y = jnp.concatenate([ao.astype(x.dtype), bo], axis=-1) * jax.nn.silu(gate)
    return x + y @ w_out, new_k, new_v, s_new

def _blockdiag(u, w, bias):
    b, tl = u.shape[:2]
    y = jnp.einsum('btnc,ncd->btnd', u.reshape(b, tl, C_BLOCKS, C_BLOCK), w)
    return y.reshape(b, tl, C_WIDTH) + bias

def _lin_comb(l, r):
    a1, b1 = l
    a2, b2 = r
    return a1 * a2, a2 * b1 + b2

def _odd_layer(x, hist, h0, norm_g, w_in, conv_w, conv_b, w_ra, b_ra, w_ri, b_ri, lam, w_out):
    b, tl, _ = x.shape
    h = _rmsnorm(x, norm_g)
    xb, gate = _split(h @ w_in, (C_WIDTH, C_WIDTH))
    xp = jnp.concatenate([hist.astype(xb.dtype), xb], axis=1)
    u = sum(xp[:, j:j + tl] * conv_w[j] for j in range(CONV_W)) + conv_b
    new_conv = xp[:, -(CONV_W - 1):]
    rg = jax.nn.sigmoid(_blockdiag(u, w_ra, b_ra).astype(jnp.float32))
    ig = jax.nn.sigmoid(_blockdiag(u, w_ri, b_ri).astype(jnp.float32))
    log_a = -LRU_C * rg * jax.nn.softplus(-lam.astype(jnp.float32))
    a = jnp.exp(log_a)
    bterm = jnp.sqrt(-jnp.expm1(2.0 * log_a)) * ig * u.astype(jnp.float32)
    bterm = bterm.at[:, 0].add(a[:, 0] * h0.astype(jnp.float32))
    _, hs = lax.associative_scan(_lin_comb, (a, bterm), axis=1)
    y = hs.astype(x.dtype) * jax.nn.silu(gate)
    return x + y @ w_out, new_conv, hs[:, -1]

def setup_inputs(seed: int = 0) -> dict:
    key = jax.random.key(seed)
    ks = jax.random.split(key, 32)
    f32 = jnp.float32
    nrm = lambda k, s, sc: jax.random.normal(k, s, f32) * sc
    u = jax.random.uniform(ks[26], (N_ODD, C_WIDTH), f32, 0.9, 0.999) ** (1.0 / LRU_C)
    return {
        "x_prompt": nrm(ks[0], (BATCH, SEQ, D_MODEL), 1.0),
        "x_sample": nrm(ks[1], (DEC_BATCH, DEC_SEQ, D_MODEL), 1.0),
        "cache_swa_k": nrm(ks[2], (N_EVEN, DEC_BATCH, WIN_ROWS, A_KV_HEADS, A_HEAD_DIM), 1.0),
        "cache_swa_v": nrm(ks[3], (N_EVEN, DEC_BATCH, WIN_ROWS, A_KV_HEADS, A_HEAD_DIM), 1.0),
        "state_gla": nrm(ks[4], (N_EVEN, DEC_BATCH, B_HEADS, B_DK, B_DV), 1.0),
        "cache_conv": nrm(ks[5], (N_ODD, DEC_BATCH, CONV_W - 1, C_WIDTH), 1.0),
        "state_lru": nrm(ks[6], (N_ODD, DEC_BATCH, C_WIDTH), 1.0),
        "norm_even": 1.0 + nrm(ks[7], (N_EVEN, D_MODEL), 0.02),
        "w_in_even": nrm(ks[8], (N_EVEN, D_MODEL, IN_EVEN), D_MODEL ** -0.5),
        "w_gate_lr": nrm(ks[9], (N_EVEN, B_LOWRANK, B_HEADS * B_DK), B_LOWRANK ** -0.5),
        "b_gate_lr": nrm(ks[10], (N_EVEN, B_HEADS * B_DK), 0.1),
        "sinks": nrm(ks[11], (N_EVEN, A_HEADS), 0.5),
        "gla_norm": 1.0 + nrm(ks[12], (N_EVEN, B_DV), 0.02),
        "w_out_even": nrm(ks[13], (N_EVEN, MIX_EVEN, D_MODEL), MIX_EVEN ** -0.5),
        "norm_odd": 1.0 + nrm(ks[14], (N_ODD, D_MODEL), 0.02),
        "w_in_odd": nrm(ks[15], (N_ODD, D_MODEL, IN_ODD), D_MODEL ** -0.5),
        "conv_w": nrm(ks[16], (N_ODD, CONV_W, C_WIDTH), CONV_W ** -0.5),
        "conv_b": nrm(ks[17], (N_ODD, C_WIDTH), 0.02),
        "w_rg_a": nrm(ks[18], (N_ODD, C_BLOCKS, C_BLOCK, C_BLOCK), C_BLOCK ** -0.5),
        "b_rg_a": nrm(ks[19], (N_ODD, C_WIDTH), 0.02),
        "w_rg_i": nrm(ks[20], (N_ODD, C_BLOCKS, C_BLOCK, C_BLOCK), C_BLOCK ** -0.5),
        "b_rg_i": nrm(ks[21], (N_ODD, C_WIDTH), 0.02),
        "lru_lambda": jnp.log(u / (1.0 - u)),
        "w_out_odd": nrm(ks[22], (N_ODD, C_WIDTH, D_MODEL), C_WIDTH ** -0.5),
        "norm_final": 1.0 + nrm(ks[23], (D_MODEL,), 0.02),
    }

def reference(x_prompt, x_sample, cache_swa_k, cache_swa_v, state_gla, cache_conv, state_lru,
              norm_even, w_in_even, w_gate_lr, b_gate_lr, sinks, gla_norm, w_out_even,
              norm_odd, w_in_odd, conv_w, conv_b, w_rg_a, b_rg_a, w_rg_i, b_rg_i, lru_lambda,
              w_out_odd, norm_final):
    xp, xs = x_prompt, x_sample
    pk, pv, pg, pc, pl = [], [], [], [], []
    sk, sv, sg, sc, sl = [], [], [], [], []
    for layer in range(DEPTH):
        if layer % 2 == 0:
            e = layer // 2
            wts = (norm_even[e], w_in_even[e], w_gate_lr[e], b_gate_lr[e], sinks[e], gla_norm[e], w_out_even[e])
            xp, k_, v_, s_ = _even_layer(xp, None, *wts)
            pk.append(k_); pv.append(v_); pg.append(s_)
            xs, k_, v_, s_ = _even_layer(xs, (cache_swa_k[e], cache_swa_v[e], state_gla[e]), *wts)
            sk.append(k_); sv.append(v_); sg.append(s_)
        else:
            o = layer // 2
            wts = (norm_odd[o], w_in_odd[o], conv_w[o], conv_b[o], w_rg_a[o], b_rg_a[o],
                   w_rg_i[o], b_rg_i[o], lru_lambda[o], w_out_odd[o])
            hist0 = jnp.zeros((xp.shape[0], CONV_W - 1, C_WIDTH), xp.dtype)
            h00 = jnp.zeros((xp.shape[0], C_WIDTH), jnp.float32)
            xp, c_, l_ = _odd_layer(xp, hist0, h00, *wts)
            pc.append(c_); pl.append(l_)
            xs, c_, l_ = _odd_layer(xs, cache_conv[o], state_lru[o], *wts)
            sc.append(c_); sl.append(l_)
    y_prompt = _rmsnorm(xp, norm_final)
    y_sample = _rmsnorm(xs, norm_final)
    new_swa_k_prompt = jnp.stack(pk)
    new_swa_v_prompt = jnp.stack(pv)
    new_gla_prompt = jnp.stack(pg)
    new_conv_prompt = jnp.stack(pc)
    new_lru_prompt = jnp.stack(pl)
    new_swa_k_sample = jnp.stack(sk)
    new_swa_v_sample = jnp.stack(sv)
    new_gla_sample = jnp.stack(sg)
    new_conv_sample = jnp.stack(sc)
    new_lru_sample = jnp.stack(sl)
    return (y_prompt, y_sample, new_swa_k_prompt, new_swa_v_prompt, new_gla_prompt, new_conv_prompt,
            new_lru_prompt, new_swa_k_sample, new_swa_v_sample, new_gla_sample, new_conv_sample,
            new_lru_sample)


_drawn_inputs = setup_inputs


def setup_inputs(seed=0):
    import zlib

    import numpy as np

    out = dict(_drawn_inputs(seed))
    spreads = {}
    factors = {'cache_swa_k': 3.08,
     'sinks': 16.128,
     'gla_norm': 7.379,
     'norm_odd': 2.822,
     'b_rg_a': 8.0,
     'b_rg_i': 7.725,
     'norm_final': 8.399}
    for name, (base, spread) in spreads.items():
        noise = np.random.default_rng([zlib.crc32(name.encode()), seed]).standard_normal(out[name].shape)
        drawn = base * np.exp(spread * noise) if base else spread * noise
        out[name] = __import__('jax').numpy.asarray(drawn.astype(out[name].dtype))
    for name, factor in factors.items():
        out[name] = (out[name] * factor).astype(out[name].dtype)
    return out
```

```python
from contextlib import ExitStack

import numpy as np

import concourse.bass as bass
from concourse import mybir

F32 = mybir.dt.float32
F32R = mybir.dt.float32r
ALU = mybir.AluOpType
ACT = mybir.ActivationFunctionType
AX = mybir.AxisListType

P = 128
DM = 1024
SEQ, DEC = 1024, 64
LIVE = SEQ + DEC
NCH = 3
CW = 364
TOK = NCH * CW
KD = DM // P
EPS = 1e-6
CHUNK = 64
A_HEADS, A_KV, A_DIM = 16, 4, 64
WIN = 128
B_HEADS, B_DK, B_DV, B_LOW = 4, 128, 256, 16
GATE_NORM = 16.0
CWID, CBLK, CONV_W = 1536, 192, 4
KC = CWID // P
EXT = CONV_W - 1
MIX = 16
OFF_Q, OFF_K, OFF_V, OFF_BQ, OFF_BK, OFF_BV, OFF_LR, OFF_G = 0, 1024, 1280, 1536, 2048, 2560, 3584, 3600

PIECE = 1024
PC_LR, PC_K, PC_V = 0, 1, 4
PC_A, A_PCS = 6, 4
PC_B, B_PCS = PC_A + A_KV * A_PCS, 6
PC_OE = PC_B + B_HEADS * B_PCS
PC_C, C_PCS = PC_OE + 2 * KD, 9
PC_OO = PC_C + 4 * C_PCS
PIECES = PC_OO + 2 * KD

USE_A = (3, 1)
USE_A1 = (USE_A[0] + 2, USE_A[1] + 2)
USE_B = (USE_A1[0] + 4 * (A_KV - 1), USE_A1[1])
USE_B1 = (USE_B[0] + 1, USE_B[1])
USE_OE = (USE_B1[0] + 3 * B_HEADS, USE_B1[1] + 3 * B_HEADS)
USE_N1 = (USE_OE[0] + 4, USE_OE[1] + 4)
USE_C = (USE_N1[0] + 1, USE_N1[1])
USE_OO = (USE_C[0] + 24, USE_C[1] + 24)
USE_N2 = (USE_OO[0] + 4, USE_OO[1] + 4)

VC_N = (0, 8, 16)
VC_BLR = 24
VC_GN = 28
VC_SINK = 30
VC_C = 46
VB = 12
VC_ALL = VC_C + KC * VB

CC_ID, CC_ONE, CC_CAUSAL, CC_DIST = 0, 128, 256, 384
CC_SLOPE = CC_DIST + 2 * P
CC_ALL = CC_SLOPE + A_HEADS

NT = 9
ATT_UNITS = 2 * NT

ARENA = 14400


def one(t, k):
    return t[bass.ds(k, 1)].rearrange("a p n -> p (a n)")


def slot(t, k, a=0, b=None):
    return t[:, bass.ds(k, 1), a:t.shape[2] if b is None else b].rearrange("p a n -> p (a n)")


def unit(u):
    return u % NT, u // NT


def key_cols(t):
    return (P, 2 * P) if t == 0 else (0, WIN + DEC) if t == NT - 1 else (0, 2 * P)


def c_use(m, n):
    return 3 + 3 * m + n


def tile_rows(t):
    return DEC if t == NT - 1 else P


def build_program(nc, xT, weights, vecs_d, consts_d, wlr_d, kc_d, vc_d, sg_d,
                  yT, k_out, v_out, gla_p_out, gla_s_out, conv_out, lru_out):
    k_all = nc.dram_tensor("k_scratch", (A_KV, A_DIM, SEQ + WIN + DEC), F32).ap()
    x1_d = nc.dram_tensor("x1_scratch", (KD, P, TOK), F32).ap()

    ctx = ExitStack()
    with ctx:
        at_byte = [32 * -(-nc.sbuf_base // 32)]

        def sb(name, shape, dt=F32, at=None):
            size = 4 * int(np.prod(shape[1:]))
            if at is None:
                at = at_byte[0]
                at_byte[0] += 32 * -(-size // 32)
            return nc.alloc_sbuf_tensor_at(name, shape, dt, offset=at)

        def sem(name):
            return ctx.enter_context(nc.semaphore(name))

        H = sb("H", [P, MIX, TOK], F32R)
        y_at = at_byte[0]
        Y = sb("Y", [P, MIX, TOK])
        Yr = sb("Yr", [P, MIX, TOK], F32R, at=y_at)
        raw = sb("raw", [P, 2, PIECE])
        w_hi = sb("w_hi", [P, 2, PIECE], F32R)
        w_lo = sb("w_lo", [P, 2, PIECE], F32R)
        vecs = sb("vecs", [P, VC_ALL])
        consts = sb("consts", [P, CC_ALL])
        wlr_cur = sb("wlr_cur", [P, P])
        sm = sb("sm", [P, 3, 12])
        nsink = sb("nsink", [P, A_HEADS])
        cur_sink = sb("cur_sink", [P, 3, 4])
        cur_b = sb("cur_b", [P, 4])
        cur = sb("cur", [P, 3, VB])
        nsp = sb("nsp", [P, KC, 4])
        cur_n = sb("cur_n", [P, 3, 4])
        lamt = sb("lamt", [P, KC])
        cvo = sb("cvo", [P, KC, 2 * EXT])
        lro = sb("lro", [P, KC, 2])
        arena_at = at_byte[0]
        arena = sb("arena", [P, ARENA])
        ur = sb("ur", [P, 2, 3, TOK], F32R, at=arena_at)

        def part(at, *shape):
            n = int(np.prod(shape))
            assert at + n <= ARENA
            v = arena[:, at:at + n]
            if len(shape) == 2:
                return v.rearrange("p (a b) -> p a b", a=shape[0])
            if len(shape) == 3:
                return v.rearrange("p (a b c) -> p a b c", a=shape[0], b=shape[1])
            return v

        X = part(0, KD, TOK)
        sq = part(KD * TOK, TOK)
        res = part(9 * TOK, 2, TOK)
        acc = part(11 * TOK, TOK)
        rb = part(12 * TOK, TOK)
        blrT = part(12 * TOK, TOK)
        KW = SEQ + WIN + DEC
        q = part(0, 2, TOK)
        kz = part(2184, 2, KW)
        Vz = part(4616, 10, 192)
        Ssb = part(6536, 3, 2, 256)
        PT = part(8072, 2, 512)
        V = Y[:, 8:11, :].rearrange("p a n -> p (a n)")[:, 0:2560].rearrange("p (a n) -> p a n", a=10)
        gt = Y[:, 12, :]
        kT = Y[:, 14:16, :]
        E = part(0, TOK)
        Ei = part(TOK, TOK)
        qg = part(2 * TOK, TOK)
        kg = part(3 * TOK, TOK)
        kd = part(4 * TOK, TOK)
        sq2 = part(2 * TOK, 2, TOK)
        gs = part(5 * TOK, 2, TOK)
        Vb = part(7 * TOK, NT, 256)
        o0 = 7 * TOK + NT * 256
        kdz = part(o0, 2, 2, P)
        aT = part(o0 + 512, 2, P)
        St = part(o0 + 768, 3, 256)
        Sst = part(o0 + 1536, 256)
        elast = part(o0 + 1792, LIVE // CHUNK)
        assert o0 + 1792 + LIVE // CHUNK <= 12 * TOK
        xc = part(6 * TOK, 1104)
        tr, ti, aa, th, sa = (part(6 * TOK + 1104 + n * TOK, TOK) for n in range(5))
        gc = part(11 * TOK + 1104, TOK)
        U = Y[:, 12:15, :]

        ps = ctx.enter_context(nc.psum_tensor("ps", [P, 8, 512], F32))
        sets = [ps[:, 0:3, :], ps[:, 3:6, :]]

        def chunks(ap):
            return ap.rearrange("p (c n) -> p c n", c=NCH)

        def setv(s):
            return sets[s][:, :, 0:CW]

        ident = consts[:, CC_ID:CC_ID + P]
        ones = consts[:, CC_ONE:CC_ONE + P]
        causal = consts[:, CC_CAUSAL:CC_CAUSAL + P]
        dist = consts[:, CC_DIST:CC_DIST + 2 * P]

        w_in = [sem("w_in0"), sem("w_in1")]
        x_in = [sem(f"x_in{b}") for b in range(KD)]
        vecs_in, consts_in, wlr_in, vcache_in = sem("vecs_in"), sem("consts_in"), sem("wlr_in"), sem("vcache_in")
        k_all_in, kz_in, gstate_in = sem("k_all_in"), sem("kz_in"), sem("gstate_in")
        res_in = [sem("res_in0"), sem("res_in1")]
        x1_saved, k_saved, v_saved, gla_saved = sem("x1_saved"), sem("k_saved"), sem("v_saved"), sem("gla_saved")
        small_saved, y_saved = sem("small_saved"), sem("y_saved")
        w_hi_done, w_split, piece_done = sem("w_hi_done"), sem("w_split"), sem("piece_done")
        drained = [sem("drained0"), sem("drained1")]
        acc_zero, sq_done, acc_done, ssq_done = sem("acc_zero"), sem("sq_done"), sem("acc_done"), sem("ssq_done")
        std_done, rstd_done, xn_done = sem("std_done"), sem("rstd_done"), sem("xn_done")
        h_hi_done, h_lo_done = sem("h_hi_done"), sem("h_lo_done")
        v_done, v_free = sem("v_done"), sem("v_free")
        a_zeroed, vz_ready, gate_tanh = sem("a_zeroed"), sem("vz_ready"), sem("gate_tanh")
        sink_neg, sink_cur = sem("sink_neg"), sem("sink_cur")
        s_done, s_free, mx_done, nm_done, ds_done = sem("s_done"), sem("s_free"), sem("mx_done"), sem("nm_done"), sem("ds_done")
        exp_done, den_done, rcp_done, p_done = sem("exp_done"), sem("den_done"), sem("rcp_done"), sem("p_done")
        pt_done, pt_free, o_done, o_free = sem("pt_done"), sem("pt_free"), sem("o_done"), sem("o_free")
        bias_ready, lora_done, z_act, z_neg, z_sub, gc_done = (sem(n) for n in (
            "bias_ready", "lora_done", "z_act", "z_neg", "z_sub", "gc_done"))
        e_done, kd_done, s0_ready, b_gate = sem("e_done"), sem("kd_done"), sem("s0_ready"), sem("b_gate")
        el_done, kt_done, y_zeroed = sem("el_done"), sem("kt_done"), sem("y_zeroed")
        at_done, kdt_done, at_masked, kdz_done, kdz_zeroed = (sem(n) for n in (
            "at_done", "kdt_done", "at_masked", "kdz_done", "kdz_zeroed"))
        gds_done, s_upd, go_done, go_saved = sem("gds_done"), sem("s_upd"), sem("go_done"), sem("go_saved")
        sq2_done, gn_done, gn_std, gn_rstd, bn_done, b_done = (sem(n) for n in (
            "sq2_done", "gn_done", "gn_std", "gn_rstd", "bn_done", "b_done"))
        y_hi_done, y_lo_done = sem("y_hi_done"), sem("y_lo_done")
        lam_act, nsp_ready, cur_ready, xc_zeroed = (sem(n) for n in (
            "lam_act", "nsp_ready", "cur_ready", "xc_zeroed"))
        cv_step, cv_done, u_hi_done, u_lo_done, cvo_done = (sem(n) for n in (
            "cv_step", "cv_done", "u_hi_done", "u_lo_done", "cvo_done"))
        c_tanh, c_gates, c_a, c_w, c_sqrt, c_iu, c_b, c_scan, c_y, lro_done = (sem(n) for n in (
            "c_tanh", "c_gates", "c_a", "c_w", "c_sqrt", "c_iu", "c_b", "c_scan", "c_y", "lro_done"))

        block = ctx.enter_context(nc.Block())

        @block.sync
        def _(sp):
            for s in range(2):
                sp.dma_start(raw[:, s, :], weights[s]).then_inc(w_in[s], 16)
            with sp.Fori(1, PIECES // 2) as i:
                for s in range(2):
                    sp.wait_ge(w_split, 2 * i + (s - 1))
                    sp.dma_start(raw[:, s, :], one(weights, 2 * i + s)).then_inc(w_in[s], 16)

        @block.gpsimd
        def _(pool):
            def split(i, s, first):
                pool.wait_ge(w_in[s], 16 * i + 16)
                if not first:
                    pool.wait_ge(piece_done, 2 * i + (s - 1))
                pool.tensor_tensor(w_hi[:, s, :].rearrange("p (k n) -> p k n", n=P),
                                   raw[:, s, :].rearrange("p (k n) -> p k n", n=P), every_tile_ones,
                                   ALU.mult).then_inc(w_hi_done, 1)
                pool.wait_ge(w_hi_done, 2 * i + (s + 1))
                pool.tensor_tensor(w_lo[:, s, :], raw[:, s, :], w_hi[:, s, :].bitcast(F32),
                                   ALU.subtract).then_inc(w_split, 1)

            every_tile_ones = ones.rearrange("p (k n) -> p k n", k=1).to_broadcast([P, PIECE // P, P])
            pool.wait_ge(consts_in, 16)
            for s in range(2):
                split(0, s, True)
            with pool.Fori(1, PIECES // 2) as i:
                for s in range(2):
                    split(i, s, False)

        @block.tensor
        def _(pe):
            def project(s, kts, piece, rhs_hi, rhs_lo, st, first=True, last=True, at0=0, ready=None):
                pe.wait_ge(w_split, piece + 1)
                for n, k in enumerate(kts):
                    if ready is not None:
                        pe.wait_ge(ready[0], ready[1] + k + 1)
                    w = slice((at0 + n) * P, (at0 + n + 1) * P)
                    for m, (lw, rx) in enumerate(((w_hi, rhs_hi), (w_lo, rhs_hi), (w_hi, rhs_lo))):
                        for c in range(NCH):
                            mm = pe.matmul(sets[st][:, c, 0:CW], lw[:, s, w], rx[:, k, c * CW:(c + 1) * CW],
                                           start=(first and n == 0 and m == 0),
                                           stop=(last and n == len(kts) - 1 and m == 2))
                return mm

            H_hi, H_lo = H[:, 0:KD, :], H[:, KD:2 * KD, :]
            K8 = range(KD)

            def in_block(s, st, piece, before):
                pe.wait_ge(drained[st], before)
                project(s, K8, piece, H_hi, H_lo, st).then_inc(piece_done, 1)

            def sum_squares(n, before):
                pe.wait_ge(acc_done, KD * (n + 1))
                if n:
                    pe.wait_ge(drained[0], before)
                for c in range(NCH):
                    mm = pe.matmul(sets[0][:, c, 0:CW], ones, acc[:, c * CW:(c + 1) * CW], start=True, stop=True)
                mm.then_inc(ssq_done, 1)

            def project_v(piece, base):
                pe.wait_ge(w_split, piece + 2)
                for t in range(NT):
                    m = TOK - SEQ if t == NT - 1 else P
                    if t >= 2:
                        pe.wait_ge(v_free, base + t - 1)
                    for k in K8:
                        wk = slice((k % 4) * 256, (k % 4) * 256 + 256)
                        for n, (lx, rw) in enumerate(((H_hi, w_hi), (H_hi, w_lo), (H_lo, w_hi))):
                            mm = pe.matmul(ps[0:m, 6 + t % 2, 0:256], lx[:, k, t * P:t * P + m], rw[:, k // 4, wk],
                                           start=(k == 0 and n == 0), stop=(k == KD - 1 and n == 2))
                    if t < NT - 1:
                        mm.then_inc(v_done, 1)
                mm.then_inc(piece_done, 2)

            pe.sem_inc(pt_done, 3)
            pe.sem_inc(o_done, 2)

            pe.wait_ge(consts_in, 16)
            sum_squares(0, 0)
            pe.wait_ge(drained[0], 1)
            for k in K8:
                a = project(0, [k], PC_LR, H_hi, H_lo, 0, first=(k == 0), last=(k == KD - 1), at0=k, ready=(h_lo_done, 0))
                if k == KD - 1:
                    a.then_inc(piece_done, 1)
                b = project(1, [k], PC_K, H_hi, H_lo, 1, first=(k == 0), last=(k == KD - 1), at0=k)
            b.then_inc(piece_done, 1)
            pe.wait_ge(drained[0], 2)
            project(0, K8, PC_K + 1, H_hi, H_lo, 0).then_inc(piece_done, 2)
            project_v(PC_V, 0)

            for n in range(A_PCS):
                in_block(n % 2, n % 2, PC_A + n, USE_A[n % 2] + n // 2)
            pe.wait_ge(v_free, NT)
            pe.wait_ge(drained[1], USE_A1[1])
            pe.wait_ge(a_zeroed, 3)

            def scores(u, U):
                t, b = unit(u)
                r = tile_rows(t)
                pe.wait_ge(s_free, U + 1)
                k0, k1, c0 = (SEQ, KW, 0) if t == NT - 1 else ((t - 1) * P, (t + 1) * P, 0)
                if t == 0:
                    k0, c0 = 0, P
                pe.matmul(ps[0:r, 3 + u % 2, :].rearrange("p (j n) -> p j n", j=2)[:, :, c0:c0 + k1 - k0],
                          q[:, b, t * P:t * P + r], kz[:, :, k0:k1], start=True, stop=True).then_inc(s_done, 1)

            def key_tiles(t):
                if t == NT - 1:
                    return [(0, 8, P), (1, 9, DEC)]
                return ([(0, t - 1, P)] if t else []) + [(1, t, P)]

            def transposes(u, U):
                t, _ = unit(u)
                pe.wait_ge(pt_free, U + 1)
                pe.wait_ge(p_done, U + 1)
                for kt, _, rows in key_tiles(t):
                    for j in range(2):
                        mm = pe.transpose(ps[0:rows, 5 + u % 2, (2 * kt + j) * P:(2 * kt + j + 1) * P],
                                          Ssb[:, u % 3, j, kt * P:kt * P + rows], ident)
                mm.then_inc(pt_done, 1)

            def mix_values(u, U):
                t, _ = unit(u)
                r = tile_rows(t)
                pe.wait_ge(pt_free, U + 3)
                pe.wait_ge(o_free, U + 1)
                tiles = key_tiles(t)
                for n, (kt, tile, rows) in enumerate(tiles):
                    for j in range(2):
                        mm = pe.matmul(ps[:, 7, 0:r], Vz[0:rows, tile, 64 * (1 - j):64 * (1 - j) + P],
                                       PT[0:rows, u % 2, (2 * kt + j) * P:(2 * kt + j) * P + r],
                                       start=(n == 0 and j == 0), stop=(n == len(tiles) - 1 and j == 1))
                mm.then_inc(o_done, 1)

            def attend(g, more):
                pe.wait_ge(drained[0], USE_A1[0] + 4 * g)
                pe.wait_ge(kz_in, 32 * g + 32)
                pe.wait_ge(vz_ready, g + 1)
                U = ATT_UNITS * g
                for s in range(ATT_UNITS + 3):
                    if s < ATT_UNITS:
                        scores(s, U + s)
                    if 0 <= s - 2 < ATT_UNITS:
                        transposes(s - 2, U + (s - 2))
                    if s >= 3:
                        mix_values(s - 3, U + (s - 3))
                    if more and s < 20:
                        n, f = s // 5, s % 5
                        if f == 0:
                            pe.wait_ge(drained[0], USE_A1[0] + 4 * g + n)
                            pe.wait_ge(w_split, PC_A + A_PCS * (g + 1) + n + 1)
                        for x in range(5 * f, min(5 * f + 5, 3 * KD)):
                            k, m = x // 3, x % 3
                            lw, rx = ((w_hi, H_hi), (w_lo, H_hi), (w_hi, H_lo))[m]
                            for c in range(NCH):
                                mm = pe.matmul(sets[0][:, c, 0:CW], lw[:, n % 2, k * P:(k + 1) * P],
                                               rx[:, k, c * CW:(c + 1) * CW], start=(x == 0), stop=(x == 3 * KD - 1))
                        if f == 4:
                            mm.then_inc(piece_done, 1)

            with pe.Fori(0, A_KV - 1) as g:
                attend(g, True)
            attend(A_KV - 1, False)

            def low_rank(h, before):
                pe.wait_ge(wlr_in, 16 * h + 16)
                pe.wait_ge(drained[0], before)
                for c in range(NCH):
                    mm = pe.matmul(sets[0][:, c, 0:CW], wlr_cur[:, :], blrT[:, c * CW:(c + 1) * CW],
                                   start=True, stop=True)
                mm.then_inc(lora_done, 1)

            low_rank(0, USE_B[0])
            pe.wait_ge(pt_free, A_KV * ATT_UNITS + 2)
            pe.wait_ge(o_free, A_KV * ATT_UNITS + 1)
            with pe.Fori(0, B_HEADS) as i:
                u0, u1 = USE_B1[0] + 3 * i, USE_B1[1] + 3 * i
                piece = PC_B + B_PCS * i
                in_block(0, 0, piece, u0)
                in_block(1, 1, piece + 1, u1)
                low_rank(i + 1, u0 + 1)
                project_v(piece + 2, NT * (i + 1))
                pe.wait_ge(kd_done, i + 1)
                pe.wait_ge(drained[0], u0 + 2)
                pe.wait_ge(drained[1], u1 + 1)
                pe.wait_ge(v_free, NT * (i + 2))
                T0 = NT * i

                def front(t):
                    r = tile_rows(t)
                    if t >= 2:
                        pe.wait_ge(at_masked, T0 + t - 1)
                        pe.wait_ge(kdz_done, T0 + t - 1)
                    cols = slice(t * P, t * P + r)
                    pe.matmul(ps[0:r, t % 2, 0:r], kg[:, cols], qg[:, cols], start=True, stop=True).then_inc(at_done, 1)
                    pe.transpose(ps[0:r, 2 + 3 * (t % 2), 0:P], kd[:, cols], ident).then_inc(kdt_done, 1)

                def back(t):
                    r = tile_rows(t)
                    pe.wait_ge(kdz_done, T0 + t + 1)
                    for h in range(r // CHUNK):
                        n = 2 * t + h
                        if n >= 2:
                            pe.wait_ge(s_upd, 17 * i + n - 1)
                        pe.matmul(ps[:, 6 + h, 0:256], kdz[0:r, t % 2, h, :], Vb[0:r, t, :],
                                  start=True, stop=True).then_inc(gds_done, 1)
                    pe.wait_ge(at_masked, T0 + t + 1)
                    if t >= 2:
                        pe.wait_ge(go_saved, T0 + t - 1)
                    if t == 0:
                        pe.wait_ge(s0_ready, i + 1)
                    if t == NT - 1:
                        pe.wait_ge(gstate_in, 16 * i + 16)
                    for e in range(2):
                        cols = slice(e * P, (e + 1) * P)
                        pe.matmul(ps[:, 3 + t % 2, e * P:e * P + r], Vb[0:r, t, cols], aT[0:r, t % 2, 0:r],
                                  start=True, stop=False)
                        for h in range(r // CHUNK):
                            n = 2 * t + h
                            if n and t < NT - 1:
                                pe.wait_ge(s_upd, 17 * i + n)
                            state = Sst[:, cols] if t == NT - 1 else St[:, n % 3, cols]
                            mm = pe.matmul(ps[:, 3 + t % 2, e * P + h * CHUNK:e * P + (h + 1) * CHUNK], state,
                                           qg[:, n * CHUNK:(n + 1) * CHUNK], start=False, stop=(h == r // CHUNK - 1))
                    mm.then_inc(go_done, 1)

                front(0)
                for t in range(NT):
                    if t + 1 < NT:
                        front(t + 1)
                    back(t)
                pe.wait_ge(go_saved, T0 + NT)
                pe.wait_ge(at_masked, T0 + NT)
                pe.wait_ge(kdz_done, T0 + NT)
                in_block(0, 1, piece + 4, u1 + 1)
                in_block(1, 0, piece + 5, u0 + 2)
                pe.wait_ge(drained[1], u1 + 2)
                pe.wait_ge(sq2_done, i + 1)
                for c in range(NCH):
                    for e in range(2):
                        mm = pe.matmul(sets[1][:, c, 0:CW], ones, sq2[:, e, c * CW:(c + 1) * CW],
                                       start=(e == 0), stop=(e == 1))
                mm.then_inc(gn_done, 1)

            def out_projection(kt, base, use, ready):
                def pair(i, first):
                    for s in range(2):
                        piece = base + 4 * i + 2 * s
                        pe.wait_ge(drained[s], use[s] + i)
                        rd = (y_lo_done, ready) if first and s == 0 else None
                        project(0, range(kt), piece, H, Yr, s, last=False, ready=rd).then_inc(piece_done, 1)
                        project(1, range(kt, 2 * kt), piece + 1, H, Yr, s, first=False, ready=rd)\
                            .then_inc(piece_done, 1)
                pair(0, True)
                with pe.Fori(1, KD // 2) as i:
                    pair(i, False)

            out_projection(8, PC_OE, USE_OE, 0)
            sum_squares(1, USE_N1[0])

            U_hi, U_lo = ur[:, 0, :, :], ur[:, 1, :, :]
            with pe.Fori(0, 2) as i:
                for p in range(2):
                    piece = PC_C + 2 * C_PCS * i + C_PCS * p
                    u = [USE_C[st] + 12 * i + 6 * p for st in range(2)]
                    G = 6 * i + 3 * p
                    for n in range(3):
                        pe.wait_ge(drained[n % 2], u[n % 2] + n // 2)
                        project((p + n) % 2, K8, piece + n, H_hi, H_lo, n % 2,
                                ready=(h_lo_done, KD) if (p, n) == (0, 0) else None).then_inc(piece_done, 1)
                    for m in range(3):
                        kts = ((0, 1), (0, 1, 2), (1, 2))[m]
                        for n in range(2):
                            v = c_use(m, n)
                            pe.wait_ge(drained[v % 2], u[v % 2] + v // 2)
                            if n == 0 and m < 2:
                                pe.wait_ge(u_lo_done, G + 2 + m)
                            project((p + 3 + 2 * m) % 2, kts, piece + 3 + 2 * m, U_hi, U_lo, v % 2,
                                    at0=n * len(kts)).then_inc(piece_done if n else c_gates, 1)
                        v = c_use(m, 2)
                        in_block((p + 4 + 2 * m) % 2, v % 2, piece + 4 + 2 * m, u[v % 2] + v // 2)
            out_projection(6, PC_OO, USE_OO, MIX)
            sum_squares(2, USE_N2[0])

        @block.scalar
        def _(act):
            act.dma_start(consts[:, :], consts_d).then_inc(consts_in, 16)
            act.dma_start(vecs[:, :], vecs_d).then_inc(vecs_in, 16)
            for b in range(KD):
                act.dma_start(X[:, b, :], xT[b]).then_inc(x_in[b], 16)

            act.sem_inc(pt_free, 2)

            def norm_rest(n, use):
                act.wait_ge(drained[0], use)
                act.activation(rb, rb, ACT.Sqrt).then_inc(std_done, 1)
                if n == 2:
                    return
                for b in range(KD):
                    act.wait_ge(xn_done, KD * n + b + 1)
                    act.activation(H[:, b, :], X[:, b, :], ACT.Copy).then_inc(h_hi_done, 1)

            for b in range(KD):
                act.wait_ge(x_in[b], 16)
                if b:
                    act.wait_ge(acc_done, b)
                act.activation(sq, X[:, b, :], ACT.Square).then_inc(sq_done, 1)
            norm_rest(0, 1)

            act.dma_start(k_all[:, :, SEQ:SEQ + WIN], kc_d).then_inc(k_all_in, 16)
            act.dma_start(V[:, 8, :], vc_d).then_inc(vcache_in, 16)
            act.wait_ge(h_lo_done, KD)
            act.wait_ge(piece_done, PC_LR + 1)
            act.activation(chunks(blrT), setv(0), ACT.Copy).then_inc(drained[0], 1)
            for b in range(2):
                act.wait_ge(piece_done, PC_K + b + 1)
                act.activation(chunks(kT[:, b, :]), setv(1 - b), ACT.Copy).then_inc(drained[1 - b], 1)
                act.wait_ge(drained[1 - b], (1, 3)[b])
                for dst, c0, c1, d0, done in ((k_all, 0, SEQ, 0, k_all_in), (k_all, SEQ, LIVE, SEQ + WIN, k_all_in),
                                              (k_out, SEQ - WIN, LIVE, 0, k_saved)):
                    act.dma_start(dst[2 * b:2 * b + 2, :, d0:d0 + c1 - c0].rearrange("g d n -> (g d) n"),
                                  kT[:, b, c0:c1]).then_inc(done, 16)

            def load_keys(g):
                for j in range(2):
                    act.dma_start(kz[64 * j:64 * j + 64, j, :], one(k_all, g)).then_inc(kz_in, 16)

            act.wait_ge(k_all_in, 80)
            act.wait_ge(a_zeroed, 3)
            load_keys(0)
            for t in range(NT):
                r = tile_rows(t)
                if t < NT - 1:
                    act.wait_ge(v_done, t + 1)
                else:
                    act.wait_ge(piece_done, PC_V + 2)
                act.activation(V[0:r, t if t < 8 else 9, :], ps[0:r, 6 + t % 2, 0:256], ACT.Copy).then_inc(v_free, 1)
            act.wait_ge(v_free, NT)
            act.dma_start(v_out[0:P, :], V[:, 7, :]).then_inc(v_saved, 16)
            act.dma_start(v_out[P:P + DEC, :], V[0:DEC, 9, :]).then_inc(v_saved, 16)

            def head_block(n, st, piece, before):
                act.wait_ge(piece_done, piece + 1)
                if n < 2:
                    if n:
                        act.wait_ge(drained[before[0]], before[1])
                    act.activation(chunks(gt), setv(st), ACT.Tanh, scale=0.5).then_inc(gate_tanh, 1)
                else:
                    act.activation(chunks(q[:, n - 2, :]), setv(st), ACT.Copy).then_inc(drained[st], 1)

            for n in range(A_PCS):
                head_block(n, n % 2, PC_A + n, (0, USE_A[0] + 1))

            def attend(g, more):
                U = ATT_UNITS * g
                for s in range(ATT_UNITS + 3):
                    if more and s and s % 5 == 0:
                        head_block(s // 5 - 1, 0, PC_A + A_PCS * (g + 1) + (s // 5 - 1), (0, USE_A1[0] + 4 * g + 1))
                    if s < ATT_UNITS:
                        t, r3 = unit(s)[0], s % 3
                        r = tile_rows(t)
                        c0, c1 = key_cols(t)
                        act.wait_ge(ds_done, U + s + 1)
                        for j in range(2):
                            act.activation(Ssb[0:r, r3, j, c0:c1], Ssb[0:r, r3, j, c0:c1], ACT.Exp,
                                           bias=sm[0:r, r3, 2 + j:3 + j], scale=float(A_DIM) ** -0.5,
                                           accum_out=sm[0:r, r3, 6 + j:7 + j])
                        act.activation(sm[0:r, r3, 8:10], sm[0:r, r3, 4:6], ACT.Exp).then_inc(exp_done, 1)
                    if more and s == ATT_UNITS - 1:
                        load_keys(g + 1)
                    if 2 <= s < ATT_UNITS + 2:
                        u = s - 2
                        t, _ = unit(u)
                        r = tile_rows(t)
                        act.wait_ge(pt_done, U + u + 4)
                        act.wait_ge(o_done, U + u + 1)
                        if t == NT - 1:
                            for kt, rows in ((0, P), (1, DEC)):
                                last = act.activation(
                                    PT[0:rows, u % 2, 2 * kt * P:2 * (kt + 1) * P].rearrange(
                                        "p (j n) -> p j n", j=2)[:, :, 0:r],
                                    ps[0:rows, 5 + u % 2, 2 * kt * P:2 * (kt + 1) * P].rearrange(
                                        "p (j n) -> p j n", j=2)[:, :, 0:r], ACT.Copy)
                        else:
                            c = 2 * P if t == 0 else 0
                            last = act.activation(PT[:, u % 2, c:512], ps[:, 5 + u % 2, c:512], ACT.Copy)
                        last.then_inc(pt_free, 1)

            with act.Fori(0, A_KV - 1) as g:
                attend(g, True)
            attend(A_KV - 1, False)
            act.wait_ge(v_saved, 32)
            act.wait_ge(k_saved, 32)

            def low_rank_in(h):
                act.dma_start(wlr_cur[:, :], one(wlr_d, h)).then_inc(wlr_in, 16)
                act.activation(cur_b[:, 0:1], vecs[:, bass.ds(VC_BLR + h, 1)], ACT.Copy).then_inc(bias_ready, 1)

            def log_gate(h):
                act.wait_ge(lora_done, h + 1)
                act.activation(chunks(E), setv(0), ACT.Abs, bias=cur_b[:, 0:1]).then_inc(z_act, 1)
                act.wait_ge(z_act, 3 * h + 1)
                act.activation(E, E, ACT.Exp, scale=-1.0).then_inc(z_act, 1)
                act.wait_ge(z_act, 3 * h + 2)
                act.activation(E, E, ACT.Ln, bias=1.0).then_inc(z_act, 1)

            def decays(h):
                act.wait_ge(gc_done, h + 1)
                act.activation(Ei, E, ACT.Exp, scale=-1.0 / GATE_NORM).then_inc(e_done, 1)
                act.wait_ge(e_done, 2 * h + 1)
                act.activation(E, E, ACT.Exp, scale=1.0 / GATE_NORM).then_inc(e_done, 1)

            act.wait_ge(vecs_in, 16)
            act.dma_start(wlr_cur[:, :], wlr_d[0]).then_inc(wlr_in, 16)
            act.activation(cur_b[:, 0:1], vecs[:, VC_BLR:VC_BLR + 1], ACT.Copy).then_inc(bias_ready, 1)
            act.wait_ge(bias_ready, 1)
            act.wait_ge(vz_ready, A_KV)
            act.wait_ge(o_free, A_KV * ATT_UNITS + 1)
            act.wait_ge(kdz_zeroed, 1)
            log_gate(0)
            decays(0)
            with act.Fori(0, B_HEADS) as i:
                piece = PC_B + B_PCS * i
                act.dma_start(Sst, one(sg_d, i)).then_inc(gstate_in, 16)
                low_rank_in(i + 1)
                act.wait_ge(bias_ready, i + 2)
                act.wait_ge(kd_done, i + 1)
                act.wait_ge(drained[1], USE_B1[1] + 3 * i + 1)
                act.wait_ge(el_done, i + 1)
                log_gate(i + 1)
                for t in range(NT):
                    r = tile_rows(t)
                    if t < NT - 1:
                        act.wait_ge(v_done, (NT - 1) * (i + 1) + t + 1)
                    else:
                        act.wait_ge(piece_done, piece + 4)
                    act.activation(Vb[0:r, t, :], ps[0:r, 6 + t % 2, 0:256], ACT.Copy).then_inc(v_free, 1)
                    if t == 4:
                        decays(i + 1)
                T0 = NT * i
                for t in range(NT):
                    act.wait_ge(kdt_done, T0 + t + 1)
                    if t >= 2:
                        act.wait_ge(go_done, T0 + t - 1)
                    for h in range(tile_rows(t) // CHUNK):
                        rows = slice(h * CHUNK, (h + 1) * CHUNK)
                        last = act.activation(kdz[rows, t % 2, h, :], ps[rows, 2 + 3 * (t % 2), 0:P], ACT.Copy)
                    last.then_inc(kdz_done, 1)
                act.wait_ge(s_upd, 17 * i + 16)
                act.dma_start(one(gla_p_out, i), St[:, 16 % 3, :]).then_inc(gla_saved, 16)
                act.wait_ge(s_upd, 17 * i + 17)
                act.wait_ge(go_saved, T0 + NT)
                act.dma_start(one(gla_s_out, i), St[:, 17 % 3, :]).then_inc(gla_saved, 16)
                act.activation(sq2, Y[:, bass.ds(2 * i + 8, 2), :], ACT.Square).then_inc(sq2_done, 1)
                for n in range(2):
                    act.wait_ge(piece_done, piece + 5 + n)
                    act.activation(chunks(gs[:, n, :]), setv(1 - n), ACT.Tanh, scale=0.5).then_inc(b_gate, 1)
                act.wait_ge(drained[1], USE_B1[1] + 3 * i + 3)
                act.activation(kd, kd, ACT.Sqrt).then_inc(gn_std, 1)
                act.wait_ge(b_done, i + 1)

            def split_mix(n, base, piece):
                act.wait_ge(piece_done, piece)
                with act.Fori(0, n) as k:
                    act.activation(slot(H, k), slot(Y, k), ACT.Copy).then_inc(y_hi_done, 1)

            def out_residual(src, use, nsq, spill):
                for s in range(2):
                    act.dma_start(res[:, s, :], src[s]).then_inc(res_in[s], 16)

                for b in range(KD):
                    i, s = b // 2, b % 2
                    act.wait_ge(drained[s], use[s] + i + 1)
                    if b + 2 < KD:
                        act.dma_start(res[:, s, :], src[b + 2]).then_inc(res_in[s], 16)
                    if spill:
                        act.dma_start(x1_d[b], X[:, b, :]).then_inc(x1_saved, 16)
                    act.wait_ge(acc_done, nsq + b)
                    act.activation(sq, X[:, b, :], ACT.Square).then_inc(sq_done, 1)

            split_mix(MIX, 0, PC_OE)
            out_residual(xT, USE_OE, KD, True)
            act.wait_ge(x1_saved, 16 * KD)
            norm_rest(1, USE_N1[0] + 1)

            act.wait_ge(vecs_in, 16)
            act.activation(lamt[:, :], vecs[:, VC_C:VC_ALL].rearrange("p (b n) -> p b n", n=VB)[:, :, 7], ACT.Abs)\
               .then_inc(lam_act, 1)
            act.wait_ge(lam_act, 1)
            act.activation(lamt[:, :], lamt[:, :], ACT.Exp, scale=-1.0).then_inc(lam_act, 1)
            act.wait_ge(lam_act, 2)
            act.activation(lamt[:, :], lamt[:, :], ACT.Ln, bias=1.0).then_inc(lam_act, 1)
            act.wait_ge(xc_zeroed, 1)
            with act.Fori(0, 2) as i:
                for p in range(2):
                    piece = PC_C + 2 * C_PCS * i + C_PCS * p
                    u = [USE_C[st] + 12 * i + 6 * p for st in range(2)]
                    G = 6 * i + 3 * p
                    act.wait_ge(cur_ready, 2 * i + p + 1)
                    for n in range(3):
                        st = n % 2
                        act.wait_ge(piece_done, piece + n + 1)
                        if n:
                            act.wait_ge(cvo_done, G + n)
                        act.activation(xc[:, EXT:EXT + 2 * CW].rearrange("p (c n) -> p c n", c=2),
                                       sets[st][:, 0:2, 0:CW], ACT.Copy)
                        act.activation(xc[:, EXT + 2 * CW:EXT + SEQ], sets[st][:, 2, 0:SEQ - 2 * CW], ACT.Copy)
                        act.activation(xc[:, EXT + SEQ:2 * EXT + SEQ], cur[:, n, 9:12], ACT.Copy)
                        act.activation(xc[:, 2 * EXT + SEQ:2 * EXT + LIVE], sets[st][:, 2, SEQ - 2 * CW:LIVE - 2 * CW],
                                       ACT.Copy).then_inc(drained[st], 1)
                        act.wait_ge(cv_done, G + n + 1)
                        act.activation(ur[:, 0, n, :], U[:, n, :], ACT.Copy).then_inc(u_hi_done, 1)
                    for m in range(3):
                        vr, vi, vg = (c_use(m, n) for n in range(3))
                        act.wait_ge(c_gates, G + m + 1)
                        act.activation(chunks(tr), setv(vr % 2), ACT.Tanh, bias=cur_n[:, m, 2:3], scale=0.5)\
                           .then_inc(drained[vr % 2], 1)
                        act.wait_ge(piece_done, piece + 4 + 2 * m)
                        if m:
                            act.wait_ge(c_scan, 2 * G + 2 * m)
                        act.activation(chunks(ti), setv(vi % 2), ACT.Tanh, bias=cur_n[:, m, 3:4], scale=0.5)\
                           .then_inc(drained[vi % 2], 1)
                        act.wait_ge(drained[vr % 2], u[vr % 2] + vr // 2 + 1)
                        act.activation(aa, tr, ACT.Exp, bias=cur_n[:, m, 0:1], scale=cur_n[:, m, 0:1]).then_inc(c_a, 1)
                        act.activation(th, tr, ACT.Tanh, bias=cur_n[:, m, 1:2], scale=cur_n[:, m, 1:2])
                        act.wait_ge(c_a, 2 * G + 2 * m + 1)
                        if m:
                            act.wait_ge(c_y, G + m)
                        act.activation(sa, aa, ACT.Square).then_inc(c_a, 1)
                        act.wait_ge(c_w, G + m + 1)
                        act.activation(th, th, ACT.Sqrt).then_inc(c_sqrt, 1)
                        act.wait_ge(piece_done, piece + 5 + 2 * m)
                        act.activation(chunks(gc), setv(vg % 2), ACT.Tanh, scale=0.5).then_inc(c_tanh, 1)
                    act.wait_ge(c_y, G + 3)
            act.wait_ge(lro_done, 12)
            act.dma_start(conv_out, cvo[:, :, :]).then_inc(small_saved, 16)
            act.dma_start(lru_out, lro[:, :, :]).then_inc(small_saved, 16)

            split_mix(KC, MIX, PC_OO)
            out_residual(x1_d, USE_OO, 2 * KD, False)
            norm_rest(2, USE_N2[0] + 1)
            for b in range(KD):
                act.wait_ge(xn_done, 2 * KD + b + 1)
                act.dma_start(yT[b], X[:, b, :]).then_inc(y_saved, 16)
            act.wait_ge(y_saved, 16 * KD)
            act.wait_ge(small_saved, 32)
            act.wait_ge(gla_saved, 32 * B_HEADS)
            act.wait_ge(k_saved, 32)
            act.wait_ge(v_saved, 32)

        @block.vector
        def _(dve):
            dve.sem_inc(s_free, 2)
            dve.sem_inc(o_free, 1)
            dve.memset(acc, 0.0).then_inc(acc_zero, 1)

            def norm(n):
                dve.wait_ge(ssq_done, n + 1)
                dve.tensor_scalar(chunks(rb), setv(0), 1.0 / DM, EPS, ALU.mult, ALU.add).then_inc(drained[0], 1)
                dve.wait_ge(std_done, n + 1)
                dve.reciprocal(rb, rb).then_inc(rstd_done, 1)
                dve.wait_ge(rstd_done, n + 1)
                for b in range(KD + 1):
                    if b < KD:
                        g = vecs[:, VC_N[n] + b:VC_N[n] + b + 1]
                        dve.scalar_tensor_tensor(X[:, b, :], X[:, b, :], g, rb, ALU.mult, ALU.mult)\
                           .then_inc(xn_done, 1)
                    if b and n < 2:
                        dve.wait_ge(h_hi_done, KD * n + b)
                        dve.tensor_tensor(H[:, KD + b - 1, :], X[:, b - 1, :], H[:, b - 1, :].bitcast(F32),
                                          ALU.subtract).then_inc(h_lo_done, 1)

            dve.wait_ge(acc_zero, 1)
            for b in range(KD):
                if b:
                    dve.wait_ge(acc_done, b)
                dve.wait_ge(sq_done, b + 1)
                dve.tensor_tensor(acc, acc, sq, ALU.add).then_inc(acc_done, 1)
            dve.wait_ge(vecs_in, 16)
            norm(0)

            dve.wait_ge(h_lo_done, KD)
            dve.memset(kz[64:P, 0, :], 0.0).then_inc(a_zeroed, 1)
            dve.memset(kz[0:64, 1, :], 0.0).then_inc(a_zeroed, 1)
            dve.memset(Vz[:, :, :], 0.0).then_inc(a_zeroed, 1)
            dve.tensor_scalar(nsink[:, :], vecs[:, VC_SINK:VC_SINK + A_HEADS], -1.0, None, ALU.mult)\
               .then_inc(sink_neg, 1)
            dve.wait_ge(a_zeroed, 3)
            dve.wait_ge(sink_neg, 1)
            dve.wait_ge(v_free, NT)
            dve.wait_ge(vcache_in, 16)
            dve.wait_ge(consts_in, 16)

            def gate(k, st):
                dve.wait_ge(gate_tanh, k + 1)
                dve.scalar_tensor_tensor(chunks(slot(Y, k)), chunks(gt), 1.0, setv(st), ALU.add, ALU.mult)\
                   .then_inc(drained[st], 1)

            def attend(g, more):
                U = ATT_UNITS * g
                dve.tensor_copy(Vz[:, 0:9, 64:128], V[:, 0:9, bass.ds(A_DIM * g, A_DIM)])
                dve.tensor_copy(Vz[0:64, 9, 64:128], V[0:64, 9, bass.ds(A_DIM * g, A_DIM)]).then_inc(vz_ready, 1)
                dve.tensor_copy(cur_sink[:, 0, :], vecs[:, bass.ds(VC_SINK + 4 * g, 4)])
                dve.tensor_copy(cur_sink[:, 2, :], consts[:, bass.ds(CC_SLOPE + 4 * g, 4)])
                dve.tensor_copy(cur_sink[:, 1, :], nsink[:, bass.ds(4 * g, 4)]).then_inc(sink_cur, 1)
                dve.wait_ge(sink_cur, g + 1)
                for s in range(ATT_UNITS + 4):
                    if s >= 4:
                        u = s - 4
                        t, b = unit(u)
                        r = tile_rows(t)
                        dve.wait_ge(o_done, U + u + 3)
                        y = slot(Y, 2 * g + b, t * P, t * P + r)
                        dve.tensor_tensor(y, ps[:, 7, 0:r], y, ALU.mult).then_inc(o_free, 1)
                    if more and s in (5, 10):
                        gate(2 * g + (s // 5 + 1), 0)
                    if s < ATT_UNITS:
                        (t, b), r3 = unit(s), s % 3
                        r = tile_rows(t)
                        c0, c1 = key_cols(t)
                        dve.wait_ge(s_done, U + s + 1)
                        dve.wait_ge(pt_done, U + s + 1)
                        for j in range(2):
                            last = dve.scalar_tensor_tensor(
                                Ssb[0:r, r3, j, c0:c1], dist[0:r, c0:c1], cur_sink[0:r, 2, 2 * b + j:2 * b + j + 1],
                                ps[0:r, 3 + s % 2, j * 256 + c0:j * 256 + c1], ALU.mult, ALU.add)
                        last.then_inc(s_free, 1)
                        dve.wait_ge(s_free, U + s + 3)
                        dve.tensor_reduce(sm[0:r, r3, 0:2], Ssb[0:r, r3, :, c0:c1], AX.X, ALU.max).then_inc(mx_done, 1)
                        dve.wait_ge(mx_done, U + s + 1)
                        dve.scalar_tensor_tensor(sm[0:r, r3, 2:4], sm[0:r, r3, 0:2], -float(A_DIM) ** -0.5,
                                                 cur_sink[0:r, 1, 2 * b:2 * b + 2], ALU.mult, ALU.min)\
                           .then_inc(nm_done, 1)
                        dve.wait_ge(nm_done, U + s + 1)
                        dve.tensor_tensor(sm[0:r, r3, 4:6], sm[0:r, r3, 2:4], cur_sink[0:r, 0, 2 * b:2 * b + 2],
                                          ALU.add).then_inc(ds_done, 1)
                    if 0 <= s - 1 < ATT_UNITS:
                        u = s - 1
                        t, r3 = unit(u)[0], u % 3
                        r = tile_rows(t)
                        c0, c1 = key_cols(t)
                        dve.wait_ge(exp_done, U + u + 1)
                        dve.tensor_tensor(sm[0:r, r3, 8:10], sm[0:r, r3, 8:10], sm[0:r, r3, 6:8], ALU.add)\
                           .then_inc(den_done, 1)
                        dve.wait_ge(den_done, U + u + 1)
                        dve.reciprocal(sm[0:r, r3, 10:12], sm[0:r, r3, 8:10]).then_inc(rcp_done, 1)
                        dve.wait_ge(rcp_done, U + u + 1)
                        for j in range(2):
                            last = dve.tensor_scalar(Ssb[0:r, r3, j, c0:c1], Ssb[0:r, r3, j, c0:c1],
                                                     sm[0:r, r3, 10 + j:11 + j], 0.5, ALU.mult, ALU.mult)
                        last.then_inc(p_done, 1)

            for n in range(2):
                gate(n, n)
            for st in range(2):
                dve.wait_ge(drained[st], USE_A1[st])
            with dve.Fori(0, A_KV - 1) as g:
                attend(g, True)
            attend(A_KV - 1, False)

            dve.wait_ge(v_saved, 32)
            dve.wait_ge(k_saved, 32)
            dve.wait_ge(vz_ready, A_KV)
            dve.memset(Y[:, KD:MIX, LIVE:TOK], 0.0).then_inc(y_zeroed, 1)
            dve.wait_ge(y_zeroed, 1)
            dve.memset(kdz, 0.0).then_inc(kdz_zeroed, 1)

            def log_gate(h, use):
                dve.wait_ge(z_act, 3 * h + 1)
                dve.tensor_scalar(chunks(Ei), setv(0), cur_b[:, 0:1], 0.0, ALU.add, ALU.min).then_inc(drained[0], 1)
                dve.wait_ge(z_act, 3 * h + 3)
                dve.wait_ge(drained[0], use)
                dve.tensor_tensor(Ei, Ei, E, ALU.subtract).then_inc(z_sub, 1)
                dve.wait_ge(z_sub, h + 1)
                for c in range(0, TOK, CHUNK):
                    e = min(c + CHUNK, TOK)
                    last = dve.tensor_tensor_scan(E[:, c:e], ones[:, 0:e - c], Ei[:, c:e], 0.0, ALU.mult, ALU.add)
                last.then_inc(gc_done, 1)

            log_gate(0, USE_B[0] + 1)
            with dve.Fori(0, B_HEADS) as i:
                u0, u1 = USE_B1[0] + 3 * i, USE_B1[1] + 3 * i
                piece = PC_B + B_PCS * i
                dve.memset(St[:, 0, :], 0.0).then_inc(s0_ready, 1)
                dve.wait_ge(e_done, 2 * i + 2)
                dve.tensor_copy(elast, E[:, 0:LIVE].rearrange("p (c n) -> p c n", n=CHUNK)[:, :, CHUNK - 1])\
                   .then_inc(el_done, 1)
                dve.wait_ge(piece_done, piece + 1)
                dve.tensor_tensor(chunks(kg), setv(0), chunks(Ei), ALU.mult).then_inc(drained[0], 1)
                dve.wait_ge(drained[0], u0 + 1)
                dve.wait_ge(el_done, i + 1)
                dve.tensor_tensor(kd[:, 0:LIVE].rearrange("p (c n) -> p c n", n=CHUNK),
                                  kg[:, 0:LIVE].rearrange("p (c n) -> p c n", n=CHUNK),
                                  elast.rearrange("p (c n) -> p c n", n=1).to_broadcast([P, LIVE // CHUNK, CHUNK]),
                                  ALU.mult).then_inc(kd_done, 1)
                dve.wait_ge(piece_done, piece + 2)
                dve.scalar_tensor_tensor(chunks(qg), setv(1), float(B_DK) ** -0.5, chunks(E), ALU.mult, ALU.mult)\
                   .then_inc(drained[1], 1)
                dve.wait_ge(drained[1], u1 + 1)
                log_gate(i + 1, u0 + 2)
                T0 = NT * i
                dve.wait_ge(s0_ready, i + 1)

                def mask(t):
                    r = tile_rows(t)
                    dve.wait_ge(at_done, T0 + t + 1)
                    if t >= 2:
                        dve.wait_ge(go_done, T0 + t - 1)
                    dve.tensor_tensor(aT[0:r, t % 2, 0:r], ps[0:r, t % 2, 0:r], causal[0:r, 0:r], ALU.mult)\
                       .then_inc(at_masked, 1)

                def save(t):
                    r = tile_rows(t)
                    dve.wait_ge(go_done, T0 + t + 1)
                    dve.tensor_scalar(Y[:, bass.ds(2 * i + 8, 2), t * P:t * P + r],
                                      ps[:, 3 + t % 2, 0:256].rearrange("p (e n) -> p e n", e=2)[:, :, 0:r],
                                      1.0, None, ALU.mult).then_inc(go_saved, 1)

                mask(0)
                for t in range(NT):
                    if t + 1 < NT:
                        mask(t + 1)
                    if t:
                        save(t - 1)
                    for h in range(tile_rows(t) // CHUNK):
                        n = 2 * t + h
                        dve.wait_ge(gds_done, 17 * i + n + 1)
                        if n:
                            dve.wait_ge(s_upd, 17 * i + n)
                        if n >= 2:
                            dve.wait_ge(go_done, T0 + (n - 2) // 2 + 1)
                        if t == NT - 1:
                            dve.wait_ge(gstate_in, 16 * i + 16)
                        state = Sst if t == NT - 1 else St[:, n % 3, :]
                        dve.scalar_tensor_tensor(St[:, (n + 1) % 3, :], state, elast[:, n:n + 1],
                                                 ps[:, 6 + h, 0:256], ALU.mult, ALU.add).then_inc(s_upd, 1)
                save(NT - 1)
                for n in range(2):
                    dve.wait_ge(b_gate, 2 * i + n + 1)
                    g = chunks(gs[:, n, :])
                    dve.scalar_tensor_tensor(g, g, 1.0, setv(1 - n), ALU.add, ALU.mult).then_inc(drained[1 - n], 1)
                dve.wait_ge(drained[1], u1 + 2)
                dve.wait_ge(drained[0], u0 + 3)
                dve.wait_ge(gn_done, i + 1)
                dve.tensor_scalar(chunks(kd), setv(1), 1.0 / B_DV, EPS, ALU.mult, ALU.add).then_inc(drained[1], 1)
                dve.wait_ge(gn_std, i + 1)
                dve.reciprocal(kd, kd).then_inc(gn_rstd, 1)
                dve.wait_ge(gn_rstd, i + 1)
                for e in range(2):
                    y = slot(Y, 2 * i + 8 + e)
                    dve.scalar_tensor_tensor(y, y, vecs[:, VC_GN + e:VC_GN + e + 1], kd, ALU.mult, ALU.mult)\
                       .then_inc(bn_done, 1)
                for e in range(2):
                    y = slot(Y, 2 * i + 8 + e)
                    dve.wait_ge(bn_done, 2 * i + e + 1)
                    last = dve.scalar_tensor_tensor(y, y, 0.5, gs[:, e, :], ALU.mult, ALU.mult)
                last.then_inc(b_done, 1)
                dve.wait_ge(gla_saved, 32 * i + 32)

            def split_mix(n, base):
                with dve.Fori(0, n) as k:
                    dve.wait_ge(y_hi_done, base + k + 1)
                    dve.tensor_tensor(slot(Yr, k), slot(Y, k), slot(H, k).bitcast(F32), ALU.subtract)\
                       .then_inc(y_lo_done, 1)

            def out_residual(n, base, use, res_base):
                dve.memset(acc, 0.0).then_inc(acc_zero, 1)
                dve.wait_ge(acc_zero, n + 1)
                with dve.Fori(0, KD // 2) as i:
                    for s in range(2):
                        dve.wait_ge(piece_done, base + 4 * i + 2 * s + 2)
                        dve.wait_ge(res_in[s], 16 * (i + res_base + 1))
                        dve.tensor_tensor(chunks(slot(X, 2 * i + s)), setv(s), chunks(res[:, s, :]), ALU.add)\
                           .then_inc(drained[s], 1)
                        dve.wait_ge(sq_done, KD * n + 2 * i + s + 1)
                        dve.wait_ge(acc_done, KD * n + 2 * i + s)
                        dve.tensor_tensor(acc, acc, sq, ALU.add).then_inc(acc_done, 1)

            split_mix(MIX, 0)
            out_residual(1, PC_OE, USE_OE, 0)
            dve.wait_ge(x1_saved, 16 * KD)
            norm(1)

            lv = vecs[:, VC_C:VC_ALL].rearrange("p (b n) -> p b n", n=VB)
            lam = lv[:, :, 7]
            dve.tensor_scalar(nsp[:, :, 1], lam, -1.0, 0.0, ALU.mult, ALU.max).then_inc(nsp_ready, 1)
            dve.tensor_scalar(nsp[:, :, 2:4], lv[:, :, 5:7], 0.5, None, ALU.mult)
            dve.wait_ge(nsp_ready, 1)
            dve.wait_ge(lam_act, 3)
            dve.tensor_tensor(nsp[:, :, 0], nsp[:, :, 1], lamt[:, :], ALU.add).then_inc(nsp_ready, 1)
            dve.wait_ge(nsp_ready, 2)
            dve.tensor_scalar(nsp[:, :, 1], nsp[:, :, 0], 4.0, None, ALU.mult).then_inc(nsp_ready, 1)
            dve.wait_ge(nsp_ready, 3)
            dve.tensor_scalar(nsp[:, :, 0], nsp[:, :, 1], -1.0, None, ALU.mult).then_inc(nsp_ready, 1)
            dve.wait_ge(nsp_ready, 4)
            dve.wait_ge(h_lo_done, 2 * KD)
            dve.memset(xc, 0.0).then_inc(xc_zeroed, 1)
            with dve.Fori(0, 2) as i:
                for p in range(2):
                    u = [USE_C[st] + 12 * i + 6 * p for st in range(2)]
                    G = 6 * i + 3 * p
                    dve.tensor_copy(cur_n[:, :, :], nsp[:, bass.ds(G, 3), :])
                    dve.tensor_copy(cur[:, :, :].rearrange("p a b -> p (a b)"),
                                    vecs[:, bass.ds(VC_C + VB * G, 3 * VB)]).then_inc(cur_ready, 1)
                    dve.wait_ge(cur_ready, 2 * i + p + 1)
                    for n in range(3):
                        st = n % 2
                        dve.wait_ge(drained[st], u[st] + n // 2 + 1)
                        dve.tensor_scalar(U[:, n, :], xc[:, 0:TOK], cur[:, n, 0:1], cur[:, n, 4:5], ALU.mult, ALU.add)\
                           .then_inc(cv_step, 1)
                        for j in range(1, CONV_W):
                            dve.wait_ge(cv_step, 3 * G + 3 * n + j)
                            dve.scalar_tensor_tensor(U[:, n, :], xc[:, j:j + TOK], cur[:, n, j:j + 1], U[:, n, :],
                                                     ALU.mult, ALU.add).then_inc(cv_step if j < 3 else cv_done, 1)
                        dve.tensor_scalar(slot(cvo, G + n, 0, EXT), xc[:, SEQ:SEQ + EXT], 1.0, None, ALU.mult)
                        dve.tensor_scalar(slot(cvo, G + n, EXT, 2 * EXT), xc[:, LIVE + EXT:LIVE + 2 * EXT], 1.0, None,
                                          ALU.mult).then_inc(cvo_done, 1)
                        dve.wait_ge(cv_done, G + n + 1)
                        dve.wait_ge(u_hi_done, G + n + 1)
                        dve.tensor_tensor(ur[:, 1, n, :], U[:, n, :], ur[:, 0, n, :].bitcast(F32), ALU.subtract)\
                           .then_inc(u_lo_done, 1)
                    for m in range(3):
                        vr, vi, vg = (c_use(m, n) for n in range(3))
                        dve.wait_ge(c_a, 2 * G + 2 * m + 2)
                        dve.scalar_tensor_tensor(th, sa, 1.0, th, ALU.add, ALU.mult).then_inc(c_w, 1)
                        dve.wait_ge(drained[vi % 2], u[vi % 2] + vi // 2 + 1)
                        dve.scalar_tensor_tensor(ti, ti, 1.0, U[:, m, :], ALU.add, ALU.mult).then_inc(c_iu, 1)
                        dve.wait_ge(c_iu, G + m + 1)
                        dve.wait_ge(c_sqrt, G + m + 1)
                        dve.scalar_tensor_tensor(ti, ti, 0.5, th, ALU.mult, ALU.mult).then_inc(c_b, 1)
                        dve.wait_ge(c_b, G + m + 1)
                        s0 = SEQ + EXT
                        dve.tensor_tensor_scan(sa[:, 0:SEQ], aa[:, 0:SEQ], ti[:, 0:SEQ], 0.0, ALU.mult, ALU.add)\
                           .then_inc(c_scan, 1)
                        dve.tensor_tensor_scan(sa[:, s0:s0 + DEC], aa[:, s0:s0 + DEC], ti[:, s0:s0 + DEC],
                                               cur[:, m, 8:9], ALU.mult, ALU.add).then_inc(c_scan, 1)
                        dve.wait_ge(c_tanh, G + m + 1)
                        dve.scalar_tensor_tensor(chunks(slot(Y, G + m)), chunks(gc), 1.0, setv(vg % 2),
                                                 ALU.add, ALU.mult).then_inc(drained[vg % 2], 1)
                        dve.wait_ge(c_scan, 2 * G + 2 * m + 2)
                        dve.wait_ge(drained[vg % 2], u[vg % 2] + vg // 2 + 1)
                        dve.tensor_copy(slot(lro, G + m, 0, 1), sa[:, SEQ - 1:SEQ])
                        dve.tensor_copy(slot(lro, G + m, 1, 2), sa[:, s0 + DEC - 1:s0 + DEC]).then_inc(lro_done, 1)
                        y = slot(Y, G + m, 0, SEQ)
                        dve.scalar_tensor_tensor(y, sa[:, 0:SEQ], 0.5, y, ALU.mult, ALU.mult)
                        y = slot(Y, G + m, SEQ, LIVE)
                        dve.scalar_tensor_tensor(y, sa[:, s0:s0 + DEC], 0.5, y, ALU.mult, ALU.mult).then_inc(c_y, 1)

            split_mix(KC, MIX)
            out_residual(2, PC_OO, USE_OO, 4)
            norm(2)


def kernel(**inputs):
    import concourse.bacc as bacc
    from concourse.bass_utils import run_bass_kernel_spmd

    f = {k: np.asarray(v) for k, v in inputs.items()}
    w_in, w_oe = f["w_in_even"][0], f["w_out_even"][0]
    w_ino, w_oo = f["w_in_odd"][0], f["w_out_odd"][0]
    dt = w_in.dtype

    W = np.zeros((PIECES, P, PIECE), dt)

    def columns(piece, w, cols):
        kt = w.shape[0] // P
        W[piece, :, :kt * P] = w[:, cols].reshape(kt, P, P).transpose(1, 0, 2).reshape(P, kt * P)

    def values(piece, w, c):
        v = w[:, c:c + 256].reshape(2, 4, P, 256).transpose(0, 2, 1, 3).reshape(2, P, PIECE)
        W[piece:piece + 2] = v

    def block_of(c):
        return np.arange(c, c + P)

    values(PC_V, w_in, OFF_V)
    columns(PC_LR, w_in, block_of(OFF_LR))
    for b in range(2):
        columns(PC_K + b, w_in, block_of(OFF_K + b * P))
    for g in range(A_KV):
        for b in range(2):
            columns(PC_A + A_PCS * g + b, w_in, block_of(OFF_G + (2 * g + b) * P))
            columns(PC_A + A_PCS * g + 2 + b, w_in, block_of(OFF_Q + (2 * g + b) * P))
    for h in range(B_HEADS):
        a = PC_B + B_PCS * h
        columns(a, w_in, block_of(OFF_BK + h * P))
        columns(a + 1, w_in, block_of(OFF_BQ + h * P))
        values(a + 2, w_in, OFF_BV + h * B_DV)
        for b in range(2):
            columns(a + 4 + b, w_in, block_of(OFF_G + (8 + 2 * h + b) * P))
    for m in range(KD):
        for half in range(2):
            columns(PC_OE + 2 * m + half, w_oe[half * 8 * P:(half + 1) * 8 * P], block_of(m * P))
            columns(PC_OO + 2 * m + half, w_oo[half * 6 * P:(half + 1) * 6 * P], block_of(m * P))
    for g in range(4):
        a = PC_C + C_PCS * g
        for n in range(3):
            columns(a + n, w_ino, block_of((3 * g + n) * P))
            columns(a + 4 + 2 * n, w_ino, block_of(CWID + (3 * g + n) * P))
        for n, name in enumerate(("w_rg_a", "w_rg_i")):
            both = np.zeros((3 * P, 3 * P), dt)
            for b in range(2):
                sl = slice(b * CBLK, (b + 1) * CBLK)
                both[sl, sl] = f[name][0, 2 * g + b]
            for m, kts in enumerate(((0, 1), (0, 1, 2), (1, 2))):
                for x, kt in enumerate(kts):
                    at = n * len(kts) + x
                    W[a + 3 + 2 * m, :, at * P:(at + 1) * P] = both[kt * P:(kt + 1) * P, m * P:(m + 1) * P]

    xT = np.zeros((KD, P, TOK), dt)
    xT[:, :, :SEQ] = f["x_prompt"][0].T.reshape(KD, P, SEQ)
    xT[:, :, SEQ:LIVE] = f["x_sample"][0].T.reshape(KD, P, DEC)

    vecs = np.zeros((P, VC_ALL), dt)
    for n, name in enumerate(("norm_even", "norm_odd", "norm_final")):
        vecs[:, VC_N[n]:VC_N[n] + KD] = f[name].reshape(KD, P).T
    vecs[:, VC_BLR:VC_BLR + 4] = f["b_gate_lr"][0].reshape(4, P).T
    vecs[:, VC_GN:VC_GN + 2] = f["gla_norm"][0].reshape(2, P).T
    vecs[:, VC_SINK:VC_SINK + A_HEADS] = f["sinks"][0][None, :]
    lv = vecs[:, VC_C:].reshape(P, KC, VB)
    for j in range(CONV_W):
        lv[:, :, j] = f["conv_w"][0, j].reshape(KC, P).T
    for n, name in enumerate(("conv_b", "b_rg_a", "b_rg_i", "lru_lambda", "state_lru")):
        lv[:, :, CONV_W + n] = f[name][0].reshape(KC, P).T
    for j in range(EXT):
        lv[:, :, 9 + j] = f["cache_conv"][0, 0, j].reshape(KC, P).T

    consts = np.zeros((P, CC_ALL), np.float32)
    r = np.arange(P)
    consts[:, CC_ID:CC_ID + P] = np.eye(P)
    consts[:, CC_ONE:CC_ONE + P] = 1.0
    consts[:, CC_CAUSAL:CC_CAUSAL + P] = (r[:, None] // CHUNK == r[None, :] // CHUNK) & (r[:, None] <= r[None, :])
    j = np.arange(2 * P)
    far = (j[None, :] // CHUNK < r[:, None] // CHUNK) | (j[None, :] // CHUNK > r[:, None] // CHUNK + 2)
    consts[:, CC_DIST:CC_DIST + 2 * P] = np.where(far, 1e34, np.abs(WIN + r[:, None] - j[None, :]))
    consts[:, CC_SLOPE:] = -(2.0 ** (-8.0 * np.arange(1, A_HEADS + 1) / A_HEADS)).astype(np.float32) * A_DIM ** 0.5

    wlr = np.zeros((B_HEADS + 1, P, P), dt)
    wlr[:B_HEADS, :B_LOW] = f["w_gate_lr"][0].reshape(B_LOW, B_HEADS, P).transpose(1, 0, 2)
    arrays = {
        "xT": xT, "weights": W, "vecs_in": vecs, "consts_in": consts, "wlr_in": wlr,
        "k_cache": np.ascontiguousarray(f["cache_swa_k"][0, 0].transpose(1, 2, 0)),
        "v_cache": np.ascontiguousarray(f["cache_swa_v"][0, 0].reshape(WIN, A_KV * A_DIM)),
        "gla_state": np.ascontiguousarray(f["state_gla"][0, 0]),
    }
    outs = {
        "yT": (KD, P, TOK), "k_new": (A_KV, A_DIM, WIN + DEC), "v_new": (WIN + DEC, A_KV * A_DIM),
        "gla_p": (B_HEADS, B_DK, B_DV), "gla_s": (B_HEADS, B_DK, B_DV),
        "conv_new": (P, KC, 2 * EXT), "lru_new": (P, KC, 2),
    }
    nc = bacc.Bacc("TRN2", target_bir_lowering=False, num_devices=1, dynamic_dma_scratch_size=1024)
    args = [nc.dram_tensor(k, a.shape, mybir.dt.from_np(a.dtype), kind="ExternalInput").ap()
            for k, a in arrays.items()]
    args += [nc.dram_tensor(k, s, F32, kind="ExternalOutput").ap() for k, s in outs.items()]
    build_program(nc, *args)
    got = run_bass_kernel_spmd(nc, [arrays], core_ids=[0]).results[0]

    y = got["yT"].reshape(DM, TOK).T
    kn = got["k_new"].transpose(2, 0, 1)
    vn = got["v_new"].reshape(WIN + DEC, A_KV, A_DIM)
    cn = got["conv_new"].transpose(2, 1, 0).reshape(2, EXT, CWID)
    ln = got["lru_new"].transpose(2, 1, 0).reshape(2, CWID)
    return (y[None, :SEQ], y[None, SEQ:LIVE],
            kn[None, None, :WIN], vn[None, None, :WIN], got["gla_p"][None, None],
            cn[None, None, 0], ln[None, None, 0],
            kn[None, None, WIN:], vn[None, None, WIN:], got["gla_s"][None, None],
            cn[None, None, 1], ln[None, None, 1])
```

```python
from contextlib import ExitStack

import numpy as np

import concourse.bass as bass
from concourse import mybir

F32 = mybir.dt.float32
F32R = mybir.dt.float32r
ALU = mybir.AluOpType
ACT = mybir.ActivationFunctionType
AX = mybir.AxisListType

P = 128
DM = 1024
SEQ, DEC = 1024, 64
LIVE = SEQ + DEC
NCH = 3
CW = 364
TOK = NCH * CW
KD = DM // P
EPS = 1e-6
CHUNK = 64
A_HEADS, A_KV, A_DIM = 16, 4, 64
WIN = 128
B_HEADS, B_DK, B_DV, B_LOW = 4, 128, 256, 16
GATE_NORM = 16.0
CWID, CBLK, CONV_W = 1536, 192, 4
KC = CWID // P
EXT = CONV_W - 1
MIX = 16
OFF_Q, OFF_K, OFF_V, OFF_BQ, OFF_BK, OFF_BV, OFF_LR, OFF_G = 0, 1024, 1280, 1536, 2048, 2560, 3584, 3600

PIECE = 1024
PC_LR, PC_K, PC_V = 0, 1, 3
PC_A, A_PCS = 5, 4
PC_B0 = PC_A + A_KV * A_PCS
PC_B, B_PCS = PC_B0 + 2, 6
PC_OE = PC_B + B_HEADS * B_PCS - 2
PC_C, C_PCS = PC_OE + 2 * KD, 9
PC_OO = PC_C + 4 * C_PCS
PIECES = PC_OO + 2 * KD + 1
HALF = PIECE // 2

USE_A = (2, 1)
USE_A1 = (USE_A[0] + 2, USE_A[1] + 2)
USE_B0 = USE_A1[0] + 4 * (A_KV - 1)
USE_B = (USE_B0 + 3, USE_A1[1])
USE_OE = (USE_B[0] + 3 * B_HEADS - 2, USE_B[1] + 3 * B_HEADS - 1)
USE_C = (USE_OE[0] + 4, USE_OE[1] + 4)
USE_OO = (USE_C[0] + 24, USE_C[1] + 24)

VC_N = (0, 8, 16)
VC_BLR = 24
VC_GN = 28
VC_SINK = 30
VC_C = 46
VB = 12
VC_ALL = VC_C + KC * VB

CC_ID, CC_ONE, CC_CAUSAL, CC_DIST = 0, 128, 256, 384
CC_SLOPE = CC_DIST + 2 * P
CC_ALL = CC_SLOPE + A_HEADS

NT = 9
ATT_UNITS = 2 * NT
K0_STEPS = 7
LR_STEP = 2 * K0_STEPS + 1

ARENA = 14400


def one(t, k):
    return t[bass.ds(k, 1)].rearrange("a p n -> p (a n)")


def slot(t, k, a=0, b=None):
    return t[:, bass.ds(k, 1), a:t.shape[2] if b is None else b].rearrange("p a n -> p (a n)")


def unit(u):
    return u % NT, u // NT


def key_cols(t):
    return (P, 2 * P) if t == 0 else (0, WIN + DEC) if t == NT - 1 else (0, 2 * P)


def c_use(m, n):
    return 3 + 3 * m + n


def tile_rows(t):
    return DEC if t == NT - 1 else P


def build_program(nc, xT, weights, vecs_d, consts_d, wlr_d, kc_d, vc_d, sg_d,
                  yT, k_out, v_out, gla_p_out, gla_s_out, conv_out, lru_out):
    k_all = nc.dram_tensor("k_scratch", (A_KV, A_DIM, SEQ + WIN + DEC), F32).ap()
    x1_d = nc.dram_tensor("x1_scratch", (KD, P, TOK), F32).ap()

    ctx = ExitStack()
    with ctx:
        at_byte = [32 * -(-nc.sbuf_base // 32)]

        def sb(name, shape, dt=F32, at=None):
            size = 4 * int(np.prod(shape[1:]))
            if at is None:
                at = at_byte[0]
                at_byte[0] += 32 * -(-size // 32)
            return nc.alloc_sbuf_tensor_at(name, shape, dt, offset=at)

        def sem(name):
            return ctx.enter_context(nc.semaphore(name))

        H = sb("H", [P, MIX, TOK], F32R)
        y_at = at_byte[0]
        Y = sb("Y", [P, MIX, TOK])
        Yr = sb("Yr", [P, MIX, TOK], F32R, at=y_at)
        raw = sb("raw", [P, 2, PIECE])
        w_hi = sb("w_hi", [P, 2, PIECE], F32R)
        w_lo = sb("w_lo", [P, 2, PIECE], F32R)
        vecs = sb("vecs", [P, VC_ALL])
        consts = sb("consts", [P, CC_ALL])
        wlr_cur = sb("wlr_cur", [P, P])
        rT = sb("rT", [P, NT])
        sm = sb("sm", [P, 3, 12])
        nsink = sb("nsink", [P, A_HEADS])
        cur_sink = sb("cur_sink", [P, 3, 4])
        cur_b = sb("cur_b", [P, 4])
        cur = sb("cur", [P, 3, VB])
        nsp = sb("nsp", [P, KC, 4])
        cur_n = sb("cur_n", [P, 3, 4])
        lamt = sb("lamt", [P, KC])
        cvo = sb("cvo", [P, KC, 2 * EXT])
        lro = sb("lro", [P, KC, 2])
        arena_at = at_byte[0]
        arena = sb("arena", [P, ARENA])
        ur = sb("ur", [P, 2, 3, TOK], F32R, at=arena_at)

        def part(at, *shape):
            n = int(np.prod(shape))
            assert at + n <= ARENA
            v = arena[:, at:at + n]
            if len(shape) == 2:
                return v.rearrange("p (a b) -> p a b", a=shape[0])
            if len(shape) == 3:
                return v.rearrange("p (a b c) -> p a b c", a=shape[0], b=shape[1])
            return v

        X = part(0, KD, TOK)
        sq = part(KD * TOK, TOK)
        res = part(9 * TOK, 2, TOK)
        acc = part(ARENA - 2 * TOK, TOK)
        rb = part(ARENA - TOK, TOK)
        diag = part(9 * TOK, NT, P)
        blr_raw = part(9 * TOK + NT * P, TOK)
        blrT = part(ARENA - 2 * TOK, TOK)
        KW = SEQ + WIN + DEC
        q = part(0, 2, TOK)
        kz = part(2184, 2, KW)
        Vz = part(4616, 10, 192)
        Ssb = part(6536, 3, 2, 256)
        PT = part(8072, 2, 512)
        V = Y[:, 8:11, :].rearrange("p a n -> p (a n)")[:, 0:2560].rearrange("p (a n) -> p a n", a=10)
        gt = Y[:, 12, :]
        gz = Y[:, 13, :]
        kT = Y[:, 14:16, :]
        E = part(0, TOK)
        Ei = part(TOK, TOK)
        qg = part(2 * TOK, TOK)
        kg = part(3 * TOK, TOK)
        kd = part(4 * TOK, TOK)
        sq2 = part(2 * TOK, 2, TOK)
        gs = part(5 * TOK, 2, TOK)
        tb = part(7 * TOK, 2, TOK)
        Vb = part(7 * TOK, NT, 256)
        o0 = 7 * TOK + NT * 256
        kdz = part(o0, 2, 2, P)
        aT = part(o0 + 512, 2, P)
        St = part(o0 + 768, 3, 256)
        Sst = part(o0 + 1536, 256)
        elast = part(o0 + 1792, LIVE // CHUNK)
        assert o0 + 1792 + LIVE // CHUNK <= ARENA - 2 * TOK
        xc = part(6 * TOK, 1104)
        tr, ti, aa, th, sa = (part(6 * TOK + 1104 + n * TOK, TOK) for n in range(5))
        gc = th
        U = Y[:, 12:15, :]
        cgz = Y[:, 15, :]

        ps = ctx.enter_context(nc.psum_tensor("ps", [P, 8, 512], F32))
        sets = [ps[:, 0:3, :], ps[:, 3:6, :]]

        def chunks(ap):
            return ap.rearrange("p (c n) -> p c n", c=NCH)

        def setv(s):
            return sets[s][:, :, 0:CW]

        ident = consts[:, CC_ID:CC_ID + P]
        ones = consts[:, CC_ONE:CC_ONE + P]
        causal = consts[:, CC_CAUSAL:CC_CAUSAL + P]
        dist = consts[:, CC_DIST:CC_DIST + 2 * P]

        w_in = [sem("w_in0"), sem("w_in1")]
        x_in = [sem(f"x_in{b}") for b in range(KD)]
        vecs_in, consts_in, wlr_in, vcache_in = sem("vecs_in"), sem("consts_in"), sem("wlr_in"), sem("vcache_in")
        k_all_in, kz_in, gstate_in = sem("k_all_in"), sem("kz_in"), sem("gstate_in")
        res_in = [sem("res_in0"), sem("res_in1")]
        x1_saved, k_saved, v_saved, gla_saved = sem("x1_saved"), sem("k_saved"), sem("v_saved"), sem("gla_saved")
        small_saved, y_saved = sem("small_saved"), sem("y_saved")
        w_hi_done, w_split = sem("w_hi_done"), sem("w_split")
        half_done, piece_done = sem("half_done"), sem("piece_done")
        drained = [sem("drained0"), sem("drained1")]
        acc_zero, sq_done, acc_done, ssq_done = sem("acc_zero"), sem("sq_done"), sem("acc_done"), sem("ssq_done")
        ms_done, std_done, rt_done, diag_done = sem("ms_done"), sem("std_done"), sem("rt_done"), sem("diag_done")
        bc_done, rb_done, rt_init, xn_done = sem("bc_done"), sem("rb_done"), sem("rt_init"), sem("xn_done")
        h_hi_done, h_lo_done = sem("h_hi_done"), sem("h_lo_done")
        v_done, v_free = sem("v_done"), sem("v_free")
        a_zeroed, vz_ready, gate_tanh = sem("a_zeroed"), sem("vz_ready"), sem("gate_tanh")
        gated, blr_ready, es_done = sem("gated"), sem("blr_ready"), sem("es_done")
        sink_neg, sink_cur = sem("sink_neg"), sem("sink_cur")
        s_done, s_free, mx_done, nm_done, ds_done = sem("s_done"), sem("s_free"), sem("mx_done"), sem("nm_done"), sem("ds_done")
        exp_done, den_done, rcp_done, p_done = sem("exp_done"), sem("den_done"), sem("rcp_done"), sem("p_done")
        pt_done, pt_free, o_done, o_free = sem("pt_done"), sem("pt_free"), sem("o_done"), sem("o_free")
        bias_ready, lora_done, z_act, z_neg, z_sub, gc_done = (sem(n) for n in (
            "bias_ready", "lora_done", "z_act", "z_neg", "z_sub", "gc_done"))
        q_ready, k0_ready, e_done, kd_done, s0_ready, b_gate = sem("q_ready"), sem("k0_ready"), sem("e_done"), sem("kd_done"), sem("s0_ready"), sem("b_gate")
        el_done, kt_done, y_zeroed = sem("el_done"), sem("kt_done"), sem("y_zeroed")
        at_done, kdt_done, at_masked, kdz_done, kdz_zeroed = (sem(n) for n in (
            "at_done", "kdt_done", "at_masked", "kdz_done", "kdz_zeroed"))
        gds_done, s_upd, go_done, go_saved = sem("gds_done"), sem("s_upd"), sem("go_done"), sem("go_saved")
        sq2_done, gn_done, gn_std, gn_rstd, gs_done, bn_done, b_done = (sem(n) for n in (
            "sq2_done", "gn_done", "gn_std", "gn_rstd", "gs_done", "bn_done", "b_done"))
        y_hi_done, y_lo_done = sem("y_hi_done"), sem("y_lo_done")
        lam_act, nsp_ready, cur_ready, xc_zeroed = (sem(n) for n in (
            "lam_act", "nsp_ready", "cur_ready", "xc_zeroed"))
        cv_step, cv_done, u_hi_done, u_lo_done, cvo_done = (sem(n) for n in (
            "cv_step", "cv_done", "u_hi_done", "u_lo_done", "cvo_done"))
        c_tanh, c_a, c_w, c_sqrt, c_iu, c_b, c_scan, c_gy, c_y, lro_done = (sem(n) for n in (
            "c_tanh", "c_a", "c_w", "c_sqrt", "c_iu", "c_b", "c_scan", "c_gy", "c_y", "lro_done"))

        block = ctx.enter_context(nc.Block())

        @block.sync
        def _(sp):
            for s in range(2):
                sp.dma_start(raw[:, s, :], weights[s]).then_inc(w_in[s], 16)
            with sp.Fori(1, PIECES // 2) as i:
                for s in range(2):
                    sp.wait_ge(w_split, 4 * i + 2 * (s - 1))
                    sp.dma_start(raw[:, s, :], one(weights, 2 * i + s)).then_inc(w_in[s], 16)

        @block.gpsimd
        def _(pool):
            def split(i, s, first):
                pool.wait_ge(w_in[s], 16 * i + 16)
                for h in range(2):
                    cols = slice(h * HALF, (h + 1) * HALF)
                    if not first:
                        pool.wait_ge((half_done, piece_done)[h], 2 * i + (s - 1))
                    pool.tensor_tensor(w_hi[:, s, cols].rearrange("p (k n) -> p k n", n=P),
                                       raw[:, s, cols].rearrange("p (k n) -> p k n", n=P), every_tile_ones,
                                       ALU.mult).then_inc(w_hi_done, 1)
                    pool.wait_ge(w_hi_done, 4 * i + (2 * s + h + 1))
                    pool.tensor_tensor(w_lo[:, s, cols], raw[:, s, cols], w_hi[:, s, cols].bitcast(F32),
                                       ALU.subtract).then_inc(w_split, 1)

            every_tile_ones = ones.rearrange("p (k n) -> p k n", k=1).to_broadcast([P, HALF // P, P])
            pool.wait_ge(consts_in, 16)
            for s in range(2):
                split(0, s, True)
            with pool.Fori(1, PIECES // 2) as i:
                for s in range(2):
                    split(i, s, False)

        @block.tensor
        def _(pe):
            def project(s, kts, piece, rhs_hi, rhs_lo, st, first=True, last=True, at0=0, ready=None, half_end=3):
                for n, k in enumerate(kts):
                    if (at0 + n) % 4 == 0:
                        pe.wait_ge(w_split, 2 * piece + ((at0 + n) // 4 + 1))
                    if ready is not None:
                        pe.wait_ge(ready[0], ready[1] + k + 1)
                    w = slice((at0 + n) * P, (at0 + n + 1) * P)
                    for m, (lw, rx) in enumerate(((w_hi, rhs_hi), (w_lo, rhs_hi), (w_hi, rhs_lo))):
                        for c in range(NCH):
                            mm = pe.matmul(sets[st][:, c, 0:CW], lw[:, s, w], rx[:, k, c * CW:(c + 1) * CW],
                                           start=(first and n == 0 and m == 0),
                                           stop=(last and n == len(kts) - 1 and m == 2))
                    if at0 + n == half_end:
                        mm.then_inc(half_done, 1)
                return mm

            H_hi, H_lo = H[:, 0:KD, :], H[:, KD:2 * KD, :]
            K8 = range(KD)

            def in_block(s, st, piece, before):
                pe.wait_ge(drained[st], before)
                project(s, K8, piece, H_hi, H_lo, st).then_inc(piece_done, 1)

            def sum_squares(n):
                pe.wait_ge(acc_done, KD * (n + 1))
                for t in range(NT):
                    m = TOK - SEQ if t == NT - 1 else P
                    mm = pe.matmul(ps[0:m, 7, t:t + 1], acc[:, t * P:t * P + m], ones[:, 0:1], start=True, stop=True)
                mm.then_inc(ssq_done, 1)

            def broadcast(n, bank):
                pe.wait_ge(diag_done, n + 1)
                for t in range(NT):
                    m = TOK - SEQ if t == NT - 1 else P
                    dst = ps[:, bank, CW:CW + m] if t == NT - 1 else ps[:, 6 + t // 4, (t % 4) * P:(t % 4 + 1) * P]
                    mm = pe.matmul(dst, ones, diag[:, t, 0:m], start=True, stop=True)
                mm.then_inc(bc_done, 1)

            def project_v(piece, base, between=None):
                for t in range(NT):
                    if between and t == 4:
                        between()
                    m = TOK - SEQ if t == NT - 1 else P
                    if t >= 2:
                        pe.wait_ge(v_free, base + t - 1)
                    for k in K8:
                        if t == 0 and k % 2 == 0:
                            pe.wait_ge(w_split, 2 * piece + (k // 2 + 1))
                        wk = slice((k % 4) * 256, (k % 4) * 256 + 256)
                        s = 1 - k // 4
                        for n, (lx, rw) in enumerate(((H_hi, w_hi), (H_hi, w_lo), (H_lo, w_hi))):
                            mm = pe.matmul(ps[0:m, 6 + t % 2, 0:256], lx[:, k, t * P:t * P + m], rw[:, s, wk],
                                           start=(k == 0 and n == 0), stop=(k == KD - 1 and n == 2))
                        if t == NT - 1 and k % 2:
                            mm.then_inc((half_done, piece_done)[k // 2 % 2], 1)
                    if t < NT - 1:
                        mm.then_inc(v_done, 1)

            pe.sem_inc(pt_done, 3)
            pe.sem_inc(o_done, 2)

            def low_rank_input(k):
                mm = project(0, [k], PC_LR, H_hi, H_lo, 0, first=(k == 0), last=(k == KD - 1), at0=k, ready=(h_lo_done, 0))
                if k == KD - 1:
                    mm.then_inc(piece_done, 1)

            for k in range(3):
                low_rank_input(k)
            for k in K8:
                if k + 3 < KD:
                    low_rank_input(k + 3)
                b = project(1, [k], PC_K, H_hi, H_lo, 1, first=(k == 0), last=(k == KD - 1), at0=k)
            b.then_inc(piece_done, 1)
            pe.wait_ge(drained[0], 1)
            for k in K8:
                if k == 2:
                    sum_squares(0)
                if k == 6:
                    broadcast(0, 5)
                a = project(0, [k], PC_K + 1, H_hi, H_lo, 0, first=(k == 0), last=(k == KD - 1), at0=k)
            a.then_inc(piece_done, 1)
            pe.wait_ge(rb_done, 1)
            project_v(PC_V, 0)

            for n in range(A_PCS):
                in_block(1 - n % 2, n % 2, PC_A + n, USE_A[n % 2] + n // 2)
            pe.wait_ge(v_free, NT)
            pe.wait_ge(drained[1], USE_A1[1])
            pe.wait_ge(a_zeroed, 3)

            def scores(u, U):
                t, b = unit(u)
                r = tile_rows(t)
                pe.wait_ge(s_free, U + 1)
                k0, k1, c0 = (SEQ, KW, 0) if t == NT - 1 else ((t - 1) * P, (t + 1) * P, 0)
                if t == 0:
                    k0, c0 = 0, P
                pe.matmul(ps[0:r, 3 + u % 2, :].rearrange("p (j n) -> p j n", j=2)[:, :, c0:c0 + k1 - k0],
                          q[:, b, t * P:t * P + r], kz[:, :, k0:k1], start=True, stop=True).then_inc(s_done, 1)

            def key_tiles(t):
                if t == NT - 1:
                    return [(0, 8, P), (1, 9, DEC)]
                return ([(0, t - 1, P)] if t else []) + [(1, t, P)]

            def transposes(u, U):
                t, _ = unit(u)
                pe.wait_ge(pt_free, U + 1)
                pe.wait_ge(p_done, U + 1)
                for kt, _, rows in key_tiles(t):
                    for j in range(2):
                        mm = pe.transpose(ps[0:rows, 5 + u % 2, (2 * kt + j) * P:(2 * kt + j + 1) * P],
                                          Ssb[:, u % 3, j, kt * P:kt * P + rows], ident)
                mm.then_inc(pt_done, 1)

            def mix_values(u, U):
                t, _ = unit(u)
                r = tile_rows(t)
                pe.wait_ge(pt_free, U + 3)
                pe.wait_ge(o_free, U + 1)
                tiles = key_tiles(t)
                for n, (kt, tile, rows) in enumerate(tiles):
                    for j in range(2):
                        mm = pe.matmul(ps[:, 7, 0:r], Vz[0:rows, tile, 64 * (1 - j):64 * (1 - j) + P],
                                       PT[0:rows, u % 2, (2 * kt + j) * P:(2 * kt + j) * P + r],
                                       start=(n == 0 and j == 0), stop=(n == len(tiles) - 1 and j == 1))
                mm.then_inc(o_done, 1)

            def low_rank(h, before):
                pe.wait_ge(wlr_in, 16 * h + 16)
                pe.wait_ge(drained[0], before)
                for c in range(NCH):
                    mm = pe.matmul(sets[0][:, c, 0:CW], wlr_cur[:, :], blrT[:, c * CW:(c + 1) * CW],
                                   start=True, stop=True)
                mm.then_inc(lora_done, 1)

            def attend(g, blocks, steps):
                pe.wait_ge(drained[0], USE_A1[0] + 4 * g)
                pe.wait_ge(kz_in, 32 * g + 32)
                pe.wait_ge(vz_ready, g + 1)
                U = ATT_UNITS * g
                tiles = -(-3 * KD // steps)
                for s in range(ATT_UNITS + 3):
                    if s < ATT_UNITS:
                        scores(s, U + s)
                    if 0 <= s - 2 < ATT_UNITS:
                        transposes(s - 2, U + (s - 2))
                    if s >= 3:
                        mix_values(s - 3, U + (s - 3))
                    if s < blocks * steps:
                        n, f = s // steps, s % steps
                        piece = PC_A + A_PCS * (g + 1) + n
                        if f == 0:
                            pe.wait_ge(drained[0], USE_A1[0] + 4 * g + n)
                        for x in range(tiles * f, min(tiles * (f + 1), 3 * KD)):
                            k, m = x // 3, x % 3
                            if k % 4 == 0 and m == 0:
                                pe.wait_ge(w_split, 2 * piece + (k // 4 + 1))
                            lw, rx = ((w_hi, H_hi), (w_lo, H_hi), (w_hi, H_lo))[m]
                            for c in range(NCH):
                                mm = pe.matmul(sets[0][:, c, 0:CW], lw[:, 1 - n % 2, k * P:(k + 1) * P],
                                               rx[:, k, c * CW:(c + 1) * CW], start=(x == 0), stop=(x == 3 * KD - 1))
                            if (k, m) == (3, 2):
                                mm.then_inc(half_done, 1)
                        if f == steps - 1:
                            mm.then_inc(piece_done, 1)
                    if blocks == 2 and s == LR_STEP:
                        pe.wait_ge(blr_ready, 1)
                        low_rank(0, USE_B0 + 2)

            with pe.Fori(0, A_KV - 1) as g:
                attend(g, A_PCS, 5)
            attend(A_KV - 1, 2, K0_STEPS)

            pe.wait_ge(pt_free, A_KV * ATT_UNITS + 2)
            pe.wait_ge(o_free, A_KV * ATT_UNITS + 1)
            def gla_head(i, last):
                u0, u1 = USE_B[0] + 3 * i, USE_B[1] + 3 * i
                piece = PC_B + B_PCS * i
                project_v(piece, NT * (i + 1), None if last else lambda: low_rank(i + 1, u0))
                pe.wait_ge(q_ready, i + 1)
                if not last:
                    pe.wait_ge(drained[0], u0 + 1)
                pe.wait_ge(v_free, NT * (i + 2))
                T0 = NT * i

                def front(t):
                    r = tile_rows(t)
                    if t >= 2:
                        pe.wait_ge(at_masked, T0 + t - 1)
                        pe.wait_ge(kdz_done, T0 + t - 1)
                    cols = slice(t * P, t * P + r)
                    pe.matmul(ps[0:r, t % 2, 0:r], kg[:, cols], qg[:, cols], start=True, stop=True).then_inc(at_done, 1)
                    pe.transpose(ps[0:r, 2 + 3 * (t % 2), 0:P], kd[:, cols], ident).then_inc(kdt_done, 1)

                def back(t):
                    r = tile_rows(t)
                    pe.wait_ge(kdz_done, T0 + t + 1)
                    for h in range(r // CHUNK):
                        n = 2 * t + h
                        if n >= 2:
                            pe.wait_ge(s_upd, 17 * i + n - 1)
                        pe.matmul(ps[:, 6 + h, 0:256], kdz[0:r, t % 2, h, :], Vb[0:r, t, :],
                                  start=True, stop=True).then_inc(gds_done, 1)
                    pe.wait_ge(at_masked, T0 + t + 1)
                    if t >= 2:
                        pe.wait_ge(go_saved, T0 + t - 1)
                    if t == 0:
                        pe.wait_ge(s0_ready, i + 1)
                    if t == NT - 1:
                        pe.wait_ge(gstate_in, 16 * i + 16)
                    for e in range(2):
                        cols = slice(e * P, (e + 1) * P)
                        pe.matmul(ps[:, 3 + t % 2, e * P:e * P + r], Vb[0:r, t, cols], aT[0:r, t % 2, 0:r],
                                  start=True, stop=False)
                        for h in range(r // CHUNK):
                            n = 2 * t + h
                            if n and t < NT - 1:
                                pe.wait_ge(s_upd, 17 * i + n)
                            state = Sst[:, cols] if t == NT - 1 else St[:, n % 3, cols]
                            mm = pe.matmul(ps[:, 3 + t % 2, e * P + h * CHUNK:e * P + (h + 1) * CHUNK], state,
                                           qg[:, n * CHUNK:(n + 1) * CHUNK], start=False, stop=(h == r // CHUNK - 1))
                    mm.then_inc(go_done, 1)

                front(0)
                for t in range(NT):
                    if t + 1 < NT:
                        front(t + 1)
                    back(t)
                pe.wait_ge(go_saved, T0 + NT)
                pe.wait_ge(at_masked, T0 + NT)
                pe.wait_ge(kdz_done, T0 + NT)
                u0 = u0 if last else u0 + 1
                in_block(1, 1, piece + 2, u1)
                in_block(0, 0, piece + 3, u0)
                pe.wait_ge(drained[1], u1 + 1)
                pe.wait_ge(sq2_done, i + 1)
                for c in range(NCH):
                    for e in range(2):
                        mm = pe.matmul(sets[1][:, c, 0:CW], ones, sq2[:, e, c * CW:(c + 1) * CW],
                                       start=(e == 0), stop=(e == 1))
                mm.then_inc(gn_done, 1)
                if not last:
                    in_block(1, 0, piece + 4, u0 + 1)
                    in_block(0, 1, piece + 5, u1 + 2)

            with pe.Fori(0, B_HEADS - 1) as i:
                gla_head(i, False)
            gla_head(B_HEADS - 1, True)

            def out_projection(kt, base, use, ready):
                def pair(i, first):
                    for half in range(2):
                        piece = base + 4 * i + 2 * half
                        if not half:
                            pe.wait_ge(drained[0], use[0] + i)
                        if first:
                            for k in range(3):
                                out_tile(0, kt, half, k, piece, ready)
                            for k in range(kt):
                                if k + 3 < kt:
                                    out_tile(0, kt, half, k + 3, piece, ready)
                                if k == 0 and not half:
                                    pe.wait_ge(drained[1], use[1])
                                out_tile(1, kt, half, k, piece + 1, ready)
                        else:
                            for s in range(2):
                                if s and not half:
                                    pe.wait_ge(drained[1], use[1] + i)
                                project(1 - s, range(half * kt, (half + 1) * kt), piece + s, H, Yr, s,
                                        first=not half, last=half == 1).then_inc(piece_done, 1)
                pair(0, True)
                with pe.Fori(1, KD // 2) as i:
                    pair(i, False)

            def out_tile(s, kt, half, k, piece, ready):
                row = half * kt + k
                mm = project(1 - s, [row], piece, H, Yr, s, first=(row == 0), last=(row == 2 * kt - 1), at0=k,
                             ready=(y_lo_done, ready))
                if k == kt - 1:
                    mm.then_inc(piece_done, 1)

            out_projection(8, PC_OE, USE_OE, 0)

            U_hi, U_lo = ur[:, 0, :, :], ur[:, 1, :, :]
            def odd_group(i, p, first=False):
                piece = PC_C + 2 * C_PCS * i + C_PCS * p
                u = [USE_C[st] + 12 * i + 6 * p for st in range(2)]
                G = 6 * i + 3 * p
                for n in range(3):
                    if first and n < 2:
                        for k in K8:
                            if (n, k) == (1, 4):
                                broadcast(1, 2)
                            mm = project(1 - n, [k], piece + n, H_hi, H_lo, n, first=(k == 0), last=(k == KD - 1),
                                         at0=k, ready=(h_lo_done, KD))
                        mm.then_inc(piece_done, 1)
                        if n == 0:
                            sum_squares(1)
                        continue
                    pe.wait_ge(drained[n % 2], u[n % 2] + n // 2)
                    project((p + n + 1) % 2, K8, piece + n, H_hi, H_lo, n % 2).then_inc(piece_done, 1)
                for m in range(3):
                    kts = ((0, 1), (0, 1, 2), (1, 2))[m]
                    for n in range(2):
                        v = c_use(m, n)
                        pe.wait_ge(drained[v % 2], u[v % 2] + v // 2)
                        if n == 0 and m < 2:
                            pe.wait_ge(u_lo_done, G + 2 + m)
                        project((p + 2 * m) % 2, kts, piece + 3 + 2 * m, U_hi, U_lo, v % 2, at0=4 * n,
                                half_end=None).then_inc(piece_done if n else half_done, 1)
                    v = c_use(m, 2)
                    in_block((p + 1 + 2 * m) % 2, v % 2, piece + 4 + 2 * m, u[v % 2] + v // 2)

            pe.wait_ge(drained[0], USE_C[0])
            pe.wait_ge(drained[1], USE_C[1] - 1)
            odd_group(0, 0, first=True)
            odd_group(0, 1)
            with pe.Fori(1, 2) as i:
                for p in range(2):
                    odd_group(i, p)
            out_projection(6, PC_OO, USE_OO, MIX)
            sum_squares(2)
            broadcast(2, 2)

        @block.scalar
        def _(act):
            act.dma_start(vecs[:, :], vecs_d).then_inc(vecs_in, 16)
            act.dma_start(X[:, 0, :], xT[0]).then_inc(x_in[0], 16)
            act.dma_start(consts[:, :], consts_d).then_inc(consts_in, 16)
            for b in range(1, KD):
                act.dma_start(X[:, b, :], xT[b]).then_inc(x_in[b], 16)

            act.sem_inc(pt_free, 2)

            def split_h(n, b):
                act.activation(H[:, b, :], X[:, b, :], ACT.Copy, scale=vecs[:, VC_N[n] + b:VC_N[n] + b + 1])\
                   .then_inc(h_hi_done, 1)

            def norm_roots(n):
                act.wait_ge(ms_done, n + 1)
                act.activation(rT[:, 0:NT - 1], rT[:, 0:NT - 1], ACT.Sqrt)
                act.activation(rT[0:TOK - SEQ, NT - 1:NT], rT[0:TOK - SEQ, NT - 1:NT], ACT.Sqrt).then_inc(std_done, 1)

            def norm_copy(n, bank):
                act.wait_ge(bc_done, n + 1)
                act.activation(rb[:, 0:SEQ].rearrange("p (a n) -> p a n", a=2), ps[:, 6:8, :], ACT.Copy)
                act.activation(rb[:, SEQ:TOK], ps[:, bank, CW:CW + TOK - SEQ], ACT.Copy).then_inc(rb_done, 1)

            act.wait_ge(vecs_in, 16)
            for b in range(KD):
                act.wait_ge(x_in[b], 16)
                split_h(0, b)
                if b:
                    act.wait_ge(acc_done, b)
                act.activation(sq, X[:, b, :], ACT.Square).then_inc(sq_done, 1)

            act.dma_start(k_all[:, :, SEQ:SEQ + WIN], kc_d).then_inc(k_all_in, 16)
            act.dma_start(V[:, 8, :], vc_d).then_inc(vcache_in, 16)
            act.wait_ge(piece_done, PC_LR + 1)
            act.activation(chunks(blr_raw), setv(0), ACT.Copy).then_inc(drained[0], 1)
            norm_roots(0)
            norm_copy(0, 5)
            for b in range(2):
                act.wait_ge(drained[1 - b], b + 1)
                for dst, c0, c1, d0, done in ((k_all, 0, SEQ, 0, k_all_in), (k_all, SEQ, LIVE, SEQ + WIN, k_all_in),
                                              (k_out, SEQ - WIN, LIVE, 0, k_saved)):
                    act.dma_start(dst[2 * b:2 * b + 2, :, d0:d0 + c1 - c0].rearrange("g d n -> (g d) n"),
                                  kT[:, b, c0:c1]).then_inc(done, 16)

            def load_keys(g):
                for j in range(2):
                    act.dma_start(kz[64 * j:64 * j + 64, j, :], one(k_all, g)).then_inc(kz_in, 16)

            act.wait_ge(k_all_in, 80)
            act.wait_ge(a_zeroed, 3)
            load_keys(0)
            act.wait_ge(rt_done, 1)
            for t in range(NT):
                r = tile_rows(t)
                if t < NT - 1:
                    act.wait_ge(v_done, t + 1)
                else:
                    act.wait_ge(piece_done, PC_V + 2)
                act.activation(V[0:r, t if t < 8 else 9, :], ps[0:r, 6 + t % 2, 0:256], ACT.Copy,
                               scale=rT[0:r, t:t + 1]).then_inc(v_free, 1)
            act.wait_ge(v_free, NT)
            act.dma_start(v_out[0:P, :], V[:, 7, :]).then_inc(v_saved, 16)
            act.dma_start(v_out[P:P + DEC, :], V[0:DEC, 9, :]).then_inc(v_saved, 16)

            def gate_tanh_of(st, use):
                act.wait_ge(drained[st], use)
                act.activation(gt, gz, ACT.Tanh, scale=0.5).then_inc(gate_tanh, 1)

            for n in range(2):
                gate_tanh_of(n, USE_A[n] + 1)

            def low_rank_in(h):
                act.dma_start(wlr_cur[:, :], one(wlr_d, h)).then_inc(wlr_in, 16)
                act.activation(cur_b[:, 0:1], vecs[:, bass.ds(VC_BLR + h, 1)], ACT.Copy).then_inc(bias_ready, 1)

            def log_gate(h, steps=range(3)):
                if 0 in steps:
                    act.wait_ge(lora_done, h + 1)
                    act.activation(chunks(E), setv(0), ACT.Abs, bias=cur_b[:, 0:1]).then_inc(z_act, 1)
                if 1 in steps:
                    act.wait_ge(z_act, 3 * h + 1)
                    act.activation(E, E, ACT.Exp, scale=-1.0).then_inc(z_act, 1)
                if 2 in steps:
                    act.wait_ge(z_act, 3 * h + 2)
                    act.activation(E, E, ACT.Ln, bias=1.0).then_inc(z_act, 1)

            act.dma_start(wlr_cur[:, :], wlr_d[0]).then_inc(wlr_in, 16)
            act.activation(cur_b[:, 0:1], vecs[:, VC_BLR:VC_BLR + 1], ACT.Copy).then_inc(bias_ready, 1)

            def attend(g, more):
                U = ATT_UNITS * g
                for s in range(ATT_UNITS + 3):
                    if s < ATT_UNITS:
                        t, r3 = unit(s)[0], s % 3
                        r = tile_rows(t)
                        c0, c1 = key_cols(t)
                        act.wait_ge(ds_done, U + s + 1)
                        for j in range(2):
                            act.activation(Ssb[0:r, r3, j, c0:c1], Ssb[0:r, r3, j, c0:c1], ACT.Exp,
                                           bias=sm[0:r, r3, 2 + j:3 + j], scale=float(A_DIM) ** -0.5,
                                           accum_out=sm[0:r, r3, 6 + j:7 + j])
                        act.activation(sm[0:r, r3, 8:10], sm[0:r, r3, 4:6], ACT.Exp).then_inc(exp_done, 1)
                    if not more and s > LR_STEP:
                        log_gate(0, [s - LR_STEP - 1])
                    if more and s in (5, 10):
                        gate_tanh_of(0, USE_A1[0] + 4 * g + s // 5)
                    if more and s == ATT_UNITS - 1:
                        load_keys(g + 1)
                    if 2 <= s < ATT_UNITS + 2:
                        u = s - 2
                        t, _ = unit(u)
                        r = tile_rows(t)
                        act.wait_ge(pt_done, U + u + 4)
                        act.wait_ge(o_done, U + u + 1)
                        if t == NT - 1:
                            for kt, rows in ((0, P), (1, DEC)):
                                last = act.activation(
                                    PT[0:rows, u % 2, 2 * kt * P:2 * (kt + 1) * P].rearrange(
                                        "p (j n) -> p j n", j=2)[:, :, 0:r],
                                    ps[0:rows, 5 + u % 2, 2 * kt * P:2 * (kt + 1) * P].rearrange(
                                        "p (j n) -> p j n", j=2)[:, :, 0:r], ACT.Copy)
                        else:
                            c = 2 * P if t == 0 else 0
                            last = act.activation(PT[:, u % 2, c:512], ps[:, 5 + u % 2, c:512], ACT.Copy)
                        last.then_inc(pt_free, 1)

            with act.Fori(0, A_KV - 1) as g:
                attend(g, True)
            attend(A_KV - 1, False)
            act.wait_ge(v_saved, 32)
            act.wait_ge(k_saved, 32)

            def decays(h):
                act.wait_ge(gc_done, h + 1)
                act.activation(Ei, E, ACT.Exp, scale=-1.0 / GATE_NORM).then_inc(e_done, 1)
                act.wait_ge(e_done, 2 * h + 1)
                act.activation(E, E, ACT.Exp, scale=1.0 / GATE_NORM).then_inc(e_done, 1)

            act.wait_ge(vz_ready, A_KV)
            act.wait_ge(o_free, A_KV * ATT_UNITS + 1)
            act.wait_ge(kdz_zeroed, 1)
            decays(0)

            def head(i, last):
                piece = PC_B + B_PCS * i
                act.dma_start(Sst, one(sg_d, i)).then_inc(gstate_in, 16)
                if not last:
                    low_rank_in(i + 1)
                    act.wait_ge(bias_ready, i + 2)
                for t in range(NT):
                    if not last and t == 5:
                        act.wait_ge(q_ready, i + 1)
                        log_gate(i + 1)
                    r = tile_rows(t)
                    if t < NT - 1:
                        act.wait_ge(v_done, (NT - 1) * (i + 1) + t + 1)
                    else:
                        act.wait_ge(piece_done, piece + 2)
                    act.activation(Vb[0:r, t, :], ps[0:r, 6 + t % 2, 0:256], ACT.Copy,
                                   scale=rT[0:r, t:t + 1]).then_inc(v_free, 1)
                    if not last and t == 5 + 2:
                        decays(i + 1)
                T0 = NT * i
                for t in range(NT):
                    act.wait_ge(kdt_done, T0 + t + 1)
                    if t >= 2:
                        act.wait_ge(go_done, T0 + t - 1)
                    for h in range(tile_rows(t) // CHUNK):
                        rows = slice(h * CHUNK, (h + 1) * CHUNK)
                        mm = act.activation(kdz[rows, t % 2, h, :], ps[rows, 2 + 3 * (t % 2), 0:P], ACT.Copy)
                    mm.then_inc(kdz_done, 1)
                act.wait_ge(s_upd, 17 * i + 16)
                act.dma_start(one(gla_p_out, i), St[:, 16 % 3, :]).then_inc(gla_saved, 16)
                act.wait_ge(s_upd, 17 * i + 17)
                act.wait_ge(go_saved, T0 + NT)
                act.dma_start(one(gla_s_out, i), St[:, 17 % 3, :]).then_inc(gla_saved, 16)
                act.activation(sq2, Y[:, bass.ds(2 * i + 8, 2), :], ACT.Square).then_inc(sq2_done, 1)
                def gate_tanh_b(n):
                    use = (USE_B[1] + 3 * i + 1, USE_B[0] + 3 * i + (1 if last else 2))[n]
                    act.wait_ge(drained[1 - n], use)
                    act.activation(tb[:, n, :], gs[:, n, :], ACT.Tanh, scale=0.5).then_inc(b_gate, 1)

                def root():
                    act.wait_ge(drained[1], USE_B[1] + 3 * i + 2)
                    act.activation(kd, kd, ACT.Sqrt).then_inc(gn_std, 1)

                gate_tanh_b(0)
                if not last:
                    gate_tanh_b(1)
                    root()
                    act.wait_ge(b_done, i + 1)
                    return
                act.wait_ge(piece_done, PC_OE)
                for k in range(MIX):
                    if k == 2:
                        gate_tanh_b(1)
                    if k == 4:
                        root()
                    if k == MIX - 2:
                        act.wait_ge(b_done, B_HEADS)
                    act.activation(H[:, k, :], Y[:, k, :], ACT.Copy).then_inc(y_hi_done, 1)

            with act.Fori(0, B_HEADS - 1) as i:
                head(i, False)
            head(B_HEADS - 1, True)

            def lambda_logs():
                act.activation(lamt[:, :], vecs[:, VC_C:VC_ALL].rearrange("p (b n) -> p b n", n=VB)[:, :, 7],
                               ACT.Abs).then_inc(lam_act, 1)
                act.wait_ge(lam_act, 1)
                act.activation(lamt[:, :], lamt[:, :], ACT.Exp, scale=-1.0).then_inc(lam_act, 1)
                act.wait_ge(lam_act, 2)
                act.activation(lamt[:, :], lamt[:, :], ACT.Ln, bias=1.0).then_inc(lam_act, 1)

            def out_residual(src, use, nsq, even):
                for s in range(2):
                    act.dma_start(res[:, s, :], src[s]).then_inc(res_in[s], 16)

                for b in range(KD):
                    i, s = b // 2, b % 2
                    if even and b == KD - 1:
                        act.wait_ge(piece_done, PC_C - 2)
                        for k in range(KD - 1):
                            split_h(1, k)
                    act.wait_ge(drained[s], use[s] + i + 1)
                    if b + 2 < KD:
                        act.dma_start(res[:, s, :], src[b + 2]).then_inc(res_in[s], 16)
                    if even:
                        act.dma_start(x1_d[b], X[:, b, :]).then_inc(x1_saved, 16)
                    if even and b == KD - 1:
                        split_h(1, b)
                    act.wait_ge(acc_done, nsq + b)
                    act.activation(sq, X[:, b, :], ACT.Square).then_inc(sq_done, 1)

            lambda_logs()
            out_residual(xT, USE_OE, KD, True)
            norm_roots(1)
            norm_copy(1, 2)

            act.wait_ge(xc_zeroed, 1)
            with act.Fori(0, 2) as i:
                for p in range(2):
                    piece = PC_C + 2 * C_PCS * i + C_PCS * p
                    u = [USE_C[st] + 12 * i + 6 * p for st in range(2)]
                    G = 6 * i + 3 * p
                    act.wait_ge(cur_ready, 2 * i + p + 1)
                    def u_high(n):
                        act.wait_ge(cv_done, G + n + 1)
                        act.activation(ur[:, 0, n, :], U[:, n, :], ACT.Copy).then_inc(u_hi_done, 1)

                    u_high(0)
                    u_high(1)
                    for m in range(3):
                        vr, vi, vg = (c_use(m, n) for n in range(3))
                        act.wait_ge(half_done, piece + 4 + 2 * m)
                        act.activation(chunks(tr), setv(vr % 2), ACT.Tanh, bias=cur_n[:, m, 2:3], scale=0.5)\
                           .then_inc(drained[vr % 2], 1)
                        act.wait_ge(piece_done, piece + 4 + 2 * m)
                        if m:
                            act.wait_ge(c_scan, 2 * G + 2 * m)
                        act.activation(chunks(ti), setv(vi % 2), ACT.Tanh, bias=cur_n[:, m, 3:4], scale=0.5)\
                           .then_inc(drained[vi % 2], 1)
                        if m == 0:
                            u_high(2)
                        act.wait_ge(drained[vr % 2], u[vr % 2] + vr // 2 + 1)
                        act.activation(aa, tr, ACT.Exp, bias=cur_n[:, m, 0:1], scale=cur_n[:, m, 0:1]).then_inc(c_a, 1)
                        if m:
                            act.wait_ge(c_y, G + m)
                        act.activation(th, tr, ACT.Tanh, bias=cur_n[:, m, 1:2], scale=cur_n[:, m, 1:2])
                        act.wait_ge(c_a, 2 * G + 2 * m + 1)
                        act.activation(sa, aa, ACT.Square).then_inc(c_a, 1)
                        act.wait_ge(c_w, G + m + 1)
                        act.activation(th, th, ACT.Sqrt).then_inc(c_sqrt, 1)
                        act.wait_ge(c_b, G + m + 1)
                        act.wait_ge(drained[vg % 2], u[vg % 2] + vg // 2 + 1)
                        act.activation(gc, cgz, ACT.Tanh, scale=0.5).then_inc(c_tanh, 1)
            act.wait_ge(piece_done, PC_OO)
            with act.Fori(0, KC - 1) as k:
                act.activation(slot(H, k), slot(Y, k), ACT.Copy).then_inc(y_hi_done, 1)
            act.wait_ge(c_y, KC)
            act.activation(H[:, KC - 1, :], Y[:, KC - 1, :], ACT.Copy).then_inc(y_hi_done, 1)
            act.dma_start(conv_out, cvo[:, :, :]).then_inc(small_saved, 16)
            act.dma_start(lru_out, lro[:, :, :]).then_inc(small_saved, 16)
            out_residual(x1_d, USE_OO, 2 * KD, False)
            norm_roots(2)
            norm_copy(2, 2)
            for b in range(KD):
                act.wait_ge(xn_done, b + 1)
                act.dma_start(yT[b], X[:, b, :]).then_inc(y_saved, 16)
            act.wait_ge(y_saved, 16 * KD)
            act.wait_ge(small_saved, 32)
            act.wait_ge(gla_saved, 32 * B_HEADS)
            act.wait_ge(k_saved, 32)
            act.wait_ge(v_saved, 32)

        @block.vector
        def _(dve):
            dve.sem_inc(s_free, 2)
            dve.sem_inc(o_free, 1)
            dve.memset(acc, 0.0).then_inc(acc_zero, 1)

            dve.memset(rT[:, :], 1.0).then_inc(rt_init, 1)

            def split_h(n, b):
                dve.wait_ge(h_hi_done, KD * n + b + 1)
                dve.scalar_tensor_tensor(H[:, KD + b, :], X[:, b, :], vecs[:, VC_N[n] + b:VC_N[n] + b + 1],
                                         H[:, b, :].bitcast(F32), ALU.mult, ALU.subtract).then_inc(h_lo_done, 1)

            def norm_factors(n):
                dve.wait_ge(ssq_done, n + 1)
                parts = [(slice(0, P), slice(0, NT - 1)), (slice(0, TOK - SEQ), slice(NT - 1, NT))]
                for r, c in parts:
                    mm = dve.tensor_scalar(rT[r, c], ps[r, 7, c], 1.0 / DM, EPS, ALU.mult, ALU.add)
                mm.then_inc(ms_done, 1)
                dve.wait_ge(std_done, n + 1)
                for r, c in parts:
                    mm = dve.reciprocal(rT[r, c], rT[r, c])
                mm.then_inc(rt_done, 1)
                dve.wait_ge(rt_done, n + 1)
                dve.tensor_tensor(diag, ident.rearrange("p (a n) -> p a n", a=1).to_broadcast([P, NT, P]),
                                  rT[:, :].rearrange("p (a n) -> p a n", n=1).to_broadcast([P, NT, P]),
                                  ALU.mult).then_inc(diag_done, 1)

            dve.wait_ge(acc_zero, 1)
            dve.wait_ge(rt_init, 1)
            dve.wait_ge(vecs_in, 16)
            for b in range(KD):
                split_h(0, b)
                if b:
                    dve.wait_ge(acc_done, b)
                dve.wait_ge(sq_done, b + 1)
                dve.tensor_tensor(acc, acc, sq, ALU.add).then_inc(acc_done, 1)
            dve.wait_ge(consts_in, 16)
            norm_factors(0)

            dve.wait_ge(h_lo_done, KD)
            dve.memset(kz[64:P, 0, :], 0.0).then_inc(a_zeroed, 1)
            dve.memset(kz[0:64, 1, :], 0.0).then_inc(a_zeroed, 1)
            dve.memset(Vz[:, :, :], 0.0).then_inc(a_zeroed, 1)
            dve.tensor_scalar(nsink[:, :], vecs[:, VC_SINK:VC_SINK + A_HEADS], -1.0, None, ALU.mult)\
               .then_inc(sink_neg, 1)
            dve.wait_ge(a_zeroed, 3)
            dve.wait_ge(sink_neg, 1)
            dve.wait_ge(rb_done, 1)
            dve.wait_ge(piece_done, PC_K + 1)
            dve.tensor_tensor(chunks(kT[:, 0, :]), setv(1), chunks(rb), ALU.mult).then_inc(drained[1], 1)
            dve.wait_ge(piece_done, PC_K + 2)
            dve.tensor_tensor(chunks(kT[:, 1, :]), setv(0), chunks(rb), ALU.mult).then_inc(drained[0], 1)
            dve.tensor_tensor(blrT, blr_raw, rb, ALU.mult).then_inc(blr_ready, 1)

            def gate_in(st, piece, before):
                dve.wait_ge(piece_done, piece + 1)
                if before is not None:
                    dve.wait_ge(gated, before)
                dve.tensor_tensor(chunks(gz), setv(st), chunks(rb), ALU.mult).then_inc(drained[st], 1)

            def gate(k):
                dve.wait_ge(gate_tanh, k + 1)
                dve.scalar_tensor_tensor(slot(Y, k), gt, 1.0, gz, ALU.add, ALU.mult).then_inc(gated, 1)

            def q_in(b, st, piece):
                dve.wait_ge(piece_done, piece + 1)
                dve.tensor_tensor(chunks(q[:, b, :]), setv(st), chunks(rb), ALU.mult).then_inc(drained[st], 1)

            def attend(g, more):
                U = ATT_UNITS * g
                dve.wait_ge(gated, 2 * g + 2)
                dve.tensor_copy(Vz[:, 0:9, 64:128], V[:, 0:9, bass.ds(A_DIM * g, A_DIM)])
                dve.tensor_copy(Vz[0:64, 9, 64:128], V[0:64, 9, bass.ds(A_DIM * g, A_DIM)]).then_inc(vz_ready, 1)
                dve.tensor_copy(cur_sink[:, 0, :], vecs[:, bass.ds(VC_SINK + 4 * g, 4)])
                dve.tensor_copy(cur_sink[:, 2, :], consts[:, bass.ds(CC_SLOPE + 4 * g, 4)])
                dve.tensor_copy(cur_sink[:, 1, :], nsink[:, bass.ds(4 * g, 4)]).then_inc(sink_cur, 1)
                dve.wait_ge(sink_cur, g + 1)
                for s in range(ATT_UNITS + 4):
                    if s >= 4:
                        u = s - 4
                        t, b = unit(u)
                        r = tile_rows(t)
                        dve.wait_ge(o_done, U + u + 3)
                        y = slot(Y, 2 * g + b, t * P, t * P + r)
                        dve.tensor_tensor(y, ps[:, 7, 0:r], y, ALU.mult).then_inc(o_free, 1)
                    if not more and s in (K0_STEPS, 2 * K0_STEPS):
                        n = s // K0_STEPS - 1
                        if n == 0:
                            dve.wait_ge(k_saved, 32)
                        dve.wait_ge(piece_done, PC_B0 + n + 1)
                        dve.tensor_tensor(chunks(kT[:, n, :]), setv(0), chunks(rb), ALU.mult)\
                           .then_inc(drained[0], 1)
                    if more and s and s % 5 == 0:
                        piece = PC_A + A_PCS * (g + 1) + (s // 5 - 1)
                        if s < 15:
                            gate_in(0, piece, 2 * g + (s // 5 + 1))
                        else:
                            q_in(s // 5 - 3, 0, piece)
                    if s < ATT_UNITS:
                        (t, b), r3 = unit(s), s % 3
                        r = tile_rows(t)
                        c0, c1 = key_cols(t)
                        dve.wait_ge(s_done, U + s + 1)
                        dve.wait_ge(pt_done, U + s + 1)
                        for j in range(2):
                            last = dve.scalar_tensor_tensor(
                                Ssb[0:r, r3, j, c0:c1], dist[0:r, c0:c1], cur_sink[0:r, 2, 2 * b + j:2 * b + j + 1],
                                ps[0:r, 3 + s % 2, j * 256 + c0:j * 256 + c1], ALU.mult, ALU.add)
                        last.then_inc(s_free, 1)
                        dve.wait_ge(s_free, U + s + 3)
                        dve.tensor_reduce(sm[0:r, r3, 0:2], Ssb[0:r, r3, :, c0:c1], AX.X, ALU.max).then_inc(mx_done, 1)
                        dve.wait_ge(mx_done, U + s + 1)
                        dve.scalar_tensor_tensor(sm[0:r, r3, 2:4], sm[0:r, r3, 0:2], -float(A_DIM) ** -0.5,
                                                 cur_sink[0:r, 1, 2 * b:2 * b + 2], ALU.mult, ALU.min)\
                           .then_inc(nm_done, 1)
                        dve.wait_ge(nm_done, U + s + 1)
                        dve.tensor_tensor(sm[0:r, r3, 4:6], sm[0:r, r3, 2:4], cur_sink[0:r, 0, 2 * b:2 * b + 2],
                                          ALU.add).then_inc(ds_done, 1)
                    if 0 <= s - 1 < ATT_UNITS:
                        u = s - 1
                        t, r3 = unit(u)[0], u % 3
                        r = tile_rows(t)
                        c0, c1 = key_cols(t)
                        dve.wait_ge(exp_done, U + u + 1)
                        dve.tensor_tensor(sm[0:r, r3, 8:10], sm[0:r, r3, 8:10], sm[0:r, r3, 6:8], ALU.add)\
                           .then_inc(den_done, 1)
                        dve.wait_ge(den_done, U + u + 1)
                        dve.reciprocal(sm[0:r, r3, 10:12], sm[0:r, r3, 8:10]).then_inc(rcp_done, 1)
                        dve.wait_ge(rcp_done, U + u + 1)
                        for j in range(2):
                            last = dve.tensor_scalar(Ssb[0:r, r3, j, c0:c1], Ssb[0:r, r3, j, c0:c1],
                                                     sm[0:r, r3, 10 + j:11 + j], 0.5, ALU.mult, ALU.mult)
                        last.then_inc(p_done, 1)
                    if more and s in (6, 11):
                        gate(2 * g + (s // 5 + 1))

            for n in range(2):
                gate_in(n, PC_A + n, n or None)
                gate(n)
            for n in range(2):
                q_in(n, n, PC_A + 2 + n)
            dve.wait_ge(v_free, NT)
            dve.wait_ge(vcache_in, 16)
            for st in range(2):
                dve.wait_ge(drained[st], USE_A1[st])
            with dve.Fori(0, A_KV - 1) as g:
                attend(g, True)
            attend(A_KV - 1, False)

            dve.wait_ge(v_saved, 32)
            dve.wait_ge(k_saved, 32)
            dve.wait_ge(vz_ready, A_KV)
            dve.memset(Y[:, KD:MIX, LIVE:TOK], 0.0).then_inc(y_zeroed, 1)
            dve.wait_ge(y_zeroed, 1)
            dve.memset(kdz, 0.0).then_inc(kdz_zeroed, 1)

            def log_gate(h, use):
                dve.wait_ge(z_act, 3 * h + 1)
                dve.tensor_scalar(chunks(Ei), setv(0), cur_b[:, 0:1], 0.0, ALU.add, ALU.min).then_inc(drained[0], 1)
                dve.wait_ge(z_act, 3 * h + 3)
                dve.wait_ge(drained[0], use)
                dve.tensor_tensor(Ei, Ei, E, ALU.subtract).then_inc(z_sub, 1)
                dve.wait_ge(z_sub, h + 1)
                for c in range(0, TOK, CHUNK):
                    e = min(c + CHUNK, TOK)
                    last = dve.tensor_tensor_scan(E[:, c:e], ones[:, 0:e - c], Ei[:, c:e], 0.0, ALU.mult, ALU.add)
                last.then_inc(gc_done, 1)

            def decays(h):
                dve.wait_ge(e_done, 2 * h + 2)
                dve.tensor_copy(elast, E[:, 0:LIVE].rearrange("p (c n) -> p c n", n=CHUNK)[:, :, CHUNK - 1])\
                   .then_inc(el_done, 1)

            def k_to_ends(h):
                dve.tensor_tensor(kd[:, 0:LIVE].rearrange("p (c n) -> p c n", n=CHUNK),
                                  kg[:, 0:LIVE].rearrange("p (c n) -> p c n", n=CHUNK),
                                  elast.rearrange("p (c n) -> p c n", n=1).to_broadcast([P, LIVE // CHUNK, CHUNK]),
                                  ALU.mult).then_inc(kd_done, 1)

            log_gate(0, USE_B0 + 3)
            decays(0)
            dve.tensor_tensor(kg, kT[:, 0, :], Ei, ALU.mult).then_inc(k0_ready, 1)
            dve.wait_ge(k0_ready, 1)
            dve.wait_ge(el_done, 1)
            k_to_ends(0)
            dve.wait_ge(kd_done, 1)
            dve.scalar_tensor_tensor(qg, kT[:, 1, :], float(B_DK) ** -0.5, E, ALU.mult, ALU.mult).then_inc(q_ready, 1)
            def split_mix(k):
                dve.wait_ge(y_hi_done, k + 1)
                dve.tensor_tensor(Yr[:, k, :], Y[:, k, :], H[:, k, :].bitcast(F32), ALU.subtract)\
                   .then_inc(y_lo_done, 1)

            def head(i, last):
                u0, u1 = USE_B[0] + 3 * i, USE_B[1] + 3 * i
                piece = PC_B + B_PCS * i
                dve.memset(St[:, 0, :], 0.0).then_inc(s0_ready, 1)
                if not last:
                    dve.wait_ge(q_ready, i + 1)
                    log_gate(i + 1, u0 + 1)
                T0 = NT * i
                dve.wait_ge(s0_ready, i + 1)

                def mask(t):
                    r = tile_rows(t)
                    dve.wait_ge(at_done, T0 + t + 1)
                    if t >= 2:
                        dve.wait_ge(go_done, T0 + t - 1)
                    dve.tensor_tensor(aT[0:r, t % 2, 0:r], ps[0:r, t % 2, 0:r], causal[0:r, 0:r], ALU.mult)\
                       .then_inc(at_masked, 1)

                def save(t):
                    r = tile_rows(t)
                    dve.wait_ge(go_done, T0 + t + 1)
                    dve.tensor_scalar(Y[:, bass.ds(2 * i + 8, 2), t * P:t * P + r],
                                      ps[:, 3 + t % 2, 0:256].rearrange("p (e n) -> p e n", e=2)[:, :, 0:r],
                                      1.0, None, ALU.mult).then_inc(go_saved, 1)

                mask(0)
                for t in range(NT):
                    if t + 1 < NT:
                        mask(t + 1)
                    if t:
                        save(t - 1)
                    for h in range(tile_rows(t) // CHUNK):
                        n = 2 * t + h
                        dve.wait_ge(gds_done, 17 * i + n + 1)
                        if n:
                            dve.wait_ge(s_upd, 17 * i + n)
                        if n >= 2:
                            dve.wait_ge(go_done, T0 + (n - 2) // 2 + 1)
                        if t == NT - 1:
                            dve.wait_ge(gstate_in, 16 * i + 16)
                        state = Sst if t == NT - 1 else St[:, n % 3, :]
                        dve.scalar_tensor_tensor(St[:, (n + 1) % 3, :], state, elast[:, n:n + 1],
                                                 ps[:, 6 + h, 0:256], ALU.mult, ALU.add).then_inc(s_upd, 1)
                save(NT - 1)
                def gate_in(n):
                    dve.wait_ge(piece_done, piece + 3 + n)
                    dve.tensor_tensor(chunks(gs[:, n, :]), setv(1 - n), chunks(rb), ALU.mult)\
                       .then_inc(drained[1 - n], 1)

                def gate(n):
                    dve.wait_ge(b_gate, 2 * i + n + 1)
                    dve.scalar_tensor_tensor(gs[:, n, :], tb[:, n, :], 1.0, gs[:, n, :], ALU.add, ALU.mult)\
                       .then_inc(gs_done, 1)

                def mean_square():
                    dve.wait_ge(gn_done, i + 1)
                    dve.tensor_scalar(chunks(kd), setv(1), 1.0 / B_DV, EPS, ALU.mult, ALU.add)\
                       .then_inc(drained[1], 1)

                def root_inverse():
                    dve.wait_ge(gn_std, i + 1)
                    dve.reciprocal(kd, kd).then_inc(gn_rstd, 1)

                def scale():
                    dve.wait_ge(gn_rstd, i + 1)
                    dve.wait_ge(gs_done, 2 * i + 2)
                    for e in range(2):
                        y = slot(Y, 2 * i + 8 + e)
                        dve.scalar_tensor_tensor(y, y, vecs[:, VC_GN + e:VC_GN + e + 1], kd, ALU.mult, ALU.mult)\
                           .then_inc(bn_done, 1)
                    for e in range(2):
                        y = slot(Y, 2 * i + 8 + e)
                        dve.wait_ge(bn_done, 2 * i + e + 1)
                        done = dve.scalar_tensor_tensor(y, y, 0.5, gs[:, e, :], ALU.mult, ALU.mult)
                    done.then_inc(b_done, 1)

                gate_in(0)
                gate(0)
                gate_in(1)
                if not last:
                    mean_square()
                    gate(1)
                    root_inverse()
                    scale()
                    decays(i + 1)
                    dve.wait_ge(el_done, i + 2)
                    dve.tensor_tensor(Ei, Ei, rb, ALU.mult).then_inc(es_done, 1)
                    dve.tensor_tensor(E, E, rb, ALU.mult).then_inc(es_done, 1)
                    dve.wait_ge(es_done, 2 * i + 2)
                    dve.wait_ge(piece_done, piece + 5)
                    dve.tensor_tensor(chunks(kg), setv(0), chunks(Ei), ALU.mult).then_inc(drained[0], 1)
                    dve.wait_ge(drained[0], u0 + 3)
                    k_to_ends(i + 1)
                    dve.wait_ge(kd_done, i + 2)
                    dve.wait_ge(piece_done, piece + 6)
                    dve.scalar_tensor_tensor(chunks(qg), setv(1), float(B_DK) ** -0.5, chunks(E), ALU.mult, ALU.mult)\
                       .then_inc(drained[1], 1)
                    dve.wait_ge(drained[1], u1 + 3)
                    dve.sem_inc(q_ready, 1)
                    dve.wait_ge(gla_saved, 32 * i + 32)
                    return
                for k in range(MIX):
                    if k == 2:
                        mean_square()
                        gate(1)
                    if k == 7:
                        root_inverse()
                    if k == 10:
                        scale()
                    split_mix(k)

            with dve.Fori(0, B_HEADS - 1) as i:
                head(i, False)
            head(B_HEADS - 1, True)

            def out_residual(n, base, res_base, last_pair):
                dve.memset(acc, 0.0).then_inc(acc_zero, 1)
                dve.wait_ge(acc_zero, n + 1)

                def residual(i, s):
                    dve.wait_ge(piece_done, base + 4 * i + s + 3)
                    dve.wait_ge(res_in[s], 16 * (i + res_base + 1))
                    dve.tensor_tensor(chunks(slot(X, 2 * i + s)), setv(s), chunks(res[:, s, :]), ALU.add)\
                       .then_inc(drained[s], 1)

                def square(i, s):
                    dve.wait_ge(sq_done, KD * n + 2 * i + s + 1)
                    dve.wait_ge(acc_done, KD * n + 2 * i + s)
                    dve.tensor_tensor(acc, acc, sq, ALU.add).then_inc(acc_done, 1)

                with dve.Fori(0, KD // 2 - 1) as i:
                    for s in range(2):
                        residual(i, s)
                        square(i, s)
                last_pair(KD // 2 - 1, residual, square)

            lv = vecs[:, VC_C:VC_ALL].rearrange("p (b n) -> p b n", n=VB)
            dve.tensor_scalar(nsp[:, :, 1], lv[:, :, 7], -1.0, 0.0, ALU.mult, ALU.max).then_inc(nsp_ready, 1)
            dve.tensor_scalar(nsp[:, :, 2:4], lv[:, :, 5:7], 0.5, None, ALU.mult)
            dve.wait_ge(nsp_ready, 1)
            dve.wait_ge(lam_act, 3)
            dve.tensor_tensor(nsp[:, :, 0], nsp[:, :, 1], lamt[:, :], ALU.add).then_inc(nsp_ready, 1)
            dve.wait_ge(nsp_ready, 2)
            dve.tensor_scalar(nsp[:, :, 1], nsp[:, :, 0], 4.0, None, ALU.mult).then_inc(nsp_ready, 1)
            dve.wait_ge(nsp_ready, 3)
            dve.tensor_scalar(nsp[:, :, 0], nsp[:, :, 1], -1.0, None, ALU.mult).then_inc(nsp_ready, 1)
            dve.wait_ge(nsp_ready, 4)

            def last_pair_even(i, residual, square):
                residual(i, 0)
                square(i, 0)
                dve.wait_ge(piece_done, PC_C)
                for k in range(KD):
                    if k == 2:
                        residual(i, 1)
                    if k == KD - 1:
                        square(i, 1)
                    split_h(1, k)

            out_residual(1, PC_OE, 0, last_pair_even)
            norm_factors(1)

            dve.wait_ge(x1_saved, 16 * KD)
            dve.wait_ge(h_lo_done, 2 * KD)
            dve.memset(xc, 0.0).then_inc(xc_zeroed, 1)
            dve.wait_ge(xc_zeroed, 1)
            dve.wait_ge(rb_done, 2)
            with dve.Fori(0, 2) as i:
                for p in range(2):
                    u = [USE_C[st] + 12 * i + 6 * p for st in range(2)]
                    piece = PC_C + 2 * C_PCS * i + C_PCS * p
                    G = 6 * i + 3 * p
                    dve.tensor_copy(cur_n[:, :, :], nsp[:, bass.ds(G, 3), :])
                    dve.tensor_copy(cur[:, :, :].rearrange("p a b -> p (a b)"),
                                    vecs[:, bass.ds(VC_C + VB * G, 3 * VB)]).then_inc(cur_ready, 1)
                    dve.wait_ge(cur_ready, 2 * i + p + 1)
                    for n in range(3):
                        st = n % 2
                        dve.wait_ge(piece_done, piece + n + 1)
                        if n:
                            dve.wait_ge(cvo_done, G + n)
                        dve.tensor_tensor(xc[:, EXT:EXT + 2 * CW].rearrange("p (c n) -> p c n", c=2),
                                          sets[st][:, 0:2, 0:CW], chunks(rb)[:, 0:2, :], ALU.mult)
                        dve.tensor_tensor(xc[:, EXT + 2 * CW:EXT + SEQ], sets[st][:, 2, 0:SEQ - 2 * CW],
                                          rb[:, 2 * CW:SEQ], ALU.mult)
                        dve.tensor_copy(xc[:, EXT + SEQ:2 * EXT + SEQ], cur[:, n, 9:12])
                        dve.tensor_tensor(xc[:, 2 * EXT + SEQ:2 * EXT + LIVE], sets[st][:, 2, SEQ - 2 * CW:LIVE - 2 * CW],
                                          rb[:, SEQ:LIVE], ALU.mult).then_inc(drained[st], 1)
                        dve.wait_ge(drained[st], u[st] + n // 2 + 1)
                        dve.tensor_scalar(U[:, n, :], xc[:, 0:TOK], cur[:, n, 0:1], cur[:, n, 4:5], ALU.mult, ALU.add)\
                           .then_inc(cv_step, 1)
                        for j in range(1, CONV_W):
                            dve.wait_ge(cv_step, 3 * G + 3 * n + j)
                            dve.scalar_tensor_tensor(U[:, n, :], xc[:, j:j + TOK], cur[:, n, j:j + 1], U[:, n, :],
                                                     ALU.mult, ALU.add).then_inc(cv_step if j < 3 else cv_done, 1)
                        dve.tensor_scalar(slot(cvo, G + n, 0, EXT), xc[:, SEQ:SEQ + EXT], 1.0, None, ALU.mult)
                        dve.tensor_scalar(slot(cvo, G + n, EXT, 2 * EXT), xc[:, LIVE + EXT:LIVE + 2 * EXT], 1.0, None,
                                          ALU.mult).then_inc(cvo_done, 1)
                        dve.wait_ge(cv_done, G + n + 1)
                        dve.wait_ge(u_hi_done, G + n + 1)
                        dve.tensor_tensor(ur[:, 1, n, :], U[:, n, :], ur[:, 0, n, :].bitcast(F32), ALU.subtract)\
                           .then_inc(u_lo_done, 1)
                    for m in range(3):
                        vr, vi, vg = (c_use(m, n) for n in range(3))
                        dve.wait_ge(c_a, 2 * G + 2 * m + 2)
                        dve.scalar_tensor_tensor(th, sa, 1.0, th, ALU.add, ALU.mult).then_inc(c_w, 1)
                        dve.wait_ge(drained[vi % 2], u[vi % 2] + vi // 2 + 1)
                        dve.scalar_tensor_tensor(ti, ti, 1.0, U[:, m, :], ALU.add, ALU.mult).then_inc(c_iu, 1)
                        dve.wait_ge(c_iu, G + m + 1)
                        dve.wait_ge(c_sqrt, G + m + 1)
                        dve.scalar_tensor_tensor(ti, ti, 0.5, th, ALU.mult, ALU.mult).then_inc(c_b, 1)
                        dve.wait_ge(c_b, G + m + 1)
                        s0 = SEQ + EXT
                        dve.tensor_tensor_scan(sa[:, 0:SEQ], aa[:, 0:SEQ], ti[:, 0:SEQ], 0.0, ALU.mult, ALU.add)\
                           .then_inc(c_scan, 1)
                        dve.tensor_tensor_scan(sa[:, s0:s0 + DEC], aa[:, s0:s0 + DEC], ti[:, s0:s0 + DEC],
                                               cur[:, m, 8:9], ALU.mult, ALU.add).then_inc(c_scan, 1)
                        dve.wait_ge(piece_done, piece + 5 + 2 * m)
                        dve.tensor_tensor(chunks(cgz), setv(vg % 2), chunks(rb), ALU.mult).then_inc(drained[vg % 2], 1)
                        dve.wait_ge(c_tanh, G + m + 1)
                        dve.scalar_tensor_tensor(slot(Y, G + m), gc, 1.0, cgz, ALU.add, ALU.mult).then_inc(c_gy, 1)
                        dve.wait_ge(c_scan, 2 * G + 2 * m + 2)
                        dve.wait_ge(c_gy, G + m + 1)
                        dve.tensor_copy(slot(lro, G + m, 0, 1), sa[:, SEQ - 1:SEQ])
                        dve.tensor_copy(slot(lro, G + m, 1, 2), sa[:, s0 + DEC - 1:s0 + DEC]).then_inc(lro_done, 1)
                        y = slot(Y, G + m, 0, SEQ)
                        dve.scalar_tensor_tensor(y, sa[:, 0:SEQ], 0.5, y, ALU.mult, ALU.mult)
                        y = slot(Y, G + m, SEQ, LIVE)
                        dve.scalar_tensor_tensor(y, sa[:, s0:s0 + DEC], 0.5, y, ALU.mult, ALU.mult).then_inc(c_y, 1)

            with dve.Fori(0, KC) as k:
                dve.wait_ge(y_hi_done, MIX + k + 1)
                dve.tensor_tensor(slot(Yr, k), slot(Y, k), slot(H, k).bitcast(F32), ALU.subtract)\
                   .then_inc(y_lo_done, 1)

            def last_pair_odd(i, residual, square):
                for s in range(2):
                    residual(i, s)
                    square(i, s)

            out_residual(2, PC_OO, 4, last_pair_odd)
            norm_factors(2)
            dve.wait_ge(rb_done, 3)
            for b in range(KD):
                g = vecs[:, VC_N[2] + b:VC_N[2] + b + 1]
                dve.scalar_tensor_tensor(X[:, b, :], X[:, b, :], g, rb, ALU.mult, ALU.mult).then_inc(xn_done, 1)


def kernel(**inputs):
    import concourse.bacc as bacc
    from concourse.bass_utils import run_bass_kernel_spmd

    f = {k: np.asarray(v) for k, v in inputs.items()}
    w_in, w_oe = f["w_in_even"][0], f["w_out_even"][0]
    w_ino, w_oo = f["w_in_odd"][0], f["w_out_odd"][0]
    dt = w_in.dtype

    W = np.zeros((PIECES, P, PIECE), dt)

    def columns(piece, w, cols):
        kt = w.shape[0] // P
        W[piece, :, :kt * P] = w[:, cols].reshape(kt, P, P).transpose(1, 0, 2).reshape(P, kt * P)

    def values(piece, w, c):
        v = w[:, c:c + 256].reshape(2, 4, P, 256).transpose(0, 2, 1, 3).reshape(2, P, PIECE)
        W[piece:piece + 2] = v

    def block_of(c):
        return np.arange(c, c + P)

    values(PC_V, w_in, OFF_V)
    columns(PC_LR, w_in, block_of(OFF_LR))
    for b in range(2):
        columns(PC_K + b, w_in, block_of(OFF_K + b * P))
    for g in range(A_KV):
        for b in range(2):
            columns(PC_A + A_PCS * g + b, w_in, block_of(OFF_G + (2 * g + b) * P))
            columns(PC_A + A_PCS * g + 2 + b, w_in, block_of(OFF_Q + (2 * g + b) * P))
    for h in range(B_HEADS):
        a = PC_B + B_PCS * h
        kq = a - 2 if h else PC_B0
        columns(kq, w_in, block_of(OFF_BK + h * P))
        columns(kq + 1, w_in, block_of(OFF_BQ + h * P))
        values(a, w_in, OFF_BV + h * B_DV)
        for b in range(2):
            columns(a + 2 + b, w_in, block_of(OFF_G + (8 + 2 * h + b) * P))
    for m in range(KD):
        for half in range(2):
            at = 4 * (m // 2) + 2 * half + m % 2
            columns(PC_OE + at, w_oe[half * 8 * P:(half + 1) * 8 * P], block_of(m * P))
            columns(PC_OO + at, w_oo[half * 6 * P:(half + 1) * 6 * P], block_of(m * P))
    for g in range(4):
        a = PC_C + C_PCS * g
        for n in range(3):
            columns(a + n, w_ino, block_of((3 * g + n) * P))
            columns(a + 4 + 2 * n, w_ino, block_of(CWID + (3 * g + n) * P))
        for n, name in enumerate(("w_rg_a", "w_rg_i")):
            both = np.zeros((3 * P, 3 * P), dt)
            for b in range(2):
                sl = slice(b * CBLK, (b + 1) * CBLK)
                both[sl, sl] = f[name][0, 2 * g + b]
            for m, kts in enumerate(((0, 1), (0, 1, 2), (1, 2))):
                for x, kt in enumerate(kts):
                    at = 4 * n + x
                    W[a + 3 + 2 * m, :, at * P:(at + 1) * P] = both[kt * P:(kt + 1) * P, m * P:(m + 1) * P]

    xT = np.zeros((KD, P, TOK), dt)
    xT[:, :, :SEQ] = f["x_prompt"][0].T.reshape(KD, P, SEQ)
    xT[:, :, SEQ:LIVE] = f["x_sample"][0].T.reshape(KD, P, DEC)

    vecs = np.zeros((P, VC_ALL), dt)
    for n, name in enumerate(("norm_even", "norm_odd", "norm_final")):
        vecs[:, VC_N[n]:VC_N[n] + KD] = f[name].reshape(KD, P).T
    vecs[:, VC_BLR:VC_BLR + 4] = f["b_gate_lr"][0].reshape(4, P).T
    vecs[:, VC_GN:VC_GN + 2] = f["gla_norm"][0].reshape(2, P).T
    vecs[:, VC_SINK:VC_SINK + A_HEADS] = f["sinks"][0][None, :]
    lv = vecs[:, VC_C:].reshape(P, KC, VB)
    for j in range(CONV_W):
        lv[:, :, j] = f["conv_w"][0, j].reshape(KC, P).T
    for n, name in enumerate(("conv_b", "b_rg_a", "b_rg_i", "lru_lambda", "state_lru")):
        lv[:, :, CONV_W + n] = f[name][0].reshape(KC, P).T
    for j in range(EXT):
        lv[:, :, 9 + j] = f["cache_conv"][0, 0, j].reshape(KC, P).T

    consts = np.zeros((P, CC_ALL), np.float32)
    r = np.arange(P)
    consts[:, CC_ID:CC_ID + P] = np.eye(P)
    consts[:, CC_ONE:CC_ONE + P] = 1.0
    consts[:, CC_CAUSAL:CC_CAUSAL + P] = (r[:, None] // CHUNK == r[None, :] // CHUNK) & (r[:, None] <= r[None, :])
    j = np.arange(2 * P)
    far = (j[None, :] // CHUNK < r[:, None] // CHUNK) | (j[None, :] // CHUNK > r[:, None] // CHUNK + 2)
    consts[:, CC_DIST:CC_DIST + 2 * P] = np.where(far, 1e34, np.abs(WIN + r[:, None] - j[None, :]))
    consts[:, CC_SLOPE:] = -(2.0 ** (-8.0 * np.arange(1, A_HEADS + 1) / A_HEADS)).astype(np.float32) * A_DIM ** 0.5

    wlr = np.zeros((B_HEADS + 1, P, P), dt)
    wlr[:B_HEADS, :B_LOW] = f["w_gate_lr"][0].reshape(B_LOW, B_HEADS, P).transpose(1, 0, 2)
    arrays = {
        "xT": xT, "weights": W, "vecs_in": vecs, "consts_in": consts, "wlr_in": wlr,
        "k_cache": np.ascontiguousarray(f["cache_swa_k"][0, 0].transpose(1, 2, 0)),
        "v_cache": np.ascontiguousarray(f["cache_swa_v"][0, 0].reshape(WIN, A_KV * A_DIM)),
        "gla_state": np.ascontiguousarray(f["state_gla"][0, 0]),
    }
    outs = {
        "yT": (KD, P, TOK), "k_new": (A_KV, A_DIM, WIN + DEC), "v_new": (WIN + DEC, A_KV * A_DIM),
        "gla_p": (B_HEADS, B_DK, B_DV), "gla_s": (B_HEADS, B_DK, B_DV),
        "conv_new": (P, KC, 2 * EXT), "lru_new": (P, KC, 2),
    }
    nc = bacc.Bacc("TRN2", target_bir_lowering=False, num_devices=1, dynamic_dma_scratch_size=1024)
    args = [nc.dram_tensor(k, a.shape, mybir.dt.from_np(a.dtype), kind="ExternalInput").ap()
            for k, a in arrays.items()]
    args += [nc.dram_tensor(k, s, F32, kind="ExternalOutput").ap() for k, s in outs.items()]
    build_program(nc, *args)
    got = run_bass_kernel_spmd(nc, [arrays], core_ids=[0]).results[0]

    y = got["yT"].reshape(DM, TOK).T
    kn = got["k_new"].transpose(2, 0, 1)
    vn = got["v_new"].reshape(WIN + DEC, A_KV, A_DIM)
    cn = got["conv_new"].transpose(2, 1, 0).reshape(2, EXT, CWID)
    ln = got["lru_new"].transpose(2, 1, 0).reshape(2, CWID)
    return (y[None, :SEQ], y[None, SEQ:LIVE],
            kn[None, None, :WIN], vn[None, None, :WIN], got["gla_p"][None, None],
            cn[None, None, 0], ln[None, None, 0],
            kn[None, None, WIN:], vn[None, None, WIN:], got["gla_s"][None, None],
            cn[None, None, 1], ln[None, None, 1])
```

```python
from contextlib import ExitStack

import numpy as np

import concourse.bass as bass
from concourse import mybir

F32 = mybir.dt.float32
F32R = mybir.dt.float32r
ALU = mybir.AluOpType
ACT = mybir.ActivationFunctionType
AX = mybir.AxisListType

P = 128
DM = 1024
SEQ, DEC = 1024, 64
LIVE = SEQ + DEC
NCH = 3
CW = 364
TOK = NCH * CW
KD = DM // P
EPS = 1e-6
CHUNK = 64
NCK = LIVE // CHUNK
A_HEADS, A_KV, A_DIM = 16, 4, 64
WIN = 128
B_HEADS, B_DK, B_DV, B_LOW = 4, 128, 256, 16
GATE_NORM = 16.0
CWID, CBLK, CONV_W = 1536, 192, 4
KC = CWID // P
EXT = CONV_W - 1
MIX = 16
OFF_Q, OFF_K, OFF_V, OFF_BQ, OFF_BK, OFF_BV, OFF_LR, OFF_G = 0, 1024, 1280, 1536, 2048, 2560, 3584, 3600

PIECE = 1024
PC_LR, PC_K, PC_V = 0, 1, 3
PC_A, A_PCS = 5, 4
PC_B0 = PC_A + A_KV * A_PCS
PC_B, B_PCS = PC_B0 + 2, 6
PC_OE = PC_B + B_HEADS * B_PCS - 2
PC_C, C_PCS = PC_OE + 2 * KD, 9
PC_OO = PC_C + 4 * C_PCS
PIECES = PC_OO + 2 * KD + 1
HALF = PIECE // 2

USE_A = (2, 1)
USE_A1 = (USE_A[0] + 2, USE_A[1] + 2)
USE_B0 = USE_A1[0] + 4 * (A_KV - 1)
USE_B = (USE_B0 + 3, USE_A1[1])
USE_OE = (USE_B[0] + 3 * B_HEADS - 2, USE_B[1] + 3 * B_HEADS - 1)
USE_C = (USE_OE[0] + 4, USE_OE[1] + 4)
USE_OO = (USE_C[0] + 24, USE_C[1] + 24)

VC_N = (0, 8, 16)
VC_BLR = 24
VC_GN = 28
VC_SINK = 30
VC_C = 46
VB = 12
VC_ALL = VC_C + KC * VB

CC_ID, CC_CAUSAL, CC_DIST = 0, 128, 256
CC_SLOPE = CC_DIST + 2 * P
CC_ALL = CC_SLOPE + A_HEADS

NT = 9
ATT_UNITS = 2 * NT
K0_STEPS = 8
LR_STEP = 2 * K0_STEPS + 1

ARENA = 14400


def one(t, k):
    return t[bass.ds(k, 1)].rearrange("a p n -> p (a n)")


def slot(t, k, a=0, b=None):
    return t[:, bass.ds(k, 1), a:t.shape[2] if b is None else b].rearrange("p a n -> p (a n)")


def unit(u):
    return u % NT, u // NT


def key_cols(t):
    return (P, 2 * P) if t == 0 else (0, WIN + DEC) if t == NT - 1 else (0, 2 * P)


def c_use(m, n):
    return 3 + 3 * m + n


def tile_rows(t):
    return DEC if t == NT - 1 else P


def build_program(nc, xT, weights, vecs_d, consts_d, wlr_d, kc_d, vc_d, sg_d,
                  yT, k_out, v_out, gla_p_out, gla_s_out, conv_out, lru_out):
    k_all = nc.dram_tensor("k_scratch", (A_KV, A_DIM, SEQ + WIN + DEC), F32).ap()
    x1_d = nc.dram_tensor("x1_scratch", (KD, P, TOK), F32).ap()

    ctx = ExitStack()
    with ctx:
        at_byte = [32 * -(-nc.sbuf_base // 32)]

        def sb(name, shape, dt=F32, at=None):
            size = 4 * int(np.prod(shape[1:]))
            if at is None:
                at = at_byte[0]
                at_byte[0] += 32 * -(-size // 32)
            return nc.alloc_sbuf_tensor_at(name, shape, dt, offset=at)

        def sem(name):
            return ctx.enter_context(nc.semaphore(name))

        H = sb("H", [P, MIX, TOK], F32R)
        y_at = at_byte[0]
        Y = sb("Y", [P, MIX, TOK])
        Yr = sb("Yr", [P, MIX, TOK], F32R, at=y_at)
        raw = sb("raw", [P, 2, PIECE])
        w_hi = sb("w_hi", [P, 2, PIECE], F32R)
        w_lo = sb("w_lo", [P, 2, PIECE], F32R)
        vecs = sb("vecs", [P, VC_ALL])
        consts = sb("consts", [P, CC_ALL])
        ones = sb("ones", [P, P])[:, :]
        wlr_cur = sb("wlr_cur", [P, P])
        rT = sb("rT", [P, NT])
        sm = sb("sm", [P, 3, 12])
        nsink = sb("nsink", [P, A_HEADS])
        cur_sink = sb("cur_sink", [P, 3, 4])
        cur_b = sb("cur_b", [P, 4])
        cur = sb("cur", [P, 3, VB])
        nsp = sb("nsp", [P, KC, 4])
        cur_n = sb("cur_n", [P, 3, 4])
        lamt = sb("lamt", [P, KC])
        cvo = sb("cvo", [P, KC, 2 * EXT])
        lro = sb("lro", [P, KC, 2])
        arena_at = at_byte[0]
        arena = sb("arena", [P, ARENA])
        ur = sb("ur", [P, 2, 3, TOK], F32R, at=arena_at)

        def part(at, *shape):
            n = int(np.prod(shape))
            assert at + n <= ARENA
            v = arena[:, at:at + n]
            if len(shape) == 2:
                return v.rearrange("p (a b) -> p a b", a=shape[0])
            if len(shape) == 3:
                return v.rearrange("p (a b c) -> p a b c", a=shape[0], b=shape[1])
            return v

        X = part(0, KD, TOK)
        sq = part(KD * TOK, TOK)
        res = part(9 * TOK, 2, TOK)
        acc = part(ARENA - 2 * TOK, TOK)
        rb = part(ARENA - TOK, TOK)
        diag = part(9 * TOK, NT, P)
        blr_raw = part(9 * TOK + NT * P, TOK)
        blrT = part(ARENA - 2 * TOK, TOK)
        KW = SEQ + WIN + DEC
        q = part(0, 2, TOK)
        kz = part(2184, 2, KW)
        Vz = part(4616, 10, 192)
        Ssb = part(6536, 3, 2, 256)
        PT = part(8072, 2, 512)
        V = Y[:, 8:11, :].rearrange("p a n -> p (a n)")[:, 0:2560].rearrange("p (a n) -> p a n", a=10)
        gt = Y[:, 12, :]
        gz = Y[:, 13, :]
        kT = Y[:, 14:16, :]
        E = part(0, TOK)
        Ei = part(TOK, TOK)
        qg = part(2 * TOK, TOK)
        kg = part(3 * TOK, TOK)
        kd = part(4 * TOK, TOK)
        sq2 = part(2 * TOK, 2, TOK)
        gs = part(5 * TOK, 2, TOK)
        tb = part(7 * TOK, 2, TOK)
        Vb = part(7 * TOK, NT, 256)
        o0 = 7 * TOK + NT * 256
        kdT = part(o0, 2, P)
        aT = part(o0 + 512, 2, P)
        St = part(o0 + 768, 3, 256)
        Sst = part(o0 + 1536, 256)
        qs, ks = gs[:, 0, :], gs[:, 1, :]
        elast = part(o0 + 1792, NCK)
        qf = part(o0 + 1792 + NCK, NCK)
        kf = part(o0 + 1792 + 2 * NCK, NCK)
        etile = part(o0 + 1792 + 3 * NCK, NT)
        assert o0 + 1792 + 3 * NCK + NT <= ARENA - 2 * TOK
        xc = part(6 * TOK, 1104)
        tr, ti, aa, th, sa = (part(6 * TOK + 1104 + n * TOK, TOK) for n in range(5))
        gc = th
        U = Y[:, 12:15, :]
        cgz = Y[:, 15, :]

        ps = ctx.enter_context(nc.psum_tensor("ps", [P, 8, 512], F32))
        sets = [ps[:, 0:3, :], ps[:, 3:6, :]]

        def chunks(ap):
            return ap.rearrange("p (c n) -> p c n", c=NCH)

        def setv(s):
            return sets[s][:, :, 0:CW]

        ident = consts[:, CC_ID:CC_ID + P]
        causal = consts[:, CC_CAUSAL:CC_CAUSAL + P]
        dist = consts[:, CC_DIST:CC_DIST + 2 * P]

        w_in = [sem("w_in0"), sem("w_in1")]
        x_in = [sem(f"x_in{b}") for b in range(KD)]
        vecs_in, consts_in, wlr_in, vcache_in = sem("vecs_in"), sem("consts_in"), sem("wlr_in"), sem("vcache_in")
        k_all_in, kz_in, gstate_in = sem("k_all_in"), sem("kz_in"), sem("gstate_in")
        res_in = [sem("res_in0"), sem("res_in1")]
        x1_saved, k_saved, v_saved, gla_saved = sem("x1_saved"), sem("k_saved"), sem("v_saved"), sem("gla_saved")
        small_saved, y_saved = sem("small_saved"), sem("y_saved")
        ones_set, w_hi_done, w_split = sem("ones_set"), sem("w_hi_done"), sem("w_split")
        half_done, piece_done = sem("half_done"), sem("piece_done")
        drained = [sem("drained0"), sem("drained1")]
        acc_zero, sq_done, acc_done, ssq_done = sem("acc_zero"), sem("sq_done"), sem("acc_done"), sem("ssq_done")
        ms_done, std_done, rt_done, diag_done = sem("ms_done"), sem("std_done"), sem("rt_done"), sem("diag_done")
        bc_done, rb_done, rt_init, xn_done = sem("bc_done"), sem("rb_done"), sem("rt_init"), sem("xn_done")
        h_hi_done, h_lo_done = sem("h_hi_done"), sem("h_lo_done")
        v_done, v_free = sem("v_done"), sem("v_free")
        a_zeroed, vz_ready, gate_tanh = sem("a_zeroed"), sem("vz_ready"), sem("gate_tanh")
        gated, blr_ready, es_done = sem("gated"), sem("blr_ready"), sem("es_done")
        sink_neg, sink_cur = sem("sink_neg"), sem("sink_cur")
        s_done, s_free, mx_done, nm_done, ds_done = (sem(n) for n in (
            "s_done", "s_free", "mx_done", "nm_done", "ds_done"))
        exp_done, den_done, rcp_done, p_done = sem("exp_done"), sem("den_done"), sem("rcp_done"), sem("p_done")
        pt_done, pt_free, o_done, o_free = sem("pt_done"), sem("pt_free"), sem("o_done"), sem("o_free")
        bias_ready, lora_done, z_act, z_sub, gc_done = (sem(n) for n in (
            "bias_ready", "lora_done", "z_act", "z_sub", "gc_done"))
        q_ready, k0_ready, q0_ready, ks_done, e_done, kd_done, s0_ready, b_gate = (sem(n) for n in (
            "q_ready", "k0_ready", "q0_ready", "ks_done", "e_done", "kd_done", "s0_ready", "b_gate"))
        el_done, y_zeroed = sem("el_done"), sem("y_zeroed")
        at_done, kdt_done, at_masked, kdT_done = (sem(n) for n in (
            "at_done", "kdt_done", "at_masked", "kdT_done"))
        tf_set, f_done = sem("tf_set"), sem("f_done")
        gds_done, s_upd, go_done, go_saved = sem("gds_done"), sem("s_upd"), sem("go_done"), sem("go_saved")
        sq2_done, sq2_added, gn_done, gn_std, gn_rstd, gs_done, bn_done, b_done = (sem(n) for n in (
            "sq2_done", "sq2_added", "gn_done", "gn_std", "gn_rstd", "gs_done", "bn_done", "b_done"))
        y_hi_done, y_lo_done = sem("y_hi_done"), sem("y_lo_done")
        lam_act, nsp_ready, cur_ready, xc_zeroed = (sem(n) for n in (
            "lam_act", "nsp_ready", "cur_ready", "xc_zeroed"))
        cv_step, cv_done, u_hi_done, u_lo_done, cvo_done = (sem(n) for n in (
            "cv_step", "cv_done", "u_hi_done", "u_lo_done", "cvo_done"))
        c_tanh, c_a, c_w, c_sqrt, c_iu, c_b, c_scan, c_gy, c_y = (sem(n) for n in (
            "c_tanh", "c_a", "c_w", "c_sqrt", "c_iu", "c_b", "c_scan", "c_gy", "c_y"))

        block = ctx.enter_context(nc.Block())

        @block.sync
        def _(sp):
            sp.dma_start(raw[:, 0, :], weights[0]).then_inc(w_in[0], 16)
            sp.dma_start(X[:, 0, :], xT[0]).then_inc(x_in[0], 16)
            sp.dma_start(raw[:, 1, :], weights[1]).then_inc(w_in[1], 16)
            with sp.Fori(1, PIECES // 2) as i:
                for s in range(2):
                    sp.wait_ge(w_split, 4 * i + 2 * (s - 1))
                    sp.dma_start(raw[:, s, :], one(weights, 2 * i + s)).then_inc(w_in[s], 16)

        @block.gpsimd
        def _(pool):
            def split(i, s, first):
                pool.wait_ge(w_in[s], 16 * i + 16)
                for h in range(2):
                    cols = slice(h * HALF, (h + 1) * HALF)
                    if not first:
                        pool.wait_ge((half_done, piece_done)[h], 2 * i + (s - 1))
                    pool.tensor_tensor(w_hi[:, s, cols].rearrange("p (k n) -> p k n", n=P),
                                       raw[:, s, cols].rearrange("p (k n) -> p k n", n=P), every_tile_ones,
                                       ALU.mult).then_inc(w_hi_done, 1)
                    pool.wait_ge(w_hi_done, 4 * i + (2 * s + h + 1))
                    pool.tensor_tensor(w_lo[:, s, cols], raw[:, s, cols], w_hi[:, s, cols].bitcast(F32),
                                       ALU.subtract).then_inc(w_split, 1)

            every_tile_ones = ones.rearrange("p (k n) -> p k n", k=1).to_broadcast([P, HALF // P, P])
            pool.memset(ones, 1.0).then_inc(ones_set, 1)
            pool.wait_ge(ones_set, 1)
            for s in range(2):
                split(0, s, True)
            with pool.Fori(1, PIECES // 2) as i:
                for s in range(2):
                    split(i, s, False)

        @block.tensor
        def _(pe):
            def project(s, kts, piece, rhs_hi, rhs_lo, st, first=True, last=True, at0=0, ready=None, half_end=3):
                for n, k in enumerate(kts):
                    if (at0 + n) % 4 == 0:
                        pe.wait_ge(w_split, 2 * piece + ((at0 + n) // 4 + 1))
                    if ready is not None:
                        pe.wait_ge(ready[0], ready[1] + k + 1)
                    w = slice((at0 + n) * P, (at0 + n + 1) * P)
                    for m, (lw, rx) in enumerate(((w_hi, rhs_hi), (w_lo, rhs_hi), (w_hi, rhs_lo))):
                        for c in range(NCH):
                            mm = pe.matmul(sets[st][:, c, 0:CW], lw[:, s, w], rx[:, k, c * CW:(c + 1) * CW],
                                           start=(first and n == 0 and m == 0),
                                           stop=(last and n == len(kts) - 1 and m == 2))
                    if at0 + n == half_end:
                        mm.then_inc(half_done, 1)
                return mm

            H_hi, H_lo = H[:, 0:KD, :], H[:, KD:2 * KD, :]
            K8 = range(KD)

            def in_block(s, st, piece, before):
                pe.wait_ge(drained[st], before)
                project(s, K8, piece, H_hi, H_lo, st).then_inc(piece_done, 1)

            def sum_squares(n):
                pe.wait_ge(acc_done, KD * (n + 1))
                for t in range(NT):
                    m = TOK - SEQ if t == NT - 1 else P
                    mm = pe.matmul(ps[0:m, 7, t:t + 1], acc[:, t * P:t * P + m], ones[:, 0:1], start=True, stop=True)
                mm.then_inc(ssq_done, 1)

            def broadcast(n, bank):
                pe.wait_ge(diag_done, n + 1)
                for c in range(2):
                    pe.matmul(ps[:, 6 + c, :], ones, diag[:, 4 * c:4 * c + 4, :].rearrange("p t n -> p (t n)"),
                              start=True, stop=True)
                mm = pe.matmul(ps[:, bank, CW:CW + TOK - SEQ], ones, diag[:, NT - 1, 0:TOK - SEQ],
                               start=True, stop=True)
                mm.then_inc(bc_done, 1)

            def project_v(piece, base, between=None):
                for t in range(NT):
                    if between and t == 3:
                        between()
                    m = TOK - SEQ if t == NT - 1 else P
                    if t >= 2:
                        pe.wait_ge(v_free, base + t - 1)
                    for k in K8:
                        if t == 0 and k % 2 == 0:
                            pe.wait_ge(w_split, 2 * piece + (k // 2 + 1))
                        wk = slice((k % 4) * 256, (k % 4) * 256 + 256)
                        s = 1 - k // 4
                        for n, (lx, rw) in enumerate(((H_hi, w_hi), (H_hi, w_lo), (H_lo, w_hi))):
                            mm = pe.matmul(ps[0:m, 6 + t % 2, 0:256], lx[:, k, t * P:t * P + m], rw[:, s, wk],
                                           start=(k == 0 and n == 0), stop=(k == KD - 1 and n == 2))
                        if t == NT - 1 and k % 2:
                            mm.then_inc((half_done, piece_done)[k // 2 % 2], 1)
                    if t < NT - 1:
                        mm.then_inc(v_done, 1)

            pe.sem_inc(pt_done, 3)
            pe.sem_inc(o_done, 2)

            pe.wait_ge(ones_set, 1)

            def low_rank_input(k):
                mm = project(0, [k], PC_LR, H_hi, H_lo, 0, first=(k == 0), last=(k == KD - 1), at0=k,
                             ready=(h_lo_done, 0))
                if k == KD - 1:
                    mm.then_inc(piece_done, 1)

            for k in range(3):
                low_rank_input(k)
            for k in K8:
                if k + 3 < KD:
                    low_rank_input(k + 3)
                b = project(1, [k], PC_K, H_hi, H_lo, 1, first=(k == 0), last=(k == KD - 1), at0=k)
            b.then_inc(piece_done, 1)
            pe.wait_ge(drained[0], 1)
            for k in K8:
                if k == 2:
                    sum_squares(0)
                if k == 6:
                    broadcast(0, 5)
                a = project(0, [k], PC_K + 1, H_hi, H_lo, 0, first=(k == 0), last=(k == KD - 1), at0=k)
            a.then_inc(piece_done, 1)
            pe.wait_ge(rb_done, 1)
            project_v(PC_V, 0)

            for n in range(A_PCS):
                in_block(1 - n % 2, n % 2, PC_A + n, USE_A[n % 2] + n // 2)
            pe.wait_ge(v_free, NT)
            pe.wait_ge(drained[1], USE_A1[1])
            pe.wait_ge(a_zeroed, 3)

            def scores(u, U):
                t, b = unit(u)
                r = tile_rows(t)
                pe.wait_ge(s_free, U + 1)
                k0, k1, c0 = (SEQ, KW, 0) if t == NT - 1 else ((t - 1) * P, (t + 1) * P, 0)
                if t == 0:
                    k0, c0 = 0, P
                pe.matmul(ps[0:r, 3 + u % 2, :].rearrange("p (j n) -> p j n", j=2)[:, :, c0:c0 + k1 - k0],
                          q[:, b, t * P:t * P + r], kz[:, :, k0:k1], start=True, stop=True).then_inc(s_done, 1)

            def key_tiles(t):
                if t == NT - 1:
                    return [(0, 8, P), (1, 9, DEC)]
                return ([(0, t - 1, P)] if t else []) + [(1, t, P)]

            def transposes(u, U):
                t, _ = unit(u)
                pe.wait_ge(pt_free, U + 1)
                pe.wait_ge(p_done, U + 1)
                for kt, _, rows in key_tiles(t):
                    for j in range(2):
                        mm = pe.transpose(ps[0:rows, 5 + u % 2, (2 * kt + j) * P:(2 * kt + j + 1) * P],
                                          Ssb[:, u % 3, j, kt * P:kt * P + rows], ident)
                mm.then_inc(pt_done, 1)

            def mix_values(u, U):
                t, _ = unit(u)
                r = tile_rows(t)
                pe.wait_ge(pt_free, U + 3)
                pe.wait_ge(o_free, U + 1)
                tiles = key_tiles(t)
                for n, (kt, tile, rows) in enumerate(tiles):
                    for j in range(2):
                        mm = pe.matmul(ps[:, 7, 0:r], Vz[0:rows, tile, 64 * (1 - j):64 * (1 - j) + P],
                                       PT[0:rows, u % 2, (2 * kt + j) * P:(2 * kt + j) * P + r],
                                       start=(n == 0 and j == 0), stop=(n == len(tiles) - 1 and j == 1))
                mm.then_inc(o_done, 1)

            def low_rank(h, before):
                pe.wait_ge(wlr_in, 16 * h + 16)
                pe.wait_ge(drained[0], before)
                for c in range(NCH):
                    mm = pe.matmul(sets[0][:, c, 0:CW], wlr_cur[:, :], blrT[:, c * CW:(c + 1) * CW],
                                   start=True, stop=True)
                mm.then_inc(lora_done, 1)

            def attend(g, blocks, steps):
                pe.wait_ge(drained[0], USE_A1[0] + 4 * g)
                pe.wait_ge(kz_in, 32 * g + 32)
                pe.wait_ge(vz_ready, g + 1)
                U = ATT_UNITS * g
                tiles = -(-3 * KD // steps)
                for s in range(ATT_UNITS + 3):
                    if s < ATT_UNITS:
                        scores(s, U + s)
                    if 0 <= s - 2 < ATT_UNITS:
                        transposes(s - 2, U + (s - 2))
                    if s >= 3:
                        mix_values(s - 3, U + (s - 3))
                    if s < blocks * steps:
                        n, f = s // steps, s % steps
                        piece = PC_A + A_PCS * (g + 1) + n
                        if f == 0:
                            pe.wait_ge(drained[0], USE_A1[0] + 4 * g + n)
                        for x in range(tiles * f, min(tiles * (f + 1), 3 * KD)):
                            k, m = x // 3, x % 3
                            if k % 4 == 0 and m == 0:
                                pe.wait_ge(w_split, 2 * piece + (k // 4 + 1))
                            lw, rx = ((w_hi, H_hi), (w_lo, H_hi), (w_hi, H_lo))[m]
                            for c in range(NCH):
                                mm = pe.matmul(sets[0][:, c, 0:CW], lw[:, 1 - n % 2, k * P:(k + 1) * P],
                                               rx[:, k, c * CW:(c + 1) * CW], start=(x == 0), stop=(x == 3 * KD - 1))
                            if (k, m) == (3, 2):
                                mm.then_inc(half_done, 1)
                        if f == steps - 1:
                            mm.then_inc(piece_done, 1)
                    if blocks == 2 and s == LR_STEP:
                        pe.wait_ge(blr_ready, 1)
                        low_rank(0, USE_B0 + 2)

            with pe.Fori(0, A_KV - 1) as g:
                attend(g, A_PCS, 5)
            attend(A_KV - 1, 2, K0_STEPS)

            pe.wait_ge(pt_free, A_KV * ATT_UNITS + 2)
            pe.wait_ge(o_free, A_KV * ATT_UNITS + 1)

            def gla_head(i, last):
                u0, u1 = USE_B[0] + 3 * i, USE_B[1] + 3 * i
                piece = PC_B + B_PCS * i
                project_v(piece, NT * (i + 1), None if last else lambda: low_rank(i + 1, u0))
                pe.wait_ge(q_ready, i + 1)
                if not last:
                    pe.wait_ge(drained[0], u0 + 1)
                pe.wait_ge(v_free, NT * (i + 2))
                T0 = NT * i

                def front(t):
                    r = tile_rows(t)
                    if t >= 2:
                        pe.wait_ge(at_masked, T0 + t - 1)
                        pe.wait_ge(kdT_done, T0 + t - 1)
                    cols = slice(t * P, t * P + r)
                    mm = pe.matmul(ps[0:r, t % 2, 0:r], kg[:, cols], qg[:, cols], start=True, stop=True)
                    if r == P:
                        mm = pe.matmul(ps[0:CHUNK, t % 2, CHUNK:P], kd[:, t * P:t * P + CHUNK],
                                       qg[:, t * P + CHUNK:(t + 1) * P], start=True, stop=True)
                    mm.then_inc(at_done, 1)
                    pe.transpose(ps[0:r, 2 + 3 * (t % 2), 0:P], ks[:, cols], ident).then_inc(kdt_done, 1)

                def back(t):
                    r = tile_rows(t)
                    pe.wait_ge(kdT_done, T0 + t + 1)
                    if t >= 2:
                        pe.wait_ge(s_upd, T0 + t - 1)
                    pe.matmul(ps[:, 6 + t % 2, 0:256], kdT[0:r, t % 2, :], Vb[0:r, t, :],
                              start=True, stop=True).then_inc(gds_done, 1)
                    pe.wait_ge(at_masked, T0 + t + 1)
                    if t >= 2:
                        pe.wait_ge(go_saved, T0 + t - 1)
                    if t == 0:
                        pe.wait_ge(s0_ready, i + 1)
                    if t == NT - 1:
                        pe.wait_ge(gstate_in, 16 * i + 16)
                    for e in range(2):
                        cols = slice(e * P, (e + 1) * P)
                        pe.matmul(ps[:, 3 + t % 2, e * P:e * P + r], Vb[0:r, t, cols], aT[0:r, t % 2, 0:r],
                                  start=True, stop=False)
                        if 0 < t < NT - 1:
                            pe.wait_ge(s_upd, T0 + t)
                        state = Sst[:, cols] if t == NT - 1 else St[:, t % 3, cols]
                        mm = pe.matmul(ps[:, 3 + t % 2, e * P:e * P + r], state, qs[:, t * P:t * P + r],
                                       start=False, stop=True)
                    mm.then_inc(go_done, 1)

                front(0)
                for t in range(NT):
                    if t + 1 < NT:
                        front(t + 1)
                    back(t)
                pe.wait_ge(go_saved, T0 + NT)
                pe.wait_ge(at_masked, T0 + NT)
                pe.wait_ge(kdT_done, T0 + NT)
                g0 = u0 if last else u0 + 1
                in_block(1, 1, piece + 2, u1)
                in_block(0, 0, piece + 3, g0)
                pe.wait_ge(drained[1], u1 + 1)
                pe.wait_ge(sq2_added, i + 1)
                for c in range(NCH):
                    mm = pe.matmul(sets[1][:, c, 0:CW], ones, sq2[:, 0, c * CW:(c + 1) * CW], start=True, stop=True)
                mm.then_inc(gn_done, 1)
                if not last:
                    in_block(1, 0, piece + 4, g0 + 1)
                    in_block(0, 1, piece + 5, u1 + 2)

            with pe.Fori(0, B_HEADS - 1) as i:
                gla_head(i, False)
            gla_head(B_HEADS - 1, True)

            def out_projection(kt, base, use, ready):
                def pair(i, first):
                    for half in range(2):
                        piece = base + 4 * i + 2 * half
                        if not half:
                            pe.wait_ge(drained[0], use[0] + i)
                        if first:
                            for k in range(3):
                                out_tile(0, kt, half, k, piece, ready)
                            for k in range(kt):
                                if k + 3 < kt:
                                    out_tile(0, kt, half, k + 3, piece, ready)
                                if k == 0 and not half:
                                    pe.wait_ge(drained[1], use[1])
                                out_tile(1, kt, half, k, piece + 1, ready)
                        else:
                            for s in range(2):
                                if s and not half:
                                    pe.wait_ge(drained[1], use[1] + i)
                                project(1 - s, range(half * kt, (half + 1) * kt), piece + s, H, Yr, s,
                                        first=not half, last=half == 1).then_inc(piece_done, 1)
                pair(0, True)
                with pe.Fori(1, KD // 2) as i:
                    pair(i, False)

            def out_tile(s, kt, half, k, piece, ready):
                row = half * kt + k
                mm = project(1 - s, [row], piece, H, Yr, s, first=(row == 0), last=(row == 2 * kt - 1), at0=k,
                             ready=(y_lo_done, ready))
                if k == kt - 1:
                    mm.then_inc(piece_done, 1)

            out_projection(8, PC_OE, USE_OE, 0)

            U_hi, U_lo = ur[:, 0, :, :], ur[:, 1, :, :]

            def odd_group(i, p, first=False):
                piece = PC_C + 2 * C_PCS * i + C_PCS * p
                u = [USE_C[st] + 12 * i + 6 * p for st in range(2)]
                G = 6 * i + 3 * p
                for n in range(3):
                    if first and n < 2:
                        for k in K8:
                            if (n, k) == (0, 7):
                                sum_squares(1)
                            if (n, k) == (1, 2):
                                broadcast(1, 2)
                            mm = project(1 - n, [k], piece + n, H_hi, H_lo, n, first=(k == 0), last=(k == KD - 1),
                                         at0=k, ready=(h_lo_done, KD))
                        mm.then_inc(piece_done, 1)
                        continue
                    pe.wait_ge(drained[n % 2], u[n % 2] + n // 2)
                    project((p + n + 1) % 2, K8, piece + n, H_hi, H_lo, n % 2).then_inc(piece_done, 1)
                for m in range(3):
                    kts = ((0, 1), (0, 1, 2), (1, 2))[m]
                    for n in range(2):
                        v = c_use(m, n)
                        pe.wait_ge(drained[v % 2], u[v % 2] + v // 2)
                        if n == 0 and m < 2:
                            pe.wait_ge(u_lo_done, G + 2 + m)
                        project((p + 2 * m) % 2, kts, piece + 3 + 2 * m, U_hi, U_lo, v % 2, at0=4 * n,
                                half_end=None).then_inc(piece_done if n else half_done, 1)
                    v = c_use(m, 2)
                    in_block((p + 1 + 2 * m) % 2, v % 2, piece + 4 + 2 * m, u[v % 2] + v // 2)

            pe.wait_ge(drained[0], USE_C[0])
            pe.wait_ge(drained[1], USE_C[1] - 1)
            odd_group(0, 0, first=True)
            odd_group(0, 1)
            with pe.Fori(1, 2) as i:
                for p in range(2):
                    odd_group(i, p)
            out_projection(6, PC_OO, USE_OO, MIX)
            sum_squares(2)
            broadcast(2, 2)

        @block.scalar
        def _(act):
            act.wait_ge(ones_set, 1)
            act.activation(lamt[:, 0:1], ones[:, 0:1], ACT.Square)
            act.dma_start(vecs[:, :], vecs_d).then_inc(vecs_in, 16)
            for b in range(1, KD):
                act.dma_start(X[:, b, :], xT[b]).then_inc(x_in[b], 16)
            act.dma_start(consts[:, :], consts_d).then_inc(consts_in, 16)

            act.sem_inc(pt_free, 2)

            def split_h(n, b):
                act.activation(H[:, b, :], X[:, b, :], ACT.Copy, scale=vecs[:, VC_N[n] + b:VC_N[n] + b + 1])\
                   .then_inc(h_hi_done, 1)

            def norm_roots(n):
                act.wait_ge(ms_done, n + 1)
                act.activation(rT[:, 0:NT - 1], rT[:, 0:NT - 1], ACT.Sqrt)
                act.activation(rT[0:TOK - SEQ, NT - 1:NT], rT[0:TOK - SEQ, NT - 1:NT], ACT.Sqrt).then_inc(std_done, 1)

            def norm_copy(n, bank):
                act.wait_ge(bc_done, n + 1)
                act.activation(rb[:, 0:SEQ].rearrange("p (a n) -> p a n", a=2), ps[:, 6:8, :], ACT.Copy)
                act.activation(rb[:, SEQ:TOK], ps[:, bank, CW:CW + TOK - SEQ], ACT.Copy).then_inc(rb_done, 1)

            act.wait_ge(vecs_in, 16)
            for b in range(KD):
                act.wait_ge(x_in[b], 16)
                split_h(0, b)
                if b:
                    act.wait_ge(acc_done, b)
                act.activation(sq, X[:, b, :], ACT.Square).then_inc(sq_done, 1)

            act.dma_start(k_all[:, :, SEQ:SEQ + WIN], kc_d).then_inc(k_all_in, 16)
            act.dma_start(V[:, 8, :], vc_d).then_inc(vcache_in, 16)
            act.wait_ge(piece_done, PC_LR + 1)
            act.activation(chunks(blr_raw), setv(0), ACT.Copy).then_inc(drained[0], 1)
            norm_roots(0)
            norm_copy(0, 5)
            for b in range(2):
                act.wait_ge(drained[1 - b], b + 1)
                for dst, c0, c1, d0, done in ((k_all, 0, SEQ, 0, k_all_in), (k_all, SEQ, LIVE, SEQ + WIN, k_all_in),
                                              (k_out, SEQ - WIN, LIVE, 0, k_saved)):
                    act.dma_start(dst[2 * b:2 * b + 2, :, d0:d0 + c1 - c0].rearrange("g d n -> (g d) n"),
                                  kT[:, b, c0:c1]).then_inc(done, 16)

            def load_keys(g):
                for j in range(2):
                    act.dma_start(kz[64 * j:64 * j + 64, j, :], one(k_all, g)).then_inc(kz_in, 16)

            act.wait_ge(k_all_in, 80)
            act.wait_ge(a_zeroed, 3)
            load_keys(0)
            act.wait_ge(rt_done, 1)
            for t in range(NT):
                r = tile_rows(t)
                if t < NT - 1:
                    act.wait_ge(v_done, t + 1)
                else:
                    act.wait_ge(piece_done, PC_V + 2)
                act.activation(V[0:r, t if t < 8 else 9, :], ps[0:r, 6 + t % 2, 0:256], ACT.Copy,
                               scale=rT[0:r, t:t + 1]).then_inc(v_free, 1)
            act.wait_ge(v_free, NT)
            act.dma_start(v_out[0:P, :], V[:, 7, :]).then_inc(v_saved, 16)
            act.dma_start(v_out[P:P + DEC, :], V[0:DEC, 9, :]).then_inc(v_saved, 16)

            def gate_tanh_of(st, use):
                act.wait_ge(drained[st], use)
                act.activation(gt, gz, ACT.Tanh, scale=0.5).then_inc(gate_tanh, 1)

            for n in range(2):
                gate_tanh_of(n, USE_A[n] + 1)

            def gate_bias(h):
                act.activation(cur_b[:, 0:1], vecs[:, bass.ds(VC_BLR + h, 1)], ACT.Copy).then_inc(bias_ready, 1)

            def log_gate(h, steps=range(3)):
                if 0 in steps:
                    act.wait_ge(lora_done, h + 1)
                    act.dma_start(wlr_cur[:, :], one(wlr_d, h + 1)).then_inc(wlr_in, 16)
                    act.activation(chunks(E), setv(0), ACT.Abs, bias=cur_b[:, 0:1]).then_inc(z_act, 1)
                if 1 in steps:
                    act.wait_ge(z_act, 3 * h + 1)
                    act.activation(E, E, ACT.Exp, scale=-1.0).then_inc(z_act, 1)
                if 2 in steps:
                    act.wait_ge(z_act, 3 * h + 2)
                    act.activation(E, E, ACT.Ln, bias=1.0).then_inc(z_act, 1)

            act.dma_start(wlr_cur[:, :], wlr_d[0]).then_inc(wlr_in, 16)
            act.activation(cur_b[:, 0:1], vecs[:, VC_BLR:VC_BLR + 1], ACT.Copy).then_inc(bias_ready, 1)

            def attend(g, more):
                U = ATT_UNITS * g
                for s in range(ATT_UNITS + 3):
                    if s < ATT_UNITS:
                        t, r3 = unit(s)[0], s % 3
                        r = tile_rows(t)
                        c0, c1 = key_cols(t)
                        act.wait_ge(ds_done, U + s + 1)
                        for j in range(2):
                            act.activation(Ssb[0:r, r3, j, c0:c1], Ssb[0:r, r3, j, c0:c1], ACT.Exp,
                                           bias=sm[0:r, r3, 2 + j:3 + j], scale=float(A_DIM) ** -0.5,
                                           accum_out=sm[0:r, r3, 6 + j:7 + j])
                        act.activation(sm[0:r, r3, 8:10], sm[0:r, r3, 4:6], ACT.Exp).then_inc(exp_done, 1)
                    if not more and s > LR_STEP:
                        log_gate(0, [s - LR_STEP - 1])
                    if more and s in (5, 10):
                        gate_tanh_of(0, USE_A1[0] + 4 * g + s // 5)
                    if more and s == ATT_UNITS - 1:
                        load_keys(g + 1)
                    if 2 <= s < ATT_UNITS + 2:
                        u = s - 2
                        t, _ = unit(u)
                        r = tile_rows(t)
                        act.wait_ge(pt_done, U + u + 4)
                        act.wait_ge(o_done, U + u + 1)
                        if t == NT - 1:
                            for kt, rows in ((0, P), (1, DEC)):
                                last = act.activation(
                                    PT[0:rows, u % 2, 2 * kt * P:2 * (kt + 1) * P].rearrange(
                                        "p (j n) -> p j n", j=2)[:, :, 0:r],
                                    ps[0:rows, 5 + u % 2, 2 * kt * P:2 * (kt + 1) * P].rearrange(
                                        "p (j n) -> p j n", j=2)[:, :, 0:r], ACT.Copy)
                        else:
                            c = 2 * P if t == 0 else 0
                            last = act.activation(PT[:, u % 2, c:512], ps[:, 5 + u % 2, c:512], ACT.Copy)
                        last.then_inc(pt_free, 1)

            with act.Fori(0, A_KV - 1) as g:
                attend(g, True)
            attend(A_KV - 1, False)
            act.wait_ge(v_saved, 32)
            act.wait_ge(k_saved, 32)

            def decays(h):
                act.wait_ge(gc_done, h + 1)
                act.activation(Ei, E, ACT.Exp, scale=-1.0 / GATE_NORM).then_inc(e_done, 1)
                act.wait_ge(e_done, 2 * h + 1)
                act.activation(E, E, ACT.Exp, scale=1.0 / GATE_NORM).then_inc(e_done, 1)

            act.wait_ge(vz_ready, A_KV)
            act.wait_ge(o_free, A_KV * ATT_UNITS + 1)
            act.wait_ge(y_zeroed, 1)

            def values(i, t):
                r = tile_rows(t)
                if t < NT - 1:
                    act.wait_ge(v_done, (NT - 1) * (i + 1) + t + 1)
                else:
                    act.wait_ge(piece_done, PC_B + B_PCS * i + 2)
                act.activation(Vb[0:r, t, :], ps[0:r, 6 + t % 2, 0:256], ACT.Copy, scale=rT[0:r, t:t + 1])\
                   .then_inc(v_free, 1)

            values(0, 0)
            values(0, 1)
            decays(0)

            def head(i, last):
                piece = PC_B + B_PCS * i
                act.dma_start(Sst, one(sg_d, i)).then_inc(gstate_in, 16)
                if not last:
                    gate_bias(i + 1)
                    act.wait_ge(bias_ready, i + 2)
                for t in range(2, NT):
                    values(i, t)
                    if not last and 4 <= t < 7:
                        if t == 4:
                            act.wait_ge(q_ready, i + 1)
                        log_gate(i + 1, [t - 4])
                T0 = NT * i
                for t in range(NT):
                    r = tile_rows(t)
                    act.wait_ge(kdt_done, T0 + t + 1)
                    if t >= 2:
                        act.wait_ge(go_done, T0 + t - 1)
                    act.activation(kdT[0:r, t % 2, :], ps[0:r, 2 + 3 * (t % 2), 0:P], ACT.Copy).then_inc(kdT_done, 1)
                act.wait_ge(s_upd, T0 + NT - 1)
                act.dma_start(one(gla_p_out, i), St[:, (NT - 1) % 3, :]).then_inc(gla_saved, 16)
                act.wait_ge(s_upd, T0 + NT)
                act.wait_ge(go_saved, T0 + NT)
                act.dma_start(one(gla_s_out, i), St[:, NT % 3, :]).then_inc(gla_saved, 16)
                act.activation(sq2, Y[:, bass.ds(2 * i + 8, 2), :], ACT.Square).then_inc(sq2_done, 1)
                if not last:
                    decays(i + 1)

                def gate_tanh_b(n):
                    use = (USE_B[1] + 3 * i + 1, USE_B[0] + 3 * i + (1 if last else 2))[n]
                    act.wait_ge(drained[1 - n], use)
                    act.activation(tb[:, n, :], gs[:, n, :], ACT.Tanh, scale=0.5).then_inc(b_gate, 1)

                def root():
                    act.wait_ge(drained[1], USE_B[1] + 3 * i + 2)
                    act.activation(kd, kd, ACT.Sqrt).then_inc(gn_std, 1)

                gate_tanh_b(0)
                if not last:
                    gate_tanh_b(1)
                    root()
                    act.wait_ge(b_done, i + 1)
                    values(i + 1, 0)
                    values(i + 1, 1)
                    return
                act.wait_ge(piece_done, PC_OE)
                for k in range(MIX):
                    if k == 2:
                        gate_tanh_b(1)
                    if k == 4:
                        root()
                    if k == MIX - 2:
                        act.wait_ge(b_done, B_HEADS)
                    act.activation(H[:, k, :], Y[:, k, :], ACT.Copy).then_inc(y_hi_done, 1)

            with act.Fori(0, B_HEADS - 1) as i:
                head(i, False)
            head(B_HEADS - 1, True)

            def lambda_logs():
                act.activation(lamt[:, :], vecs[:, VC_C:VC_ALL].rearrange("p (b n) -> p b n", n=VB)[:, :, 7],
                               ACT.Abs).then_inc(lam_act, 1)
                act.wait_ge(lam_act, 1)
                act.activation(lamt[:, :], lamt[:, :], ACT.Exp, scale=-1.0).then_inc(lam_act, 1)
                act.wait_ge(lam_act, 2)
                act.activation(lamt[:, :], lamt[:, :], ACT.Ln, bias=1.0).then_inc(lam_act, 1)

            def out_residual(src, use, nsq, even):
                for s in range(2):
                    act.dma_start(res[:, s, :], src[s]).then_inc(res_in[s], 16)

                for b in range(KD):
                    i, s = b // 2, b % 2
                    if even and b == KD - 1:
                        act.wait_ge(piece_done, PC_C - 2)
                        for k in range(KD - 1):
                            split_h(1, k)
                    act.wait_ge(drained[s], use[s] + i + 1)
                    if b + 2 < KD:
                        act.dma_start(res[:, s, :], src[b + 2]).then_inc(res_in[s], 16)
                    if even:
                        act.dma_start(x1_d[b], X[:, b, :]).then_inc(x1_saved, 16)
                    if even and b == KD - 1:
                        split_h(1, b)
                    act.wait_ge(acc_done, nsq + b)
                    act.activation(sq, X[:, b, :], ACT.Square).then_inc(sq_done, 1)

            lambda_logs()
            out_residual(xT, USE_OE, KD, True)
            norm_roots(1)
            norm_copy(1, 2)

            act.wait_ge(xc_zeroed, 1)

            def mix_high(k):
                act.activation(slot(H, k), slot(Y, k), ACT.Copy).then_inc(y_hi_done, 1)

            def group(g, last):
                piece = PC_C + C_PCS * g
                u = [USE_C[st] + 6 * g for st in range(2)]
                G = 3 * g
                act.wait_ge(cur_ready, g + 1)

                def u_high(n):
                    act.wait_ge(cv_done, G + n + 1)
                    act.activation(ur[:, 0, n, :], U[:, n, :], ACT.Copy).then_inc(u_hi_done, 1)

                u_high(0)
                u_high(1)
                for m in range(3):
                    vr, vi, vg = (c_use(m, n) for n in range(3))
                    act.wait_ge(half_done, piece + 4 + 2 * m)
                    act.activation(chunks(tr), setv(vr % 2), ACT.Tanh, bias=cur_n[:, m, 2:3], scale=0.5)\
                       .then_inc(drained[vr % 2], 1)
                    act.wait_ge(piece_done, piece + 4 + 2 * m)
                    if m:
                        act.wait_ge(c_scan, 2 * G + 2 * m)
                    act.activation(chunks(ti), setv(vi % 2), ACT.Tanh, bias=cur_n[:, m, 3:4], scale=0.5)\
                       .then_inc(drained[vi % 2], 1)
                    if m == 0:
                        u_high(2)
                    act.wait_ge(drained[vr % 2], u[vr % 2] + vr // 2 + 1)
                    act.activation(aa, tr, ACT.Exp, bias=cur_n[:, m, 0:1], scale=cur_n[:, m, 0:1]).then_inc(c_a, 1)
                    if m:
                        act.wait_ge(c_y, G + m)
                    act.activation(th, tr, ACT.Tanh, bias=cur_n[:, m, 1:2], scale=cur_n[:, m, 1:2])
                    act.wait_ge(c_a, 2 * G + 2 * m + 1)
                    act.activation(sa, aa, ACT.Square).then_inc(c_a, 1)
                    act.wait_ge(c_w, G + m + 1)
                    act.activation(th, th, ACT.Sqrt).then_inc(c_sqrt, 1)
                    if last and m == 2:
                        act.wait_ge(piece_done, PC_OO)
                        mix_high(0)
                        mix_high(1)
                    act.wait_ge(c_b, G + m + 1)
                    act.wait_ge(drained[vg % 2], u[vg % 2] + vg // 2 + 1)
                    act.activation(gc, cgz, ACT.Tanh, scale=0.5).then_inc(c_tanh, 1)

            with act.Fori(0, KC // 3 - 1) as g:
                group(g, False)
            group(KC // 3 - 1, True)
            with act.Fori(2, KC - 1) as k:
                mix_high(k)
            act.wait_ge(c_y, KC)
            mix_high(KC - 1)
            act.dma_start(conv_out, cvo[:, :, :]).then_inc(small_saved, 16)
            act.dma_start(lru_out, lro[:, :, :]).then_inc(small_saved, 16)
            act.wait_ge(x1_saved, 16 * KD)
            out_residual(x1_d, USE_OO, 2 * KD, False)
            norm_roots(2)
            for b in range(KD):
                act.wait_ge(xn_done, b + 1)
                act.dma_start(yT[b], X[:, b, :]).then_inc(y_saved, 16)
            act.wait_ge(y_saved, 16 * KD)
            act.wait_ge(small_saved, 32)
            act.wait_ge(gla_saved, 32 * B_HEADS)
            act.wait_ge(k_saved, 32)
            act.wait_ge(v_saved, 32)

        @block.vector
        def _(dve):
            dve.sem_inc(s_free, 2)
            dve.sem_inc(o_free, 1)
            dve.memset(acc, 0.0).then_inc(acc_zero, 1)

            dve.memset(rT[:, :], 1.0).then_inc(rt_init, 1)

            def split_h(n, b):
                dve.wait_ge(h_hi_done, KD * n + b + 1)
                dve.scalar_tensor_tensor(H[:, KD + b, :], X[:, b, :], vecs[:, VC_N[n] + b:VC_N[n] + b + 1],
                                         H[:, b, :].bitcast(F32), ALU.mult, ALU.subtract).then_inc(h_lo_done, 1)

            def norm_factors(n):
                dve.wait_ge(ssq_done, n + 1)
                parts = [(slice(0, P), slice(0, NT - 1)), (slice(0, TOK - SEQ), slice(NT - 1, NT))]
                for r, c in parts:
                    mm = dve.tensor_scalar(rT[r, c], ps[r, 7, c], 1.0 / DM, EPS, ALU.mult, ALU.add)
                mm.then_inc(ms_done, 1)
                dve.wait_ge(std_done, n + 1)
                for r, c in parts:
                    mm = dve.reciprocal(rT[r, c], rT[r, c])
                mm.then_inc(rt_done, 1)
                dve.wait_ge(rt_done, n + 1)
                dve.tensor_tensor(diag, ident.rearrange("p (a n) -> p a n", a=1).to_broadcast([P, NT, P]),
                                  rT[:, :].rearrange("p (a n) -> p a n", n=1).to_broadcast([P, NT, P]),
                                  ALU.mult).then_inc(diag_done, 1)

            dve.wait_ge(ones_set, 1)
            dve.wait_ge(acc_zero, 1)
            dve.wait_ge(rt_init, 1)
            dve.wait_ge(vecs_in, 16)
            for b in range(KD):
                split_h(0, b)
                if b:
                    dve.wait_ge(acc_done, b)
                dve.wait_ge(sq_done, b + 1)
                dve.tensor_tensor(acc, acc, sq, ALU.add).then_inc(acc_done, 1)
            dve.wait_ge(consts_in, 16)
            norm_factors(0)

            dve.wait_ge(h_lo_done, KD)
            dve.memset(kz[64:P, 0, :], 0.0).then_inc(a_zeroed, 1)
            dve.memset(kz[0:64, 1, :], 0.0).then_inc(a_zeroed, 1)
            dve.memset(Vz[:, :, :], 0.0).then_inc(a_zeroed, 1)
            dve.tensor_scalar(nsink[:, :], vecs[:, VC_SINK:VC_SINK + A_HEADS], -1.0, None, ALU.mult)\
               .then_inc(sink_neg, 1)
            dve.wait_ge(a_zeroed, 3)
            dve.wait_ge(sink_neg, 1)
            dve.wait_ge(rb_done, 1)
            dve.wait_ge(piece_done, PC_K + 1)
            dve.tensor_tensor(chunks(kT[:, 0, :]), setv(1), chunks(rb), ALU.mult).then_inc(drained[1], 1)
            dve.wait_ge(piece_done, PC_K + 2)
            dve.tensor_tensor(chunks(kT[:, 1, :]), setv(0), chunks(rb), ALU.mult).then_inc(drained[0], 1)
            dve.tensor_tensor(blrT, blr_raw, rb, ALU.mult).then_inc(blr_ready, 1)

            def gate_in(st, piece, before):
                dve.wait_ge(piece_done, piece + 1)
                if before is not None:
                    dve.wait_ge(gated, before)
                dve.tensor_tensor(chunks(gz), setv(st), chunks(rb), ALU.mult).then_inc(drained[st], 1)

            def gate(k):
                dve.wait_ge(gate_tanh, k + 1)
                dve.scalar_tensor_tensor(slot(Y, k), gt, 1.0, gz, ALU.add, ALU.mult).then_inc(gated, 1)

            def q_in(b, st, piece):
                dve.wait_ge(piece_done, piece + 1)
                dve.tensor_tensor(chunks(q[:, b, :]), setv(st), chunks(rb), ALU.mult).then_inc(drained[st], 1)

            def attend(g, more):
                U = ATT_UNITS * g
                dve.wait_ge(gated, 2 * g + 2)
                dve.tensor_copy(Vz[:, 0:9, 64:128], V[:, 0:9, bass.ds(A_DIM * g, A_DIM)])
                dve.tensor_copy(Vz[0:64, 9, 64:128], V[0:64, 9, bass.ds(A_DIM * g, A_DIM)]).then_inc(vz_ready, 1)
                dve.tensor_copy(cur_sink[:, 0, :], vecs[:, bass.ds(VC_SINK + 4 * g, 4)])
                dve.tensor_copy(cur_sink[:, 2, :], consts[:, bass.ds(CC_SLOPE + 4 * g, 4)])
                dve.tensor_copy(cur_sink[:, 1, :], nsink[:, bass.ds(4 * g, 4)]).then_inc(sink_cur, 1)
                dve.wait_ge(sink_cur, g + 1)
                for s in range(ATT_UNITS + 4):
                    if s >= 4:
                        u = s - 4
                        t, b = unit(u)
                        r = tile_rows(t)
                        dve.wait_ge(o_done, U + u + 3)
                        y = slot(Y, 2 * g + b, t * P, t * P + r)
                        dve.tensor_tensor(y, ps[:, 7, 0:r], y, ALU.mult).then_inc(o_free, 1)
                    if not more and s in (K0_STEPS, 2 * K0_STEPS):
                        n = s // K0_STEPS - 1
                        if n == 0:
                            dve.wait_ge(k_saved, 32)
                        dve.wait_ge(piece_done, PC_B0 + n + 1)
                        dve.tensor_tensor(chunks(kT[:, n, :]), setv(0), chunks(rb), ALU.mult)\
                           .then_inc(drained[0], 1)
                    if more and s and s % 5 == 0:
                        piece = PC_A + A_PCS * (g + 1) + (s // 5 - 1)
                        if s < 15:
                            gate_in(0, piece, 2 * g + (s // 5 + 1))
                        else:
                            q_in(s // 5 - 3, 0, piece)
                    if s < ATT_UNITS:
                        (t, b), r3 = unit(s), s % 3
                        r = tile_rows(t)
                        c0, c1 = key_cols(t)
                        dve.wait_ge(s_done, U + s + 1)
                        dve.wait_ge(pt_done, U + s + 1)
                        for j in range(2):
                            last = dve.scalar_tensor_tensor(
                                Ssb[0:r, r3, j, c0:c1], dist[0:r, c0:c1], cur_sink[0:r, 2, 2 * b + j:2 * b + j + 1],
                                ps[0:r, 3 + s % 2, j * 256 + c0:j * 256 + c1], ALU.mult, ALU.add)
                        last.then_inc(s_free, 1)
                        dve.wait_ge(s_free, U + s + 3)
                        dve.tensor_reduce(sm[0:r, r3, 0:2], Ssb[0:r, r3, :, c0:c1], AX.X, ALU.max).then_inc(mx_done, 1)
                        dve.wait_ge(mx_done, U + s + 1)
                        dve.scalar_tensor_tensor(sm[0:r, r3, 2:4], sm[0:r, r3, 0:2], -float(A_DIM) ** -0.5,
                                                 cur_sink[0:r, 1, 2 * b:2 * b + 2], ALU.mult, ALU.min)\
                           .then_inc(nm_done, 1)
                        dve.wait_ge(nm_done, U + s + 1)
                        dve.tensor_tensor(sm[0:r, r3, 4:6], sm[0:r, r3, 2:4], cur_sink[0:r, 0, 2 * b:2 * b + 2],
                                          ALU.add).then_inc(ds_done, 1)
                    if 0 <= s - 1 < ATT_UNITS:
                        u = s - 1
                        t, r3 = unit(u)[0], u % 3
                        r = tile_rows(t)
                        c0, c1 = key_cols(t)
                        dve.wait_ge(exp_done, U + u + 1)
                        dve.tensor_tensor(sm[0:r, r3, 8:10], sm[0:r, r3, 8:10], sm[0:r, r3, 6:8], ALU.add)\
                           .then_inc(den_done, 1)
                        dve.wait_ge(den_done, U + u + 1)
                        dve.reciprocal(sm[0:r, r3, 10:12], sm[0:r, r3, 8:10]).then_inc(rcp_done, 1)
                        dve.wait_ge(rcp_done, U + u + 1)
                        for j in range(2):
                            last = dve.tensor_scalar(Ssb[0:r, r3, j, c0:c1], Ssb[0:r, r3, j, c0:c1],
                                                     sm[0:r, r3, 10 + j:11 + j], 0.5, ALU.mult, ALU.mult)
                        last.then_inc(p_done, 1)
                    if more and s in (6, 11):
                        gate(2 * g + (s // 5 + 1))

            for n in range(2):
                gate_in(n, PC_A + n, n or None)
                gate(n)
            for n in range(2):
                q_in(n, n, PC_A + 2 + n)
            dve.wait_ge(v_free, NT)
            dve.wait_ge(vcache_in, 16)
            for st in range(2):
                dve.wait_ge(drained[st], USE_A1[st])
            with dve.Fori(0, A_KV - 1) as g:
                attend(g, True)
            attend(A_KV - 1, False)

            dve.wait_ge(v_saved, 32)
            dve.wait_ge(k_saved, 32)
            dve.wait_ge(vz_ready, A_KV)
            dve.memset(Y[:, KD:MIX, LIVE:TOK], 0.0).then_inc(y_zeroed, 1)
            dve.wait_ge(y_zeroed, 1)
            dve.memset(qf, 1.0).then_inc(tf_set, 1)
            dve.memset(kf, 1.0).then_inc(tf_set, 1)
            dve.wait_ge(tf_set, 2)

            def log_gate(h, use):
                dve.wait_ge(z_act, 3 * h + 1)
                dve.tensor_scalar(chunks(Ei), setv(0), cur_b[:, 0:1], 0.0, ALU.add, ALU.min).then_inc(drained[0], 1)
                dve.wait_ge(z_act, 3 * h + 3)
                dve.wait_ge(drained[0], use)
                dve.tensor_tensor(Ei, Ei, E, ALU.subtract).then_inc(z_sub, 1)
                dve.wait_ge(z_sub, h + 1)
                for c in range(0, TOK, CHUNK):
                    e = min(c + CHUNK, TOK)
                    last = dve.tensor_tensor_scan(E[:, c:e], ones[:, 0:e - c], Ei[:, c:e], 0.0, ALU.mult, ALU.add)
                last.then_inc(gc_done, 1)

            def decays(h):
                dve.wait_ge(e_done, 2 * h + 2)
                dve.tensor_copy(elast, E[:, 0:LIVE].rearrange("p (c n) -> p c n", n=CHUNK)[:, :, CHUNK - 1])\
                   .then_inc(el_done, 1)
                dve.wait_ge(el_done, h + 1)
                e0, e1 = (elast[:, 0:NCK - 1].rearrange("p (t c) -> p t c", c=2)[:, :, c] for c in range(2))
                dve.tensor_copy(qf[:, 0:NCK - 1].rearrange("p (t c) -> p t c", c=2)[:, :, 1], e0)
                dve.tensor_copy(kf[:, 0:NCK - 1].rearrange("p (t c) -> p t c", c=2)[:, :, 0], e1)
                dve.tensor_tensor(etile[:, 0:NT - 1], e0, e1, ALU.mult)
                dve.tensor_copy(etile[:, NT - 1:NT], elast[:, NCK - 1:NCK]).then_inc(f_done, 1)
                dve.wait_ge(f_done, h + 1)

            def by_chunk(out, x, f):
                return dve.tensor_tensor(out[:, 0:LIVE].rearrange("p (c n) -> p c n", n=CHUNK),
                                         x[:, 0:LIVE].rearrange("p (c n) -> p c n", n=CHUNK),
                                         f.rearrange("p (c n) -> p c n", n=1).to_broadcast([P, NCK, CHUNK]), ALU.mult)

            def k_to_ends(h):
                by_chunk(kd, kg, elast).then_inc(kd_done, 1)
                dve.wait_ge(kd_done, h + 1)
                by_chunk(ks, kd, kf).then_inc(ks_done, 1)

            log_gate(0, USE_B0 + 3)
            decays(0)
            dve.tensor_tensor(kg, kT[:, 0, :], Ei, ALU.mult).then_inc(k0_ready, 1)
            dve.wait_ge(k0_ready, 1)
            k_to_ends(0)
            dve.scalar_tensor_tensor(qg, kT[:, 1, :], float(B_DK) ** -0.5, E, ALU.mult, ALU.mult).then_inc(q0_ready, 1)
            dve.wait_ge(q0_ready, 1)
            dve.wait_ge(ks_done, 1)
            by_chunk(qs, qg, qf).then_inc(q_ready, 1)

            def split_mix(k):
                dve.wait_ge(y_hi_done, k + 1)
                dve.tensor_tensor(Yr[:, k, :], Y[:, k, :], H[:, k, :].bitcast(F32), ALU.subtract)\
                   .then_inc(y_lo_done, 1)

            def head(i, last):
                u0, u1 = USE_B[0] + 3 * i, USE_B[1] + 3 * i
                piece = PC_B + B_PCS * i
                dve.memset(St[:, 0, :], 0.0).then_inc(s0_ready, 1)
                if not last:
                    dve.wait_ge(q_ready, i + 1)
                    log_gate(i + 1, u0 + 1)
                T0 = NT * i
                dve.wait_ge(s0_ready, i + 1)

                def mask(t):
                    r = tile_rows(t)
                    dve.wait_ge(at_done, T0 + t + 1)
                    if t >= 2:
                        dve.wait_ge(go_done, T0 + t - 1)
                    dve.tensor_tensor(aT[0:r, t % 2, 0:r], ps[0:r, t % 2, 0:r], causal[0:r, 0:r], ALU.mult)\
                       .then_inc(at_masked, 1)

                def save(t):
                    r = tile_rows(t)
                    dve.wait_ge(go_done, T0 + t + 1)
                    dve.tensor_scalar(Y[:, bass.ds(2 * i + 8, 2), t * P:t * P + r],
                                      ps[:, 3 + t % 2, 0:256].rearrange("p (e n) -> p e n", e=2)[:, :, 0:r],
                                      1.0, None, ALU.mult).then_inc(go_saved, 1)

                mask(0)
                for t in range(NT):
                    if t + 1 < NT:
                        mask(t + 1)
                    if t:
                        save(t - 1)
                    dve.wait_ge(gds_done, T0 + t + 1)
                    if t:
                        dve.wait_ge(s_upd, T0 + t)
                    if t >= 2:
                        dve.wait_ge(go_done, T0 + t - 1)
                    if t == NT - 1:
                        dve.wait_ge(gstate_in, 16 * i + 16)
                    state = Sst if t == NT - 1 else St[:, t % 3, :]
                    dve.scalar_tensor_tensor(St[:, (t + 1) % 3, :], state, etile[:, t:t + 1],
                                             ps[:, 6 + t % 2, 0:256], ALU.mult, ALU.add).then_inc(s_upd, 1)
                save(NT - 1)
                def gate_in(n):
                    dve.wait_ge(piece_done, piece + 3 + n)
                    dve.tensor_tensor(chunks(gs[:, n, :]), setv(1 - n), chunks(rb), ALU.mult)\
                       .then_inc(drained[1 - n], 1)

                def gate(n):
                    dve.wait_ge(b_gate, 2 * i + n + 1)
                    dve.scalar_tensor_tensor(gs[:, n, :], tb[:, n, :], 1.0, gs[:, n, :], ALU.add, ALU.mult)\
                       .then_inc(gs_done, 1)

                def mean_square():
                    dve.wait_ge(gn_done, i + 1)
                    dve.tensor_scalar(chunks(kd), setv(1), 1.0 / B_DV, EPS, ALU.mult, ALU.add)\
                       .then_inc(drained[1], 1)

                def root_inverse():
                    dve.wait_ge(gn_std, i + 1)
                    dve.reciprocal(kd, kd).then_inc(gn_rstd, 1)

                def scale():
                    dve.wait_ge(gn_rstd, i + 1)
                    dve.wait_ge(gs_done, 2 * i + 2)
                    for e in range(2):
                        y = slot(Y, 2 * i + 8 + e)
                        dve.scalar_tensor_tensor(y, y, vecs[:, VC_GN + e:VC_GN + e + 1], kd, ALU.mult, ALU.mult)\
                           .then_inc(bn_done, 1)
                    for e in range(2):
                        y = slot(Y, 2 * i + 8 + e)
                        dve.wait_ge(bn_done, 2 * i + e + 1)
                        done = dve.scalar_tensor_tensor(y, y, 0.5, gs[:, e, :], ALU.mult, ALU.mult)
                    done.then_inc(b_done, 1)

                dve.wait_ge(sq2_done, i + 1)
                dve.tensor_tensor(sq2[:, 0, :], sq2[:, 0, :], sq2[:, 1, :], ALU.add).then_inc(sq2_added, 1)
                gate_in(0)
                gate(0)
                gate_in(1)
                if not last:
                    mean_square()
                    gate(1)
                    root_inverse()
                    scale()
                    decays(i + 1)
                    dve.tensor_tensor(Ei, Ei, rb, ALU.mult).then_inc(es_done, 1)
                    dve.tensor_tensor(E, E, rb, ALU.mult).then_inc(es_done, 1)
                    dve.wait_ge(es_done, 2 * i + 2)
                    dve.wait_ge(piece_done, piece + 5)
                    dve.tensor_tensor(chunks(kg), setv(0), chunks(Ei), ALU.mult).then_inc(drained[0], 1)
                    dve.wait_ge(drained[0], u0 + 3)
                    dve.wait_ge(b_done, i + 1)
                    k_to_ends(i + 1)
                    dve.wait_ge(piece_done, piece + 6)
                    dve.scalar_tensor_tensor(chunks(qg), setv(1), float(B_DK) ** -0.5, chunks(E), ALU.mult, ALU.mult)\
                       .then_inc(drained[1], 1)
                    dve.wait_ge(drained[1], u1 + 3)
                    dve.wait_ge(ks_done, i + 2)
                    by_chunk(qs, qg, qf).then_inc(q_ready, 1)
                    dve.wait_ge(gla_saved, 32 * i + 32)
                    return
                for k in range(MIX):
                    if k == 2:
                        mean_square()
                        gate(1)
                    if k == 7:
                        root_inverse()
                    if k == 10:
                        scale()
                    split_mix(k)

            with dve.Fori(0, B_HEADS - 1) as i:
                head(i, False)
            head(B_HEADS - 1, True)

            def out_residual(n, base, res_base, last_pair):
                dve.memset(acc, 0.0).then_inc(acc_zero, 1)
                dve.wait_ge(acc_zero, n + 1)

                def residual(i, s):
                    dve.wait_ge(piece_done, base + 4 * i + s + 3)
                    dve.wait_ge(res_in[s], 16 * (i + res_base + 1))
                    dve.tensor_tensor(chunks(slot(X, 2 * i + s)), setv(s), chunks(res[:, s, :]), ALU.add)\
                       .then_inc(drained[s], 1)

                def square(i, s):
                    dve.wait_ge(sq_done, KD * n + 2 * i + s + 1)
                    dve.wait_ge(acc_done, KD * n + 2 * i + s)
                    dve.tensor_tensor(acc, acc, sq, ALU.add).then_inc(acc_done, 1)

                with dve.Fori(0, KD // 2 - 1) as i:
                    for s in range(2):
                        residual(i, s)
                        square(i, s)
                last_pair(KD // 2 - 1, residual, square)

            lv = vecs[:, VC_C:VC_ALL].rearrange("p (b n) -> p b n", n=VB)
            dve.tensor_scalar(nsp[:, :, 1], lv[:, :, 7], -1.0, 0.0, ALU.mult, ALU.max).then_inc(nsp_ready, 1)
            dve.tensor_scalar(nsp[:, :, 2:4], lv[:, :, 5:7], 0.5, None, ALU.mult)
            dve.wait_ge(nsp_ready, 1)
            dve.wait_ge(lam_act, 3)
            dve.tensor_tensor(nsp[:, :, 0], nsp[:, :, 1], lamt[:, :], ALU.add).then_inc(nsp_ready, 1)
            dve.wait_ge(nsp_ready, 2)
            dve.tensor_scalar(nsp[:, :, 1], nsp[:, :, 0], 4.0, None, ALU.mult).then_inc(nsp_ready, 1)
            dve.wait_ge(nsp_ready, 3)
            dve.tensor_scalar(nsp[:, :, 0], nsp[:, :, 1], -1.0, None, ALU.mult).then_inc(nsp_ready, 1)
            dve.wait_ge(nsp_ready, 4)

            def last_pair_even(i, residual, square):
                residual(i, 0)
                square(i, 0)
                dve.wait_ge(piece_done, PC_C)
                for k in range(KD):
                    if k == 2:
                        residual(i, 1)
                    if k == 5:
                        square(i, 1)
                    split_h(1, k)

            out_residual(1, PC_OE, 0, last_pair_even)
            norm_factors(1)

            dve.wait_ge(x1_saved, 16 * KD)
            dve.wait_ge(h_lo_done, 2 * KD)
            dve.memset(xc, 0.0).then_inc(xc_zeroed, 1)
            dve.memset(Y[:, 0:KC, LIVE:TOK], 0.0).then_inc(xc_zeroed, 1)
            dve.wait_ge(xc_zeroed, 2)
            dve.wait_ge(rb_done, 2)
            def mix_rest(k):
                dve.wait_ge(y_hi_done, MIX + k + 1)
                dve.tensor_tensor(slot(Yr, k), slot(Y, k), slot(H, k).bitcast(F32), ALU.subtract)\
                   .then_inc(y_lo_done, 1)

            def group(g, last):
                piece = PC_C + C_PCS * g
                u = [USE_C[st] + 6 * g for st in range(2)]
                G = 3 * g
                dve.tensor_copy(cur_n[:, :, :], nsp[:, bass.ds(G, 3), :])
                dve.tensor_copy(cur[:, :, :].rearrange("p a b -> p (a b)"),
                                vecs[:, bass.ds(VC_C + VB * G, 3 * VB)]).then_inc(cur_ready, 1)
                dve.wait_ge(cur_ready, g + 1)
                for n in range(3):
                    st = n % 2
                    dve.wait_ge(piece_done, piece + n + 1)
                    if n:
                        dve.wait_ge(cvo_done, G + n)
                    dve.tensor_tensor(xc[:, EXT:EXT + 2 * CW].rearrange("p (c n) -> p c n", c=2),
                                      sets[st][:, 0:2, 0:CW], chunks(rb)[:, 0:2, :], ALU.mult)
                    dve.tensor_tensor(xc[:, EXT + 2 * CW:EXT + SEQ], sets[st][:, 2, 0:SEQ - 2 * CW],
                                      rb[:, 2 * CW:SEQ], ALU.mult)
                    dve.tensor_copy(xc[:, EXT + SEQ:2 * EXT + SEQ], cur[:, n, 9:12])
                    dve.tensor_tensor(xc[:, 2 * EXT + SEQ:2 * EXT + LIVE], sets[st][:, 2, SEQ - 2 * CW:LIVE - 2 * CW],
                                      rb[:, SEQ:LIVE], ALU.mult).then_inc(drained[st], 1)
                    dve.wait_ge(drained[st], u[st] + n // 2 + 1)
                    dve.tensor_scalar(U[:, n, :], xc[:, 0:TOK], cur[:, n, 0:1], cur[:, n, 4:5], ALU.mult, ALU.add)\
                       .then_inc(cv_step, 1)
                    for j in range(1, CONV_W):
                        dve.wait_ge(cv_step, 3 * G + 3 * n + j)
                        dve.scalar_tensor_tensor(U[:, n, :], xc[:, j:j + TOK], cur[:, n, j:j + 1], U[:, n, :],
                                                 ALU.mult, ALU.add).then_inc(cv_step if j < 3 else cv_done, 1)
                    dve.tensor_scalar(slot(cvo, G + n, 0, EXT), xc[:, SEQ:SEQ + EXT], 1.0, None, ALU.mult)
                    dve.tensor_scalar(slot(cvo, G + n, EXT, 2 * EXT), xc[:, LIVE + EXT:LIVE + 2 * EXT], 1.0, None,
                                      ALU.mult).then_inc(cvo_done, 1)
                    dve.wait_ge(cv_done, G + n + 1)
                    dve.wait_ge(u_hi_done, G + n + 1)
                    dve.tensor_tensor(ur[:, 1, n, :], U[:, n, :], ur[:, 0, n, :].bitcast(F32), ALU.subtract)\
                       .then_inc(u_lo_done, 1)
                for m in range(3):
                    vr, vi, vg = (c_use(m, n) for n in range(3))
                    dve.wait_ge(c_a, 2 * G + 2 * m + 2)
                    dve.scalar_tensor_tensor(th, sa, 1.0, th, ALU.add, ALU.mult).then_inc(c_w, 1)
                    dve.wait_ge(drained[vi % 2], u[vi % 2] + vi // 2 + 1)
                    dve.scalar_tensor_tensor(ti, ti, 1.0, U[:, m, :], ALU.add, ALU.mult).then_inc(c_iu, 1)
                    dve.wait_ge(c_iu, G + m + 1)
                    dve.wait_ge(c_sqrt, G + m + 1)
                    dve.scalar_tensor_tensor(ti, ti, 0.5, th, ALU.mult, ALU.mult).then_inc(c_b, 1)
                    dve.wait_ge(c_b, G + m + 1)
                    s0 = SEQ + EXT
                    dve.tensor_tensor_scan(sa[:, 0:SEQ], aa[:, 0:SEQ], ti[:, 0:SEQ], 0.0, ALU.mult, ALU.add)\
                       .then_inc(c_scan, 1)
                    dve.tensor_tensor_scan(sa[:, s0:s0 + DEC], aa[:, s0:s0 + DEC], ti[:, s0:s0 + DEC],
                                           cur[:, m, 8:9], ALU.mult, ALU.add).then_inc(c_scan, 1)
                    dve.wait_ge(piece_done, piece + 5 + 2 * m)
                    dve.tensor_tensor(chunks(cgz), setv(vg % 2), chunks(rb), ALU.mult).then_inc(drained[vg % 2], 1)
                    if last and m == 2:
                        mix_rest(0)
                        mix_rest(1)
                    dve.wait_ge(c_scan, 2 * G + 2 * m + 2)
                    dve.wait_ge(drained[vg % 2], u[vg % 2] + vg // 2 + 1)
                    y = slot(Y, G + m, 0, SEQ)
                    dve.scalar_tensor_tensor(y, sa[:, 0:SEQ], 0.5, cgz[:, 0:SEQ], ALU.mult, ALU.mult)
                    y = slot(Y, G + m, SEQ, LIVE)
                    dve.scalar_tensor_tensor(y, sa[:, s0:s0 + DEC], 0.5, cgz[:, SEQ:LIVE], ALU.mult, ALU.mult)\
                       .then_inc(c_gy, 1)
                    dve.tensor_copy(slot(lro, G + m, 0, 1), sa[:, SEQ - 1:SEQ])
                    dve.tensor_copy(slot(lro, G + m, 1, 2), sa[:, s0 + DEC - 1:s0 + DEC])
                    dve.wait_ge(c_gy, G + m + 1)
                    dve.wait_ge(c_tanh, G + m + 1)
                    y = slot(Y, G + m, 0, LIVE)
                    dve.scalar_tensor_tensor(y, gc[:, 0:LIVE], 1.0, y, ALU.add, ALU.mult).then_inc(c_y, 1)

            with dve.Fori(0, KC // 3 - 1) as g:
                group(g, False)
            group(KC // 3 - 1, True)
            with dve.Fori(2, KC) as k:
                mix_rest(k)

            def last_pair_odd(i, residual, square):
                for s in range(2):
                    residual(i, s)
                    square(i, s)

            out_residual(2, PC_OO, 4, last_pair_odd)
            norm_factors(2)
            dve.wait_ge(bc_done, 3)
            for b in range(KD):
                g = vecs[:, VC_N[2] + b:VC_N[2] + b + 1]
                for x, r in ((X[:, b, 0:SEQ], ps[:, 6:8, :].rearrange("p a n -> p (a n)")),
                             (X[:, b, SEQ:TOK], ps[:, 2, CW:CW + TOK - SEQ])):
                    done = dve.scalar_tensor_tensor(x, x, g, r, ALU.mult, ALU.mult)
                done.then_inc(xn_done, 1)


def kernel(**inputs):
    import concourse.bacc as bacc
    from concourse.bass_utils import run_bass_kernel_spmd

    f = {k: np.asarray(v) for k, v in inputs.items()}
    w_in, w_oe = f["w_in_even"][0], f["w_out_even"][0]
    w_ino, w_oo = f["w_in_odd"][0], f["w_out_odd"][0]
    dt = w_in.dtype

    W = np.zeros((PIECES, P, PIECE), dt)

    def columns(piece, w, cols):
        kt = w.shape[0] // P
        W[piece, :, :kt * P] = w[:, cols].reshape(kt, P, P).transpose(1, 0, 2).reshape(P, kt * P)

    def values(piece, w, c):
        v = w[:, c:c + 256].reshape(2, 4, P, 256).transpose(0, 2, 1, 3).reshape(2, P, PIECE)
        W[piece:piece + 2] = v

    def block_of(c):
        return np.arange(c, c + P)

    values(PC_V, w_in, OFF_V)
    columns(PC_LR, w_in, block_of(OFF_LR))
    for b in range(2):
        columns(PC_K + b, w_in, block_of(OFF_K + b * P))
    for g in range(A_KV):
        for b in range(2):
            columns(PC_A + A_PCS * g + b, w_in, block_of(OFF_G + (2 * g + b) * P))
            columns(PC_A + A_PCS * g + 2 + b, w_in, block_of(OFF_Q + (2 * g + b) * P))
    for h in range(B_HEADS):
        a = PC_B + B_PCS * h
        kq = a - 2 if h else PC_B0
        columns(kq, w_in, block_of(OFF_BK + h * P))
        columns(kq + 1, w_in, block_of(OFF_BQ + h * P))
        values(a, w_in, OFF_BV + h * B_DV)
        for b in range(2):
            columns(a + 2 + b, w_in, block_of(OFF_G + (8 + 2 * h + b) * P))
    for m in range(KD):
        for half in range(2):
            at = 4 * (m // 2) + 2 * half + m % 2
            columns(PC_OE + at, w_oe[half * 8 * P:(half + 1) * 8 * P], block_of(m * P))
            columns(PC_OO + at, w_oo[half * 6 * P:(half + 1) * 6 * P], block_of(m * P))
    for g in range(4):
        a = PC_C + C_PCS * g
        for n in range(3):
            columns(a + n, w_ino, block_of((3 * g + n) * P))
            columns(a + 4 + 2 * n, w_ino, block_of(CWID + (3 * g + n) * P))
        for n, name in enumerate(("w_rg_a", "w_rg_i")):
            both = np.zeros((3 * P, 3 * P), dt)
            for b in range(2):
                sl = slice(b * CBLK, (b + 1) * CBLK)
                both[sl, sl] = f[name][0, 2 * g + b]
            for m, kts in enumerate(((0, 1), (0, 1, 2), (1, 2))):
                for x, kt in enumerate(kts):
                    at = 4 * n + x
                    W[a + 3 + 2 * m, :, at * P:(at + 1) * P] = both[kt * P:(kt + 1) * P, m * P:(m + 1) * P]

    xT = np.zeros((KD, P, TOK), dt)
    xT[:, :, :SEQ] = f["x_prompt"][0].T.reshape(KD, P, SEQ)
    xT[:, :, SEQ:LIVE] = f["x_sample"][0].T.reshape(KD, P, DEC)

    vecs = np.zeros((P, VC_ALL), dt)
    for n, name in enumerate(("norm_even", "norm_odd", "norm_final")):
        vecs[:, VC_N[n]:VC_N[n] + KD] = f[name].reshape(KD, P).T
    vecs[:, VC_BLR:VC_BLR + 4] = f["b_gate_lr"][0].reshape(4, P).T
    vecs[:, VC_GN:VC_GN + 2] = f["gla_norm"][0].reshape(2, P).T
    vecs[:, VC_SINK:VC_SINK + A_HEADS] = f["sinks"][0][None, :]
    lv = vecs[:, VC_C:].reshape(P, KC, VB)
    for j in range(CONV_W):
        lv[:, :, j] = f["conv_w"][0, j].reshape(KC, P).T
    for n, name in enumerate(("conv_b", "b_rg_a", "b_rg_i", "lru_lambda", "state_lru")):
        lv[:, :, CONV_W + n] = f[name][0].reshape(KC, P).T
    for j in range(EXT):
        lv[:, :, 9 + j] = f["cache_conv"][0, 0, j].reshape(KC, P).T

    consts = np.zeros((P, CC_ALL), np.float32)
    r = np.arange(P)
    consts[:, CC_ID:CC_ID + P] = np.eye(P)
    consts[:, CC_CAUSAL:CC_CAUSAL + P] = r[:, None] <= r[None, :]
    j = np.arange(2 * P)
    far = (j[None, :] // CHUNK < r[:, None] // CHUNK) | (j[None, :] // CHUNK > r[:, None] // CHUNK + 2)
    consts[:, CC_DIST:CC_DIST + 2 * P] = np.where(far, 1e34, np.abs(WIN + r[:, None] - j[None, :]))
    consts[:, CC_SLOPE:] = -(2.0 ** (-8.0 * np.arange(1, A_HEADS + 1) / A_HEADS)).astype(np.float32) * A_DIM ** 0.5

    wlr = np.zeros((B_HEADS + 1, P, P), dt)
    wlr[:B_HEADS, :B_LOW] = f["w_gate_lr"][0].reshape(B_LOW, B_HEADS, P).transpose(1, 0, 2)
    arrays = {
        "xT": xT, "weights": W, "vecs_in": vecs, "consts_in": consts, "wlr_in": wlr,
        "k_cache": np.ascontiguousarray(f["cache_swa_k"][0, 0].transpose(1, 2, 0)),
        "v_cache": np.ascontiguousarray(f["cache_swa_v"][0, 0].reshape(WIN, A_KV * A_DIM)),
        "gla_state": np.ascontiguousarray(f["state_gla"][0, 0]),
    }
    outs = {
        "yT": (KD, P, TOK), "k_new": (A_KV, A_DIM, WIN + DEC), "v_new": (WIN + DEC, A_KV * A_DIM),
        "gla_p": (B_HEADS, B_DK, B_DV), "gla_s": (B_HEADS, B_DK, B_DV),
        "conv_new": (P, KC, 2 * EXT), "lru_new": (P, KC, 2),
    }
    nc = bacc.Bacc("TRN2", target_bir_lowering=False, num_devices=1, dynamic_dma_scratch_size=1024)
    args = [nc.dram_tensor(k, a.shape, mybir.dt.from_np(a.dtype), kind="ExternalInput").ap()
            for k, a in arrays.items()]
    args += [nc.dram_tensor(k, s, F32, kind="ExternalOutput").ap() for k, s in outs.items()]
    build_program(nc, *args)
    got = run_bass_kernel_spmd(nc, [arrays], core_ids=[0]).results[0]

    y = got["yT"].reshape(DM, TOK).T
    kn = got["k_new"].transpose(2, 0, 1)
    vn = got["v_new"].reshape(WIN + DEC, A_KV, A_DIM)
    cn = got["conv_new"].transpose(2, 1, 0).reshape(2, EXT, CWID)
    ln = got["lru_new"].transpose(2, 1, 0).reshape(2, CWID)
    return (y[None, :SEQ], y[None, SEQ:LIVE],
            kn[None, None, :WIN], vn[None, None, :WIN], got["gla_p"][None, None],
            cn[None, None, 0], ln[None, None, 0],
            kn[None, None, WIN:], vn[None, None, WIN:], got["gla_s"][None, None],
            cn[None, None, 1], ln[None, None, 1])
```
